# Optimizing a Trainium2 kernel written in Bass

```python
import jax
import jax.numpy as jnp
from jax import lax
import math
import jax, jax.numpy as jnp
import numpy as np

D_MODEL = 1024
BATCH = 1
SEQ = 512
DEPTH = 2

GRID_W = 64
CTX_LEN = 256
HEAD_DIM = 64
A_Q_HEADS = 8
A_KV_HEADS = 2
A_GROUP = A_Q_HEADS // A_KV_HEADS
A_WINDOW = 128
A_BLOCK = 128
B_HEADS = 4
NA_ROWS = 8
NA_COLS = 16
C_CHANNELS = 256
C_CONV_WIDTH = 31
A_Q_W = A_Q_HEADS * HEAD_DIM
A_KV_W = A_KV_HEADS * HEAD_DIM
B_W = B_HEADS * HEAD_DIM
MIX_WIDTH = A_Q_W + B_W + C_CHANNELS
IN_WIDTH = A_Q_W + 2 * A_KV_W + 3 * B_W + 2 * C_CHANNELS
OFF_AQ = 0
OFF_AK = OFF_AQ + A_Q_W
OFF_AV = OFF_AK + A_KV_W
OFF_BQ = OFF_AV + A_KV_W
OFF_BK = OFF_BQ + B_W
OFF_BV = OFF_BK + B_W
OFF_C = OFF_BV + B_W
N_EXPERTS = 16
EXPERT_FF = 1024
EC_CAPACITY = 2
ROPE_BASE = 10000.0
LN_EPS = 1e-6
N_MOD = 6
MOD_INIT = 0.5
DEEPNORM_ALPHA = (2 * DEPTH) ** 0.25
DEEPNORM_BETA = (8 * DEPTH) ** -0.25
NEG_INF = -1e30


def layer_norm(x, g=None, b=None):
    xf = x.astype(jnp.float32)
    mu = jnp.mean(xf, axis=-1, keepdims=True)
    var = jnp.mean(jnp.square(xf - mu), axis=-1, keepdims=True)
    y = (xf - mu) * lax.rsqrt(var + LN_EPS)
    if g is not None:
        y = y * g.astype(jnp.float32) + b.astype(jnp.float32)
    return y.astype(x.dtype)

def modulate(x, shift, scale):
    return layer_norm(x) * (1 + scale) + shift

def adaln(cond, w_mod_l, b_mod_l, n_chunks):
    m = jax.nn.silu(cond) @ w_mod_l[:, :n_chunks * D_MODEL] + b_mod_l[:n_chunks * D_MODEL]
    return jnp.split(m, n_chunks, axis=-1)

def split_heads(t, n_heads):
    return t.reshape(t.shape[:-1] + (n_heads, HEAD_DIM))

def axial_rope(n_tokens, dtype):
    t = jnp.arange(n_tokens, dtype=jnp.int32)
    row = (t // GRID_W).astype(jnp.float32)[:, None]
    col = (t % GRID_W).astype(jnp.float32)[:, None]
    n_freq = HEAD_DIM // 4
    inv_freq = ROPE_BASE ** (-jnp.arange(n_freq, dtype=jnp.float32) / n_freq)
    ang_r = row * inv_freq
    ang_c = col * inv_freq
    return (jnp.cos(ang_r)[:, None, :].astype(dtype), jnp.sin(ang_r)[:, None, :].astype(dtype),
            jnp.cos(ang_c)[:, None, :].astype(dtype), jnp.sin(ang_c)[:, None, :].astype(dtype))

def rope_half(x, cos, sin):
    x1, x2 = jnp.split(x, 2, axis=-1)
    return jnp.concatenate([x1 * cos - x2 * sin, x2 * cos + x1 * sin], axis=-1)

def apply_axial_rope(x, cos_r, sin_r, cos_c, sin_c):
    xr, xc = jnp.split(x, 2, axis=-1)
    return jnp.concatenate([rope_half(xr, cos_r, sin_r), rope_half(xc, cos_c, sin_c)], axis=-1)

def window_gqa_latent(q, k, v, kc, vc, sink):
    bsz, n_lat = q.shape[:2]
    n_blk = n_lat // A_BLOCK
    span = A_BLOCK + 2 * A_WINDOW
    pad = ((0, 0), (A_WINDOW, A_WINDOW), (0, 0), (0, 0))
    kp = jnp.pad(k, pad)
    vp = jnp.pad(v, pad)
    scale = HEAD_DIM ** -0.5
    sink_l = sink.reshape(1, A_KV_HEADS, A_GROUP, 1, 1).astype(jnp.float32)
    q_off = jnp.arange(A_BLOCK)
    k_off = jnp.arange(span) - A_WINDOW
    band = jnp.abs(k_off[None, :] - q_off[:, None]) <= A_WINDOW

    def block(i):
        start = i * A_BLOCK
        qb = lax.dynamic_slice_in_dim(q, start, A_BLOCK, axis=1)
        kb = lax.dynamic_slice_in_dim(kp, start, span, axis=1)
        vb = lax.dynamic_slice_in_dim(vp, start, span, axis=1)
        kpos = start + k_off
        valid = band & ((kpos >= 0) & (kpos < n_lat))[None, :]
        s_win = jnp.einsum('bqhgd,bkhd->bhgqk', qb, kb).astype(jnp.float32) * scale
        s_win = jnp.where(valid, s_win, NEG_INF)
        s_ctx = jnp.einsum('bqhgd,bkhd->bhgqk', qb, kc).astype(jnp.float32) * scale
        s_sink = jnp.broadcast_to(sink_l, s_win.shape[:-1] + (1,))
        p = jax.nn.softmax(jnp.concatenate([s_win, s_ctx, s_sink], axis=-1), axis=-1).astype(q.dtype)
        return (jnp.einsum('bhgqk,bkhd->bqhgd', p[..., :span], vb)
                + jnp.einsum('bhgqk,bkhd->bqhgd', p[..., span:span + kc.shape[1]], vc))

    out = lax.map(block, jnp.arange(n_blk))
    return jnp.moveaxis(out, 0, 1).reshape(bsz, n_lat, A_Q_W)

def context_gqa(qc, kc, vc, sink):
    s = jnp.einsum('bqhgd,bkhd->bhgqk', qc, kc).astype(jnp.float32) * HEAD_DIM ** -0.5
    s_sink = jnp.broadcast_to(sink.reshape(1, A_KV_HEADS, A_GROUP, 1, 1).astype(jnp.float32), s.shape[:-1] + (1,))
    p = jax.nn.softmax(jnp.concatenate([s, s_sink], axis=-1), axis=-1).astype(qc.dtype)
    o = jnp.einsum('bhgqk,bkhd->bqhgd', p[..., :-1], vc)
    return o.reshape(qc.shape[0], qc.shape[1], A_Q_W)

def neighbourhood_latent(q, k, v, kc, vc, rel_bias):
    bsz, n_lat = q.shape[:2]
    rows = n_lat // GRID_W
    kr_n = min(NA_ROWS, rows)
    n_keys = kr_n * GRID_W
    scale = HEAD_DIM ** -0.5
    qg = q.reshape(bsz, rows, GRID_W, B_HEADS, HEAD_DIM)
    kg = k.reshape(bsz, rows, GRID_W, B_HEADS, HEAD_DIM)
    vg = v.reshape(bsz, rows, GRID_W, B_HEADS, HEAD_DIM)
    cols = jnp.arange(GRID_W)
    c_start = jnp.clip(cols - NA_COLS // 2, 0, GRID_W - NA_COLS)
    col_mask = (cols[None, :] >= c_start[:, None]) & (cols[None, :] < c_start[:, None] + NA_COLS)
    mask = jnp.broadcast_to(col_mask[:, None, :], (GRID_W, kr_n, GRID_W)).reshape(GRID_W, n_keys)
    dc = jnp.clip(cols[None, :] - cols[:, None], -(NA_COLS - 1), NA_COLS - 1) + NA_COLS - 1

    def row(r):
        r_start = jnp.clip(r - kr_n // 2, 0, rows - kr_n)
        qr = lax.dynamic_index_in_dim(qg, r, axis=1, keepdims=False)
        kr = lax.dynamic_slice_in_dim(kg, r_start, kr_n, axis=1).reshape(bsz, n_keys, B_HEADS, HEAD_DIM)
        vr = lax.dynamic_slice_in_dim(vg, r_start, kr_n, axis=1).reshape(bsz, n_keys, B_HEADS, HEAD_DIM)
        dr = r_start + jnp.arange(kr_n) - r + NA_ROWS - 1
        bias = rel_bias[:, dr[None, :, None], dc[:, None, :]].reshape(B_HEADS, GRID_W, n_keys)
        s_nb = jnp.einsum('bqhd,bkhd->bhqk', qr, kr).astype(jnp.float32) * scale + bias.astype(jnp.float32)
        s_nb = jnp.where(mask, s_nb, NEG_INF)
        s_ctx = jnp.einsum('bqhd,bkhd->bhqk', qr, kc).astype(jnp.float32) * scale
        p = jax.nn.softmax(jnp.concatenate([s_nb, s_ctx], axis=-1), axis=-1).astype(q.dtype)
        return (jnp.einsum('bhqk,bkhd->bqhd', p[..., :n_keys], vr)
                + jnp.einsum('bhqk,bkhd->bqhd', p[..., n_keys:], vc))

    out = lax.map(row, jnp.arange(rows))
    return jnp.moveaxis(out, 0, 1).reshape(bsz, n_lat, B_W)

def context_mha(qc, kc, vc):
    s = jnp.einsum('bqhd,bkhd->bhqk', qc, kc).astype(jnp.float32) * HEAD_DIM ** -0.5
    p = jax.nn.softmax(s, axis=-1).astype(qc.dtype)
    o = jnp.einsum('bhqk,bkhd->bqhd', p, vc)
    return o.reshape(qc.shape[0], qc.shape[1], B_W)

def conformer_conv(u, conv_w, conv_b, ln_g, ln_b):
    a, gate = jnp.split(u, 2, axis=-1)
    h = a * jax.nn.sigmoid(gate)
    half = C_CONV_WIDTH // 2
    h = lax.conv_general_dilated(h, conv_w[:, None, :], window_strides=(1,), padding=((half, half),),
                                 dimension_numbers=('NWC', 'WIO', 'NWC'),
                                 feature_group_count=C_CHANNELS) + conv_b
    return jax.nn.silu(layer_norm(h, ln_g, ln_b))

def ec_moe(h, w_router, w_gate, w_up, w_down):
    bsz, n_tok, d = h.shape
    cap = EC_CAPACITY * n_tok // N_EXPERTS
    aff = jax.nn.softmax(jnp.einsum('bnd,de->bne', h, w_router).astype(jnp.float32), axis=-1)
    g, idx = lax.top_k(jnp.swapaxes(aff, 1, 2), cap)
    xs = jax.vmap(lambda hb, ib: hb[ib])(h, idx)
    hid = jax.nn.silu(jnp.einsum('becd,edf->becf', xs, w_gate)) * jnp.einsum('becd,edf->becf', xs, w_up)
    ye = jnp.einsum('becf,efd->becd', hid, w_down) * g[..., None].astype(h.dtype)
    return jax.vmap(lambda yb, ib: jnp.zeros((n_tok, d), h.dtype).at[ib.reshape(-1)].add(yb.reshape(-1, d)))(ye, idx)

def context_kv(hc, w_in_l):
    ka, va = jnp.split(hc @ w_in_l[:, OFF_AK:OFF_BQ], 2, axis=-1)
    kb, vb = jnp.split(hc @ w_in_l[:, OFF_BK:OFF_C], 2, axis=-1)
    return (split_heads(ka, A_KV_HEADS), split_heads(va, A_KV_HEADS),
            split_heads(kb, B_HEADS), split_heads(vb, B_HEADS))

def first_inputs(seed: int = 0) -> dict:
    key = jax.random.key(seed)
    ks = jax.random.split(key, 22)
    L, D = DEPTH, D_MODEL

    def nrm(k, shape, s):
        return s * jax.random.normal(k, shape, jnp.float32)

    return {
        'x': nrm(ks[0], (BATCH, SEQ, D), 1.0),
        'c': nrm(ks[1], (BATCH, D), 1.0),
        'ctx': nrm(ks[2], (BATCH, CTX_LEN, D), 1.0),
        'c_ctx': nrm(ks[3], (D,), 1.0),
        'w_mod': nrm(ks[4], (L, D, N_MOD * D), MOD_INIT * D ** -0.5),
        'b_mod': nrm(ks[5], (L, N_MOD * D), 0.02),
        'w_in': nrm(ks[6], (L, D, IN_WIDTH), D ** -0.5),
        'a_sink': nrm(ks[7], (L, A_Q_HEADS), 0.5),
        'nat_bias': nrm(ks[8], (L, B_HEADS, 2 * NA_ROWS - 1, 2 * NA_COLS - 1), 0.1),
        'conv_w': nrm(ks[9], (L, C_CONV_WIDTH, C_CHANNELS), C_CONV_WIDTH ** -0.5),
        'conv_b': nrm(ks[10], (L, C_CHANNELS), 0.02),
        'conv_ln_g': 1.0 + nrm(ks[11], (L, C_CHANNELS), 0.05),
        'conv_ln_b': nrm(ks[12], (L, C_CHANNELS), 0.02),
        'w_out': nrm(ks[13], (L, MIX_WIDTH, D), DEEPNORM_BETA * MIX_WIDTH ** -0.5),
        'ln1_g': 1.0 + nrm(ks[14], (L, D), 0.05),
        'ln1_b': nrm(ks[15], (L, D), 0.02),
        'w_router': nrm(ks[16], (L, D, N_EXPERTS), D ** -0.5),
        'w_gate': nrm(ks[17], (L, N_EXPERTS, D, EXPERT_FF), D ** -0.5),
        'w_up': nrm(ks[18], (L, N_EXPERTS, D, EXPERT_FF), D ** -0.5),
        'w_down': nrm(ks[19], (L, N_EXPERTS, EXPERT_FF, D), DEEPNORM_BETA * EXPERT_FF ** -0.5),
        'ln2_g': 1.0 + nrm(ks[20], (L, D), 0.05),
        'ln2_b': nrm(ks[21], (L, D), 0.02),
    }

def first_block(x, c, ctx, c_ctx, w_mod, b_mod, w_in, a_sink, nat_bias, conv_w, conv_b, conv_ln_g, conv_ln_b,
              w_out, ln1_g, ln1_b, w_router, w_gate, w_up, w_down, ln2_g, ln2_b):
    bsz, n_lat, _ = x.shape
    n_ctx = ctx.shape[1]
    rope = axial_rope(n_lat, x.dtype)
    for l in range(DEPTH):
        last = l == DEPTH - 1
        w_in_l = w_in[l]
        sh1, sc1, g1, sh2, sc2, g2 = [m[:, None, :] for m in adaln(c, w_mod[l], b_mod[l], N_MOD)]

        ctx_mod = adaln(c_ctx, w_mod[l], b_mod[l], 2 if last else N_MOD)
        hc = modulate(ctx, ctx_mod[0], ctx_mod[1])
        kc_a, vc_a, kc_b, vc_b = context_kv(hc, w_in_l)
        if not last:
            qc_a = split_heads(hc @ w_in_l[:, OFF_AQ:OFF_AK], A_Q_HEADS).reshape(bsz, n_ctx, A_KV_HEADS, A_GROUP, HEAD_DIM)
            qc_b = split_heads(hc @ w_in_l[:, OFF_BQ:OFF_BK], B_HEADS)
            oc = jnp.concatenate([
                context_gqa(qc_a, kc_a, vc_a, a_sink[l]),
                context_mha(qc_b, kc_b, vc_b),
                conformer_conv(hc @ w_in_l[:, OFF_C:], conv_w[l], conv_b[l], conv_ln_g[l], conv_ln_b[l]),
            ], axis=-1) @ w_out[l]
            ctx_new = layer_norm(DEEPNORM_ALPHA * ctx + ctx_mod[2] * oc, ln1_g[l], ln1_b[l])
            hc2 = modulate(ctx_new, ctx_mod[3], ctx_mod[4])
            ctx_new = layer_norm(DEEPNORM_ALPHA * ctx_new + ctx_mod[5] * ec_moe(hc2, w_router[l], w_gate[l], w_up[l], w_down[l]),
                                 ln2_g[l], ln2_b[l])

        h = modulate(x, sh1, sc1)
        u = h @ w_in_l
        q_a = apply_axial_rope(split_heads(u[..., OFF_AQ:OFF_AK], A_Q_HEADS), *rope)
        k_a = apply_axial_rope(split_heads(u[..., OFF_AK:OFF_AV], A_KV_HEADS), *rope)
        v_a = split_heads(u[..., OFF_AV:OFF_BQ], A_KV_HEADS)
        q_b = split_heads(u[..., OFF_BQ:OFF_BK], B_HEADS)
        k_b = split_heads(u[..., OFF_BK:OFF_BV], B_HEADS)
        v_b = split_heads(u[..., OFF_BV:OFF_C], B_HEADS)
        o_a = window_gqa_latent(q_a.reshape(bsz, n_lat, A_KV_HEADS, A_GROUP, HEAD_DIM), k_a, v_a, kc_a, vc_a, a_sink[l])
        o_b = neighbourhood_latent(q_b, k_b, v_b, kc_b, vc_b, nat_bias[l])
        o_c = conformer_conv(u[..., OFF_C:], conv_w[l], conv_b[l], conv_ln_g[l], conv_ln_b[l])
        o = jnp.concatenate([o_a, o_b, o_c], axis=-1) @ w_out[l]
        x = layer_norm(DEEPNORM_ALPHA * x + g1 * o, ln1_g[l], ln1_b[l])
        h2 = modulate(x, sh2, sc2)
        x = layer_norm(DEEPNORM_ALPHA * x + g2 * ec_moe(h2, w_router[l], w_gate[l], w_up[l], w_down[l]),
                       ln2_g[l], ln2_b[l])
        if not last:
            ctx = ctx_new
    return x


DEPTH_2 = 1

NSA_HEADS = 8
NSA_KV_HEADS = 2
NSA_GROUP = NSA_HEADS // NSA_KV_HEADS
CMP_BLOCK = 32
CMP_STRIDE = 16
CMP_HIDDEN = 256
SEL_BLOCK = 64
SEL_TOPK = 8
WINDOW = 256
WIN_QBLOCK = 128
FORCE_SCORE = 1.0e4
RET_HEADS = 4
RET_QK_DIM = 64
RET_V_DIM = 128
RET_CHUNK = 128
D_FF = 4 * D_MODEL
ROPE_THETA = 10000.0
EPS = 1e-6
NEG_INF_2 = -1.0e30

NSA_Q_DIM = NSA_HEADS * HEAD_DIM
NSA_KV_DIM = NSA_KV_HEADS * HEAD_DIM
NSA_GATE_DIM = 3 * NSA_HEADS
RET_QK_WIDTH = RET_HEADS * RET_QK_DIM
RET_V_WIDTH = RET_HEADS * RET_V_DIM
MIX_WIDTH_2 = NSA_Q_DIM + RET_V_WIDTH
IN_SIZES = [NSA_Q_DIM, NSA_KV_DIM, NSA_KV_DIM, NSA_KV_DIM, NSA_KV_DIM, NSA_KV_DIM, NSA_KV_DIM,
            NSA_GATE_DIM, RET_QK_WIDTH, RET_QK_WIDTH, RET_V_WIDTH, RET_V_WIDTH]
IN_WIDTH_2 = sum(IN_SIZES)


def rms_norm(x, w):
    xf = x.astype(jnp.float32)
    y = xf * lax.rsqrt(jnp.mean(xf * xf, axis=-1, keepdims=True) + EPS)
    return (y * w.astype(jnp.float32)).astype(x.dtype)

def rope(x, pos):
    half = x.shape[-1] // 2
    inv = ROPE_THETA ** (-jnp.arange(half, dtype=jnp.float32) / half)
    ang = pos.astype(jnp.float32)[:, None] * inv[None, :]
    cos, sin = jnp.cos(ang), jnp.sin(ang)
    xf = x.astype(jnp.float32)
    x1, x2 = xf[..., :half], xf[..., half:]
    return jnp.concatenate([x1 * cos - x2 * sin, x2 * cos + x1 * sin], axis=-1).astype(x.dtype)

def masked_softmax(s, mask):
    s = jnp.where(mask, s.astype(jnp.float32), NEG_INF_2)
    p = jax.nn.softmax(s, axis=-1)
    return jnp.where(mask, p, 0.0)

def compress(blocks, w1, w2):
    b, g, n, l, d = blocks.shape
    return jax.nn.silu(blocks.reshape(b, g, n, l * d) @ w1) @ w2

def nsa_mixer(q, kc, vc, ks, vs, kw, vw, gates, q_norm_w, k_norm_w,
              cmp_pe_k, cmp_pe_v, cmp_wk1, cmp_wk2, cmp_wv1, cmp_wv2):
    B, S, _ = q.shape
    G, R, dh = NSA_KV_HEADS, NSA_GROUP, HEAD_DIM
    pos = jnp.arange(S)
    scale = dh ** -0.5
    q = q.reshape(B, S, G, R, dh).transpose(0, 2, 3, 1, 4)
    q = rope(rms_norm(q, q_norm_w), pos)

    def prep_k(k, w):
        k = k.reshape(B, S, G, dh).transpose(0, 2, 1, 3)
        return rope(rms_norm(k, w), pos)

    def prep_v(v):
        return v.reshape(B, S, G, dh).transpose(0, 2, 1, 3)

    kc, ks, kw = prep_k(kc, k_norm_w[0]), prep_k(ks, k_norm_w[1]), prep_k(kw, k_norm_w[2])
    vc, vs, vw = prep_v(vc), prep_v(vs), prep_v(vw)

    n_cmp = (S - CMP_BLOCK) // CMP_STRIDE + 1
    c_start = jnp.arange(n_cmp) * CMP_STRIDE
    cidx = c_start[:, None] + jnp.arange(CMP_BLOCK)[None, :]
    k_cmp = compress(kc[:, :, cidx] + cmp_pe_k, cmp_wk1, cmp_wk2)
    v_cmp = compress(vc[:, :, cidx] + cmp_pe_v, cmp_wv1, cmp_wv2)
    s_cmp = jnp.einsum('bgrqd,bgcd->bgrqc', q, k_cmp) * scale
    cmask = (c_start + CMP_BLOCK - 1)[None, :] <= pos[:, None]
    p_cmp = masked_softmax(s_cmp, cmask)
    o_cmp = jnp.einsum('bgrqc,bgcd->bgrqd', p_cmp.astype(v_cmp.dtype), v_cmp)

    n_blk = S // SEL_BLOCK
    jb = jnp.arange(n_blk)
    overlap = ((c_start[:, None] < (jb[None, :] + 1) * SEL_BLOCK)
               & (c_start[:, None] + CMP_BLOCK > jb[None, :] * SEL_BLOCK)).astype(jnp.float32)
    p_slc = jnp.einsum('bgrqc,cj->bgqj', p_cmp, overlap)
    cur = pos // SEL_BLOCK
    forced = (jb[None, :] == 0) | (jb[None, :] == cur[:, None]) | (jb[None, :] == cur[:, None] - 1)
    valid = jb[None, :] <= cur[:, None]
    score = jnp.where(forced, FORCE_SCORE, jnp.where(valid, p_slc, -1.0))
    n_sel = min(SEL_TOPK, n_blk)
    _, sel_idx = lax.top_k(score, n_sel)

    k_blocks = ks.reshape(B, G, n_blk, SEL_BLOCK, dh)
    v_blocks = vs.reshape(B, G, n_blk, SEL_BLOCK, dh)
    nq = S // SEL_BLOCK
    q_b = jnp.moveaxis(q.reshape(B, G, R, nq, SEL_BLOCK, dh), 3, 0)
    idx_b = jnp.moveaxis(sel_idx.reshape(B, G, nq, SEL_BLOCK, n_sel), 2, 0)
    t_b = pos.reshape(nq, SEL_BLOCK)
    bi = jnp.arange(B)[:, None, None, None]
    gi = jnp.arange(G)[None, :, None, None]
    n_keys = n_sel * SEL_BLOCK

    def sel_block(args):
        qc, ic, tc = args
        ksel = k_blocks[bi, gi, ic]
        vsel = v_blocks[bi, gi, ic]
        s = jnp.einsum('bgrqd,bgqnkd->bgrqnk', qc, ksel) * scale
        kpos = ic[..., None] * SEL_BLOCK + jnp.arange(SEL_BLOCK)
        mask = (kpos <= tc[None, None, :, None, None])[:, :, None]
        p = masked_softmax(s.reshape(B, G, R, SEL_BLOCK, n_keys),
                           mask.reshape(B, G, 1, SEL_BLOCK, n_keys))
        return jnp.einsum('bgrqk,bgqkd->bgrqd', p.astype(vsel.dtype),
                          vsel.reshape(B, G, SEL_BLOCK, n_keys, dh))

    o_sel = lax.map(sel_block, (q_b, idx_b, t_b))
    o_sel = jnp.moveaxis(o_sel, 0, 3).reshape(B, G, R, S, dh)

    nw = S // WIN_QBLOCK
    n_wk = WIN_QBLOCK + WINDOW
    widx = jnp.arange(nw)[:, None] * WIN_QBLOCK + jnp.arange(n_wk)[None, :]
    pad = ((0, 0), (0, 0), (WINDOW, 0), (0, 0))
    kwin = jnp.pad(kw, pad)[:, :, widx]
    vwin = jnp.pad(vw, pad)[:, :, widx]
    kpos = widx - WINDOW
    qw = q.reshape(B, G, R, nw, WIN_QBLOCK, dh)
    s_w = jnp.einsum('bgrcqd,bgckd->bgrcqk', qw, kwin) * scale
    tq = pos.reshape(nw, WIN_QBLOCK)
    diff = tq[:, :, None] - kpos[:, None, :]
    wmask = (diff >= 0) & (diff < WINDOW) & (kpos[:, None, :] >= 0)
    p_w = masked_softmax(s_w, wmask)
    o_win = jnp.einsum('bgrcqk,bgckd->bgrcqd', p_w.astype(vwin.dtype), vwin).reshape(B, G, R, S, dh)

    g = jax.nn.sigmoid(gates.astype(jnp.float32)).reshape(B, S, 3, G, R)
    g = g.transpose(2, 0, 3, 4, 1)[..., None].astype(q.dtype)
    o = g[0] * o_cmp + g[1] * o_sel + g[2] * o_win
    return o.transpose(0, 3, 1, 2, 4).reshape(B, S, NSA_Q_DIM)

def retention_mixer(q, k, v, gate, ret_norm_w):
    B, S, _ = q.shape
    H, dk, dv, C = RET_HEADS, RET_QK_DIM, RET_V_DIM, RET_CHUNK
    out_dtype = q.dtype
    pos = jnp.arange(S)
    q = rope(q.reshape(B, S, H, dk).transpose(0, 2, 1, 3), pos).astype(jnp.float32)
    k = (rope(k.reshape(B, S, H, dk).transpose(0, 2, 1, 3), pos).astype(jnp.float32)) * (dk ** -0.5)
    v = v.reshape(B, S, H, dv).transpose(0, 2, 1, 3).astype(jnp.float32)

    log_gamma = jnp.log(1.0 - 2.0 ** (-5.0 - jnp.arange(H, dtype=jnp.float32)))
    i = jnp.arange(C)
    d_int = i[:, None] - i[None, :]
    dmat = jnp.where(d_int >= 0,
                     jnp.exp(log_gamma[:, None, None] * jnp.maximum(d_int, 0).astype(jnp.float32)), 0.0)
    xi = jnp.exp(log_gamma[:, None] * (i + 1).astype(jnp.float32))[..., None]
    zeta = jnp.exp(log_gamma[:, None] * (C - 1 - i).astype(jnp.float32))[..., None]
    gamma_c = jnp.exp(log_gamma * C)[:, None, None]

    nc = S // C
    to_chunks = lambda t: jnp.moveaxis(t.reshape(B, H, nc, C, t.shape[-1]), 2, 0)

    def step(state, inp):
        qc, kc, vc = inp
        inner = jnp.einsum('bhqd,bhkd->bhqk', qc, kc) * dmat
        y = (jnp.einsum('bhqk,bhkv->bhqv', inner, vc)
             + jnp.einsum('bhqd,bhdv->bhqv', qc, state) * xi)
        state = gamma_c * state + jnp.einsum('bhkd,bhkv->bhdv', kc * zeta, vc)
        return state, y

    state0 = jnp.zeros((B, H, dk, dv), jnp.float32)
    _, y = lax.scan(step, state0, (to_chunks(q), to_chunks(k), to_chunks(v)))
    y = jnp.moveaxis(y, 0, 2).reshape(B, H, S, dv)
    mu = jnp.mean(y, axis=-1, keepdims=True)
    var = jnp.mean(jnp.square(y - mu), axis=-1, keepdims=True)
    y = (y - mu) * lax.rsqrt(var + EPS) * ret_norm_w.astype(jnp.float32)[None, :, None, :]
    y = y.transpose(0, 2, 1, 3).reshape(B, S, RET_V_WIDTH)
    return (jax.nn.silu(gate.astype(jnp.float32)) * y).astype(out_dtype)

def second_inputs(seed: int = 0) -> dict:
    key = jax.random.key(seed)
    ks = jax.random.split(key, 16)
    nrm = lambda k, shape, s: jax.random.normal(k, shape, jnp.float32) * s
    L = DEPTH_2
    return {
        "x": nrm(ks[0], (BATCH, SEQ, D_MODEL), 1.0),
        "ln1_w": 1.0 + nrm(ks[1], (L, D_MODEL), 0.02),
        "w_in": nrm(ks[2], (L, D_MODEL, IN_WIDTH_2), D_MODEL ** -0.5),
        "q_norm_w": 1.0 + nrm(ks[3], (L, HEAD_DIM), 0.02),
        "k_norm_w": 1.0 + nrm(ks[4], (L, 3, HEAD_DIM), 0.02),
        "cmp_pe_k": nrm(ks[5], (L, CMP_BLOCK, HEAD_DIM), 0.02),
        "cmp_pe_v": nrm(ks[6], (L, CMP_BLOCK, HEAD_DIM), 0.02),
        "cmp_wk1": nrm(ks[7], (L, CMP_BLOCK * HEAD_DIM, CMP_HIDDEN), (CMP_BLOCK * HEAD_DIM) ** -0.5),
        "cmp_wk2": nrm(ks[8], (L, CMP_HIDDEN, HEAD_DIM), CMP_HIDDEN ** -0.5),
        "cmp_wv1": nrm(ks[9], (L, CMP_BLOCK * HEAD_DIM, CMP_HIDDEN), (CMP_BLOCK * HEAD_DIM) ** -0.5),
        "cmp_wv2": nrm(ks[10], (L, CMP_HIDDEN, HEAD_DIM), CMP_HIDDEN ** -0.5),
        "ret_norm_w": 1.0 + nrm(ks[11], (L, RET_HEADS, RET_V_DIM), 0.02),
        "w_out": nrm(ks[12], (L, MIX_WIDTH_2, D_MODEL), MIX_WIDTH_2 ** -0.5),
        "ln2_w": 1.0 + nrm(ks[13], (L, D_MODEL), 0.02),
        "w_up": nrm(ks[14], (L, D_MODEL, D_FF), D_MODEL ** -0.5),
        "w_down": nrm(ks[15], (L, D_FF, D_MODEL), D_FF ** -0.5),
    }

def second_block(x, ln1_w, w_in, q_norm_w, k_norm_w, cmp_pe_k, cmp_pe_v, cmp_wk1, cmp_wk2,
              cmp_wv1, cmp_wv2, ret_norm_w, w_out, ln2_w, w_up, w_down):
    split_points = [int(p) for p in np.cumsum(IN_SIZES)[:-1]]
    h = x
    for l in range(DEPTH_2):
        xn = rms_norm(h, ln1_w[l])
        proj = xn @ w_in[l]
        (nq_, nkc, nvc, nks, nvs, nkw, nvw, ngate,
         rq, rk, rv, rg) = jnp.split(proj, split_points, axis=-1)
        o_nsa = nsa_mixer(nq_, nkc, nvc, nks, nvs, nkw, nvw, ngate, q_norm_w[l], k_norm_w[l],
                          cmp_pe_k[l], cmp_pe_v[l], cmp_wk1[l], cmp_wk2[l], cmp_wv1[l], cmp_wv2[l])
        o_ret = retention_mixer(rq, rk, rv, rg, ret_norm_w[l])
        mix = jnp.concatenate([o_nsa, o_ret], axis=-1)
        h = h + mix @ w_out[l]
        hn = rms_norm(h, ln2_w[l])
        h = h + jnp.square(jax.nn.relu(hn @ w_up[l])) @ w_down[l]
    return h


def setup_inputs(seed=0):
    out = dict(first_inputs(seed))
    for name, value in second_inputs(seed + 1).items():
        if name != "x":
            out[name + "_2"] = value
    return out


def reference(
    x, c, ctx, c_ctx, w_mod, b_mod, w_in, a_sink, nat_bias, conv_w, conv_b, conv_ln_g,
    conv_ln_b, w_out, ln1_g, ln1_b, w_router, w_gate, w_up, w_down, ln2_g, ln2_b, ln1_w_2,
    w_in_2, q_norm_w_2, k_norm_w_2, cmp_pe_k_2, cmp_pe_v_2, cmp_wk1_2, cmp_wk2_2, cmp_wv1_2,
    cmp_wv2_2, ret_norm_w_2, w_out_2, ln2_w_2, w_up_2, w_down_2,
):
    x = first_block(
        x, c, ctx, c_ctx, w_mod, b_mod, w_in, a_sink, nat_bias, conv_w, conv_b, conv_ln_g,
        conv_ln_b, w_out, ln1_g, ln1_b, w_router, w_gate, w_up, w_down, ln2_g, ln2_b,
    )
    return second_block(
        x, ln1_w_2, w_in_2, q_norm_w_2, k_norm_w_2, cmp_pe_k_2, cmp_pe_v_2, cmp_wk1_2,
        cmp_wk2_2, cmp_wv1_2, cmp_wv2_2, ret_norm_w_2, w_out_2, ln2_w_2, w_up_2, w_down_2,
    )


_drawn_inputs = setup_inputs


def setup_inputs(seed=0):
    import zlib

    import numpy as np

    out = dict(_drawn_inputs(seed))
    spreads = {}
    factors = {'ctx': 4.158,
     'b_mod': 6.589,
     'a_sink': 64.0,
     'nat_bias': 29.002,
     'conv_b': 8.0,
     'conv_ln_g': 8.0,
     'conv_ln_b': 8.0,
     'ln1_w_2': 3.171,
     'q_norm_w_2': 8.0,
     'k_norm_w_2': 8.0,
     'cmp_pe_k_2': 64.0,
     'cmp_pe_v_2': 64.0,
     'ret_norm_w_2': 6.546,
     'ln2_w_2': 9.972}
    for name, (base, spread) in spreads.items():
        noise = np.random.default_rng([zlib.crc32(name.encode()), seed]).standard_normal(out[name].shape)
        drawn = base * np.exp(spread * noise) if base else spread * noise
        out[name] = jnp.asarray(drawn.astype(out[name].dtype))
    for name, factor in factors.items():
        out[name] = (out[name] * factor).astype(out[name].dtype)
    return out
```

```python
from contextlib import ExitStack

import numpy as np

import concourse.bass as bass
from concourse import mybir
from concourse.alu_op_type import AluOpType as ALU

F32 = mybir.dt.float32
ACT = mybir.ActivationFunctionType
AX = mybir.AxisListType

P = 128
D = 1024
KD = D // P
SEQ, CTX = 512, 256
TX, TC = SEQ // P, CTX // P
T = TX + TC
LAYERS = 2
HD = 64
SCALE = HD ** -0.5
NEG = -1e30
A_HEADS, A_KV = 8, 2
A_GROUP = A_HEADS // A_KV
B_HEADS = 4
GRID = 64
ROWS = SEQ // GRID
RB_R, RB_C = 15, 31
C_CH, TAPS = 256, 31
HALF = TAPS // 2
IN_W = 2048
QKV_W = IN_W - 2 * C_CH
E = 16
CAP_X, CAP_C = 2 * SEQ // E, 2 * CTX // E
ALPHA = (2 * LAYERS) ** 0.25
LN_EPS = 1e-6
IN2_W = 2840
FF2 = 4096
N_CMP = (SEQ - 32) // 16 + 1
CMP_HID = 256
K1 = 1024


def shape_constants():
    q = np.arange(P)[:, None]
    k = np.arange(P)[None, :]
    eye = np.eye(P)
    lower = np.where(k <= q, 0.0, NEG)
    upper = np.where(k >= q, 0.0, NEG)
    above = np.where(k > q, 0.0, NEG)
    pos = np.arange(SEQ, dtype=np.float32)

    def tile(a):
        return a.reshape(TX, P, HD).transpose(1, 0, 2).reshape(P, TX * HD)

    inv = (10000.0 ** (-np.arange(16, dtype=np.float32) / np.float32(16))).astype(np.float32)
    ar = (pos // GRID)[:, None].astype(np.float32) * inv
    ac = (pos % GRID)[:, None].astype(np.float32) * inv
    cos1 = np.concatenate([np.cos(ar), np.cos(ar), np.cos(ac), np.cos(ac)], 1)
    sin1 = np.concatenate([-np.sin(ar), np.sin(ar), -np.sin(ac), np.sin(ac)], 1)
    inv = (10000.0 ** (-np.arange(32, dtype=np.float32) / np.float32(32))).astype(np.float32)
    an = pos[:, None] * inv
    cos2 = np.concatenate([np.cos(an), np.cos(an)], 1)
    sin2 = np.concatenate([-np.sin(an), np.sin(an)], 1)

    c = np.arange(P) % GRID
    start = np.clip(c - 8, 0, GRID - 16)[:, None]
    kc = np.arange(GRID)[None, :]
    near = np.where((kc >= start) & (kc < start + 16), 0.0, NEG)
    slots = np.broadcast_to(np.arange(64)[None, :], (P, 64))
    tri = np.where(q <= k, 1.0, 0.0)
    first = dict(ident=eye, lower=lower, upper=upper, near=near, slots=slots, tri=tri,
                 ones=np.ones((P, P)), cos=tile(cos1), sin=tile(sin1))

    cend = np.arange(32) * 16 + 31
    seen = np.zeros((P, TX, 32))
    some = np.zeros((P, TX))
    for t in range(TX):
        at = t * P + np.arange(P)
        seen[:, t] = np.where(cend[None, :] <= at[:, None], 0.0, NEG)
        some[:, t] = at >= 31
    lg = np.log(1.0 - 2.0 ** (-5.0 - np.arange(4)))
    decay = np.zeros((P, 4, P))
    for h in range(4):
        decay[:, h] = np.where(q <= k, np.exp(lg[h] * np.maximum(k - q, 0)), 0.0)
    i = np.arange(P)[:, None]
    xi = np.exp(lg[None, :] * (i + 1))
    zeta = np.exp(lg[None, :] * (P - 1 - i)) * SCALE
    gc = np.broadcast_to(np.exp(lg * P)[None, :], (P, 4))
    second = dict(ident=eye, lower=lower, above=above, seen=seen.reshape(P, -1), some=some,
                  decay=decay.reshape(P, -1), xi=xi, zeta=zeta, gc=gc,
                  cos=tile(cos2), sin=tile(sin2))

    def pack(parts):
        at, where = 0, {}
        for name, a in parts.items():
            where[name] = (at, at + a.shape[1])
            at += a.shape[1]
        return np.concatenate([np.asarray(a, np.float32) for a in parts.values()], 1), where

    return pack(first), pack(second)


def build(nc, t_in, out_ap, debug=None):
    (c1, at1), (c2, at2) = shape_constants()
    NC = max(c1.shape[1], c2.shape[1])
    ctx = ExitStack()

    def sb(name, n):
        return ctx.enter_context(nc.sbuf_tensor(name, [P, n], F32))

    arena = sb("arena", 49 * K1 + 512)
    at = [0]

    def region(n):
        a = at[0]
        at[0] += n
        return a

    RES0, HT0, LNX0 = region(6 * K1), region(6 * K1), region(6 * K1)
    EXTRA0 = region(7 * K1 + 512)
    RING0 = region(24 * K1)

    def mem(start, *dims, parts=P, p0=0):
        n = int(np.prod(dims))
        v = arena[p0:p0 + parts, start:start + n]
        if len(dims) == 2:
            v = v.rearrange("p (a b) -> p a b", b=dims[1])
        if len(dims) == 3:
            v = v.rearrange("p (a b c) -> p a b c", b=dims[1], c=dims[2])
        return v

    consts = sb("consts", NC)
    small = sb("small", 704)
    mod = sb("mod", 96)
    res = mem(RES0, T, D)
    ht = mem(HT0, KD, SEQ + CTX)
    lnx = mem(LNX0, T, D)

    pair = [ctx.enter_context(nc.psum_tensor(f"pair{i}", [P, 1024], F32)) for i in range(4)]
    bank = [pair[i // 2][:, (i % 2) * 512:(i % 2) * 512 + 512] for i in range(8)]

    mod_rows = nc.dram_tensor("mod_rows", [2, 2, D], F32, kind="Internal").ap()
    bias_rows = nc.dram_tensor("bias_rows", [LAYERS, 64 * B_HEADS * RB_R * RB_C], F32, kind="Internal").ap()

    class Signal:
        def __init__(self, name):
            self.sem = ctx.enter_context(nc.semaphore(name))
            self.base = 0

        def upto(self, i, each=1):
            return self.base + (i + 1) * each

        def advance(self, total):
            self.base += total

    known = {}

    def signal(name):
        if name not in known:
            known[name] = Signal(name)
        return known[name]

    class Chain:

        def __init__(self, eng, name):
            self.eng, self.s = eng, signal(name)

        def link(self, ins):
            self.s.advance(1)
            ins.then_inc(self.s.sem, 1)
            self.eng.wait_ge(self.s.sem, self.s.base)

    def cst(where, name):
        a, b = where[name]
        return consts[:, a:b]

    def load(pairs, name):
        s = signal(name)
        with nc.Block() as block:
            @block.sync
            def _(sp):
                for dst, src in pairs:
                    sp.dma_start(dst, src).then_inc(s.sem, 16)
                sp.wait_ge(s.sem, s.upto(len(pairs) - 1, 16))
        s.advance(16 * len(pairs))

    def products(groups, loads=(), frees=True):
        full, taken, landed = signal("bank_full"), signal("bank_taken"), [signal(f"landed{i}") for i in range(8)]
        takers = [g % 2 for g in range(len(groups))]
        base_landed = [s.base for s in landed]

        def value(n):
            return base_landed[n % 8] + 16 * (n // 8 + 1)

        counts = {0: [], 1: []}
        for g in range(len(groups)):
            counts[g % 2].append(g)
        taken = [signal("bank_taken_act"), signal("bank_taken_dve")]

        with nc.Block() as block:
            @block.sync
            def _(sp):
                for n, (dst, src, after) in enumerate(loads):
                    if after > 0:
                        sp.wait_ge(full.sem, full.upto(after - 1))
                    sp.dma_start(dst, src).then_inc(landed[n % 8].sem, 16)

            @block.tensor
            def _(pe):
                seen = 0
                for g, group in enumerate(groups):
                    for n in range(seen, group.get("need", 0)):
                        pe.wait_ge(landed[n % 8].sem, value(n))
                    seen = max(seen, group.get("need", 0))
                    if g >= 8:
                        pe.wait_ge(taken[g % 2].sem, taken[g % 2].upto((g - 8) // 2))
                    ps = bank[g % 8]
                    mm = group["mm"]
                    for i, (col, lhs, rhs) in enumerate(mm):
                        p0 = group.get("p0", 0)
                        if rhs is None:
                            k, m = lhs.shape[0], lhs.shape[-1]
                            ins = nc.tensor.transpose(ps[0:m, col:col + k], lhs, cst(at1, "ident")[0:k, 0:k])
                        else:
                            m = lhs.shape[-1]
                            n = int(np.prod(rhs.shape[1:]))
                            o = ps[p0:p0 + m, col:col + n]
                            if len(rhs.shape) == 3:
                                o = o.rearrange("p (a b) -> p a b", b=rhs.shape[2])
                            ins = nc.tensor.matmul(
                                o, lhsT=lhs, rhs=rhs,
                                start=i == 0 or mm[i - 1][0] != col,
                                stop=i == len(mm) - 1 or mm[i + 1][0] != col)
                    ins.then_inc(full.sem, 1)

            @block.scalar
            def _(act):
                chain = Chain(act, "act_chain")
                for i, g in enumerate(counts[0]):
                    act.wait_ge(full.sem, full.upto(g))
                    o = groups[g]["out"]
                    for j, (psv, dst, *more) in enumerate(o["parts"](bank[g % 8])):
                        if o["kind"] == "copy":
                            ins = nc.scalar.activation(dst, psv, ACT.Copy)
                        elif o["kind"] == "affine":
                            ins = nc.scalar.activation(dst, psv, ACT.Identity, bias=more[1], scale=more[0])
                        elif o["kind"] == "scale":
                            ins = nc.scalar.activation(dst, psv, ACT.Copy, scale=more[0])
                        elif o["kind"] == "relu2":
                            chain.link(nc.scalar.activation(dst, psv, ACT.Relu))
                            ins = nc.scalar.activation(dst, dst, ACT.Square)
                    ins.then_inc(taken[0].sem, 1)

            @block.vector
            def _(dve):
                chain = Chain(dve, "dve_chain")
                for i, g in enumerate(counts[1]):
                    dve.wait_ge(full.sem, full.upto(g))
                    o = groups[g]["out"]
                    for j, (psv, dst, *more) in enumerate(o["parts"](bank[g % 8])):
                        if o["kind"] == "copy":
                            ins = nc.vector.tensor_copy(dst, psv)
                        elif o["kind"] == "affine":
                            ins = nc.vector.tensor_scalar(dst, psv, more[0], more[1], ALU.mult, ALU.add)
                        elif o["kind"] == "scale":
                            ins = nc.vector.tensor_scalar(dst, psv, more[0], None, ALU.mult)
                        elif o["kind"] == "relu2":
                            chain.link(nc.vector.tensor_scalar(dst, psv, 0.0, None, ALU.max))
                            ins = nc.vector.tensor_tensor(dst, dst, dst, ALU.mult)
                    ins.then_inc(taken[1].sem, 1)
        full.advance(len(groups))
        taken[0].advance(len(counts[0]))
        taken[1].advance(len(counts[1]))
        for n in range(len(loads)):
            landed[n % 8].advance(16)

    def out(kind, *parts):
        def views(ps):
            for (r0, r1, c0, c1, dst, *more) in parts:
                v = ps[r0:r1, c0:c1]
                if len(dst.shape) == 3:
                    v = v.rearrange("p (a b) -> p a b", b=dst.shape[2])
                yield (v, dst, *more)
        return dict(kind=kind, parts=views)

    def normalise(rows, eps, post=(), mean=True, width=D):
        n = len(rows)
        halves = (width + 511) // 512
        hw = width // halves
        stats = small[:, 0:n * halves * 6].rearrange("p (n k) -> p n k", k=6 * halves)
        mv = small[:, 288:288 + 2 * n].rearrange("p (n k) -> p n k", k=2)
        ve, sd, rs = (small[:, 352 + 32 * i:352 + 32 * i + n] for i in range(3))
        v_ready, v_root, gained = signal("var_ready"), signal("root_ready"), signal("row_normal")
        finished = signal("row_finished")
        with nc.Block() as block:
            @block.vector
            def _(dve):
                chain = Chain(dve, "dve_chain")
                for i, (src, _) in enumerate(rows):
                    for h in range(halves):
                        ins = nc.vector.bn_stats(stats[:, i, 6 * h:6 * h + 6], src[:, h * hw:(h + 1) * hw])
                chain.link(ins)
                for i in range(n):
                    ins = nc.vector.bn_aggr(mv[:, i, :], stats[:, i, :])
                chain.link(ins)
                if mean:
                    nc.vector.tensor_scalar(ve, mv[:, :, 1], eps, None, ALU.add).then_inc(v_ready.sem, 1)
                else:
                    chain.link(nc.vector.tensor_tensor(ve, mv[:, :, 0], mv[:, :, 0], ALU.mult))
                    nc.vector.scalar_tensor_tensor(ve, ve, eps, mv[:, :, 1], ALU.add, ALU.add).then_inc(v_ready.sem, 1)
                dve.wait_ge(v_root.sem, v_root.upto(0))
                chain.link(nc.vector.reciprocal(rs, sd))
                for i, (src, dst) in enumerate(rows):
                    if mean:
                        ins = nc.vector.tensor_scalar(dst, src, mv[:, i, 0:1], rs[:, i:i + 1], ALU.subtract, ALU.mult)
                    else:
                        ins = nc.vector.tensor_scalar(dst, src, rs[:, i:i + 1], None, ALU.mult)
                    if post:
                        chain.link(ins)
                        ins = nc.vector.tensor_tensor(dst, dst, post[i][0], ALU.mult)
                    ins.then_inc(gained.sem, 1)

            @block.scalar
            def _(act):
                act.wait_ge(v_ready.sem, v_ready.upto(0))
                nc.scalar.activation(sd, ve, ACT.Sqrt).then_inc(v_root.sem, 1)

            @block.gpsimd
            def _(pool):
                if post:
                    for i, (_, dst) in enumerate(rows):
                        pool.wait_ge(gained.sem, gained.upto(i))
                        nc.gpsimd.tensor_tensor(dst, dst, post[i][1], ALU.add).then_inc(finished.sem, 1)
        v_ready.advance(1)
        v_root.advance(1)
        gained.advance(n)
        if post:
            finished.advance(n)

    def turn_rows(src, scale, shift, chunks):
        groups = []
        for k in range(KD):
            for stream, (t0, t1) in enumerate(((0, TX), (TX, T))):
                if t0 >= chunks:
                    continue
                mm = [((t - t0) * P, src[:, t, k * P:(k + 1) * P], None) for t in range(t0, t1)]
                n = (t1 - t0) * P
                dst = ht[:, k, t0 * P:t1 * P]
                if shift is None:
                    o = out("scale", (0, P, 0, n, dst, scale(stream, k)))
                else:
                    o = out("affine", (0, P, 0, n, dst, scale(stream, k), shift(stream, k)))
                groups.append(dict(mm=mm, out=o))
        products(groups)

    def rotate(jobs, where, seg):
        done, half_done = signal("rotated"), signal("swapped")
        tmp = mem(RING0 + 23 * K1, 2, 512)
        with nc.Block() as block:
            @block.gpsimd
            def _(pool):
                for i, (src, dst, t, heads) in enumerate(jobs):
                    if i >= 2:
                        pool.wait_ge(done.sem, done.upto(i - 2))
                    cosv = cst(where, "cos")[:, t * HD:(t + 1) * HD].unsqueeze(1).to_broadcast([P, heads, HD])
                    tv = tmp[:, i % 2, 0:heads * HD].rearrange("p (h d) -> p h d", d=HD)
                    nc.gpsimd.tensor_tensor(tv, src, cosv, ALU.mult).then_inc(half_done.sem, 1)

            @block.vector
            def _(dve):
                chain = Chain(dve, "dve_chain")
                for i, (src, dst, t, heads) in enumerate(jobs):
                    for a in range(0, HD, 2 * seg):
                        for s in range(2):
                            o, x = a + s * seg, a + (1 - s) * seg
                            sinv = cst(where, "sin")[:, t * HD + o:t * HD + o + seg].unsqueeze(1).to_broadcast([P, heads, seg])
                            ins = nc.vector.tensor_tensor(dst[:, :, o:o + seg], src[:, :, x:x + seg], sinv, ALU.mult)
                    chain.link(ins)
                    dve.wait_ge(half_done.sem, half_done.upto(i))
                    tv = tmp[:, i % 2, 0:heads * HD].rearrange("p (h d) -> p h d", d=HD)
                    nc.vector.tensor_tensor(dst, dst, tv, ALU.add).then_inc(done.sem, 1)
        done.advance(len(jobs))
        half_done.advance(len(jobs))

    def attend(units, work, where, biases=()):
        n = len(units)
        sc = mem(work, 2, 768)
        pt = mem(work + 1536, 2, 768)
        bt = mem(work + 3072, 2, 512)
        mx = small[:, 0:4]
        nm = small[:, 4:8]
        rs = small[:, 8:12]
        es = small[:, 12:16]
        den = small[:, 16:20]
        rc = small[:, 20:24]
        scored, maxed, probs = signal("scored"), signal("maxed"), signal("probs")
        turned, turned_sb, valued, written = (signal(x) for x in ("turned", "turned_sb", "valued", "written"))
        tile_in, tile_ready = [signal("bias_in0"), signal("bias_in1")], signal("bias_ready")
        kb = {u: i for i, u in enumerate(sorted(biases))} if biases else {}
        order = sorted(kb)
        ident = cst(where, "ident")
        wide = pair[2]
        po = [pair[3][:, 0:512], pair[3][:, 512:1024]]

        with nc.Block() as block:
            @block.sync
            def _(sp):
                for i, u in enumerate(order):
                    if i >= 2:
                        sp.wait_ge(maxed.sem, maxed.upto(order[i - 2]))
                    for r in range(2):
                        sp.dma_start(bt[64 * r:64 * r + 64, i % 2, :].rearrange("p (a b) -> p a b", b=GRID),
                                     biases[u][r]).then_inc(tile_in[i % 2].sem, 16)

            @block.gpsimd
            def _(pool):
                chain = Chain(pool, "pool_chain")
                for i, u in enumerate(order):
                    pool.wait_ge(tile_in[i % 2].sem, tile_in[i % 2].upto(i // 2, 32))
                    chain.link(nc.gpsimd.tensor_scalar(bt[:, i % 2, :], bt[:, i % 2, :], 1.0 / SCALE, None, ALU.mult))
                    tv = bt[:, i % 2, :].rearrange("p (a b) -> p a b", b=GRID)
                    near = cst(where, "near").unsqueeze(1).to_broadcast([P, ROWS, GRID])
                    nc.gpsimd.tensor_tensor(tv, tv, near, ALU.add).then_inc(tile_ready.sem, 1)

            @block.tensor
            def _(pe):
                for i in range(n + 2):
                    if i < n:
                        if i >= 2:
                            pe.wait_ge(maxed.sem, maxed.upto(i - 2))
                        for col, kT in units[i]["keys"]:
                            m = kT.shape[-1]
                            ins = nc.tensor.matmul(pair[i % 2][:, col:col + m], lhsT=units[i]["q"], rhs=kT,
                                                   start=True, stop=True)
                        ins.then_inc(scored.sem, 1)
                    j = i - 1
                    if 0 <= j < n:
                        pe.wait_ge(probs.sem, probs.upto(j))
                        if j >= 1:
                            pe.wait_ge(turned_sb.sem, turned_sb.upto(j - 1))
                        nk = units[j]["n"]
                        for c in range(0, nk, P):
                            w = min(P, nk - c)
                            ins = nc.tensor.transpose(wide[0:w, c:c + P], sc[:, j % 2, c:c + w], ident)
                        ins.then_inc(turned.sem, 1)
                    j = i - 2
                    if 0 <= j < n:
                        pe.wait_ge(turned_sb.sem, turned_sb.upto(j))
                        if j >= 2:
                            pe.wait_ge(written.sem, written.upto(j - 2))
                        v = units[j]["v"]
                        for c, vc in enumerate(v):
                            w = vc.shape[0]
                            ins = nc.tensor.matmul(po[j % 2][:, 0:HD], lhsT=pt[0:w, j % 2, c * P:(c + 1) * P], rhs=vc,
                                                   start=c == 0, stop=c == len(v) - 1)
                        ins.then_inc(valued.sem, 1)

            @block.vector
            def _(dve):
                chain = Chain(dve, "dve_chain")
                for i in range(n + 2):
                    if i < n:
                        u = units[i]
                        dve.wait_ge(scored.sem, scored.upto(i))
                        if i >= 2:
                            dve.wait_ge(turned.sem, turned.upto(i - 2))
                        if i in kb:
                            dve.wait_ge(tile_ready.sem, tile_ready.upto(kb[i]))
                        for pc, c, m, bias in u["evac"]:
                            if bias is None:
                                ins = nc.vector.tensor_copy(sc[:, i % 2, c:c + m], pair[i % 2][:, pc:pc + m])
                            else:
                                if i in kb:
                                    bias = bt[:, kb[i] % 2, :]
                                ins = nc.vector.tensor_tensor(sc[:, i % 2, c:c + m], pair[i % 2][:, pc:pc + m], bias, ALU.add)
                        chain.link(ins)
                        k = i % 4
                        chain.link(nc.vector.tensor_reduce(mx[:, k:k + 1], sc[:, i % 2, 0:u["n"]], AX.X, ALU.max))
                        if u.get("sink") is None:
                            nc.vector.tensor_scalar(nm[:, k:k + 1], mx[:, k:k + 1], -SCALE, None, ALU.mult).then_inc(maxed.sem, 1)
                        else:
                            chain.link(nc.vector.tensor_scalar(nm[:, k:k + 1], mx[:, k:k + 1], -SCALE, None, ALU.mult))
                            nc.vector.tensor_scalar(nm[:, k:k + 1], nm[:, k:k + 1], u["nsink"], None, ALU.min).then_inc(maxed.sem, 1)
                    j = i - 2
                    if 0 <= j < n:
                        u = units[j]
                        k = j % 4
                        dve.wait_ge(valued.sem, valued.upto(j))
                        total = rs[:, k:k + 1]
                        if u.get("sink") is not None:
                            chain.link(nc.vector.tensor_tensor(den[:, k:k + 1], rs[:, k:k + 1], es[:, k:k + 1], ALU.add))
                            total = den[:, k:k + 1]
                        chain.link(nc.vector.reciprocal(rc[:, k:k + 1], total))
                        if u.get("gate") is not None:
                            chain.link(nc.vector.tensor_tensor(rc[:, k:k + 1], rc[:, k:k + 1], u["gate"], ALU.mult))
                        if u.get("add"):
                            ins = nc.vector.scalar_tensor_tensor(u["out"], po[j % 2][:, 0:HD], rc[:, k:k + 1], u["out"],
                                                                 ALU.mult, ALU.add)
                        else:
                            ins = nc.vector.tensor_scalar(u["out"], po[j % 2][:, 0:HD], rc[:, k:k + 1], None, ALU.mult)
                        ins.then_inc(written.sem, 1)

            @block.scalar
            def _(act):
                for i in range(n + 1):
                    if i < n:
                        u = units[i]
                        k = i % 4
                        act.wait_ge(maxed.sem, maxed.upto(i))
                        if i >= 4:
                            act.wait_ge(written.sem, written.upto(i - 4))
                        if u.get("sink") is not None:
                            nc.scalar.activation(es[:, k:k + 1], u["sink"], ACT.Exp, bias=nm[:, k:k + 1])
                        nc.scalar.activation(sc[:, i % 2, 0:u["n"]], sc[:, i % 2, 0:u["n"]], ACT.Exp,
                                             bias=nm[:, k:k + 1], scale=SCALE, accum_out=rs[:, k:k + 1]).then_inc(probs.sem, 1)
                    j = i - 1
                    if 0 <= j < n:
                        act.wait_ge(turned.sem, turned.upto(j))
                        if j >= 2:
                            act.wait_ge(valued.sem, valued.upto(j - 2))
                        nk = units[j]["n"]
                        cols = (nk + P - 1) // P * P
                        rows = P if nk >= P else nk
                        for c in range(0, cols, 512):
                            m = min(512, cols - c)
                            ins = nc.scalar.activation(pt[0:rows, j % 2, c:c + m], wide[0:rows, c:c + m], ACT.Copy)
                        ins.then_inc(turned_sb.sem, 1)
        for s in (scored, maxed, probs, turned, turned_sb, valued, written):
            s.advance(n)
        tile_in[0].advance(32 * ((len(order) + 1) // 2))
        tile_in[1].advance(32 * (len(order) // 2))
        tile_ready.advance(len(order))

    def adaln(l):
        cond = small[:, 0:16].rearrange("p (k s) -> p k s", s=2)
        cs = small[:, 16:32].rearrange("p (k s) -> p k s", s=2)
        bm = small[:, 32:80]
        rows = small[0:8, 128:640].rearrange("p (s g d) -> p s g d", s=2, g=2)
        m3 = mod[:, :].rearrange("p (m s) -> p m s", s=2)
        panel = [mem(RING0 + 8 * K1 * i, KD, 1024) for i in range(3)]
        n_panels = 6
        cond_in, cond_silu = signal("cond_in"), signal("cond_silu")
        panel_in = [signal(f"panel_in{i}") for i in range(3)]
        panel_full, panel_taken = signal("panel_full"), signal("panel_taken")
        gates_turned, gates_sb, gates_out = signal("gates_turned"), signal("gates_sb"), signal("gates_out")
        wm = t_in["w_mod"][l].rearrange("(k p) n -> p k n", p=P)
        with nc.Block() as block:
            @block.sync
            def _(sp):
                sp.dma_start(small[:, 0:16], t_in["cond_cols"]).then_inc(cond_in.sem, 16)
                sp.dma_start(bm, t_in["b_mod_cols"][l]).then_inc(cond_in.sem, 16)
                for m in range(n_panels):
                    if m >= 3:
                        sp.wait_ge(panel_full.sem, panel_full.upto(m - 3))
                    sp.dma_start(panel[m % 3], wm[:, :, m * 1024:(m + 1) * 1024]).then_inc(panel_in[m % 3].sem, 16)
                sp.wait_ge(gates_sb.sem, gates_sb.upto(0))
                for s in range(2):
                    for g in range(2):
                        sp.dma_start(mod_rows[s, g].rearrange("(k d) -> k d", d=P), rows[:, s, g, :]).then_inc(gates_out.sem, 16)
                sp.wait_ge(gates_out.sem, gates_out.upto(3, 16))

            @block.scalar
            def _(act):
                act.wait_ge(cond_in.sem, cond_in.upto(1, 16))
                nc.scalar.activation(cs, cond, ACT.Silu).then_inc(cond_silu.sem, 1)

            @block.tensor
            def _(pe):
                pe.wait_ge(cond_silu.sem, cond_silu.upto(0))
                for m in range(n_panels):
                    pe.wait_ge(panel_in[m % 3].sem, panel_in[m % 3].upto(m // 3, 16))
                    if m >= 2:
                        pe.wait_ge(panel_taken.sem, panel_taken.upto(m - 2))
                    for j in range(8):
                        for k in range(KD):
                            ins = nc.tensor.matmul(bank[m % 2][:, 2 * j:2 * j + 2], lhsT=panel[m % 3][:, k, j * P:(j + 1) * P],
                                                   rhs=cs[:, k, :], start=k == 0, stop=k == KD - 1)
                    ins.then_inc(panel_full.sem, 1)
                pe.wait_ge(panel_taken.sem, panel_taken.upto(n_panels - 1))
                for s in range(2):
                    for g in range(2):
                        a = 16 + 24 * g
                        ins = nc.tensor.transpose(bank[2][0:8, (2 * s + g) * P:(2 * s + g + 1) * P],
                                                  m3[:, a:a + 8, s], cst(at1, "ident"))
                ins.then_inc(gates_turned.sem, 1)

            @block.vector
            def _(dve):
                for m in range(n_panels):
                    dve.wait_ge(panel_full.sem, panel_full.upto(m))
                    b = bm[:, 8 * m:8 * m + 8].unsqueeze(2).to_broadcast([P, 8, 2])
                    o = m3[:, 8 * m:8 * m + 8, :]
                    v = bank[m % 2][:, 0:16].rearrange("p (a b) -> p a b", b=2)
                    one = 1.0 if m in (1, 4) else 0.0
                    nc.vector.scalar_tensor_tensor(o, v, one, b, ALU.add, ALU.add).then_inc(panel_taken.sem, 1)
                dve.wait_ge(gates_turned.sem, gates_turned.upto(0))
                nc.vector.tensor_copy(small[0:8, 128:640], bank[2][0:8, :]).then_inc(gates_sb.sem, 1)
        cond_in.advance(32)
        cond_silu.advance(1)
        for s in panel_in:
            s.advance(32)
        panel_full.advance(6)
        panel_taken.advance(6)
        gates_turned.advance(1)
        gates_sb.advance(1)
        gates_out.advance(64)

    def convolve(l, glu, padded, y, wcol, bcol, chunks):
        width = 2 * HALF + SEQ + (2 * HALF + CTX if chunks > TX else 0)
        span = width - 2 * HALF
        w_in_, cleared, sig, ready = signal("taps_in"), signal("pads_cleared"), signal("gate_sigmoid"), signal("glu_ready")
        with nc.Block() as block:
            @block.sync
            def _(sp):
                sp.dma_start(wcol, t_in["conv_w_cols"][l]).then_inc(w_in_.sem, 16)
                sp.dma_start(bcol, t_in["conv_b_cols"][l]).then_inc(w_in_.sem, 16)

            @block.gpsimd
            def _(pool):
                nc.gpsimd.memset(padded[:, :, 0:width], 0.0).then_inc(cleared.sem, 1)

            @block.scalar
            def _(act):
                nc.scalar.activation(glu[:, 2:4, 0:chunks * P], glu[:, 2:4, 0:chunks * P], ACT.Sigmoid).then_inc(sig.sem, 1)

            @block.vector
            def _(dve):
                chain = Chain(dve, "dve_chain")
                dve.wait_ge(cleared.sem, cleared.upto(0))
                dve.wait_ge(sig.sem, sig.upto(0))
                ins = nc.vector.tensor_tensor(padded[:, :, HALF:HALF + SEQ], glu[:, 0:2, 0:SEQ], glu[:, 2:4, 0:SEQ], ALU.mult)
                if chunks > TX:
                    a = 3 * HALF + SEQ
                    ins = nc.vector.tensor_tensor(padded[:, :, a:a + CTX], glu[:, 0:2, SEQ:], glu[:, 2:4, SEQ:], ALU.mult)
                chain.link(ins)
                dve.wait_ge(w_in_.sem, w_in_.upto(1, 16))
                for j in range(TAPS):
                    for c in range(2):
                        x = padded[:, c, j:j + span]
                        o = y[:, c, 0:span]
                        if j == 0:
                            ins = nc.vector.tensor_scalar(o, x, wcol[:, c, 0:1], bcol[:, c:c + 1], ALU.mult, ALU.add)
                        else:
                            ins = nc.vector.scalar_tensor_tensor(o, x, wcol[:, c, j:j + 1], o, ALU.mult, ALU.add)
                    chain.link(ins)
        w_in_.advance(32)
        cleared.advance(1)
        sig.advance(1)
        return span

    def silu_rows(rows):
        s = signal("row_silu")
        with nc.Block() as block:
            @block.scalar
            def _(act):
                for dst, src in rows:
                    nc.scalar.activation(dst, src, ACT.Silu).then_inc(s.sem, 1)
        s.advance(len(rows))

    def gate_rows(jobs, alpha):
        gated, summed = signal("branch_gated"), signal("branch_added")
        with nc.Block() as block:
            @block.gpsimd
            def _(pool):
                for i, (r, b, g) in enumerate(jobs):
                    if g is not None:
                        nc.gpsimd.tensor_tensor(b, b, g, ALU.mult).then_inc(gated.sem, 1)

            @block.vector
            def _(dve):
                for i, (r, b, g) in enumerate(jobs):
                    if g is not None:
                        dve.wait_ge(gated.sem, gated.upto(i))
                    nc.vector.scalar_tensor_tensor(r, r, alpha, b, ALU.mult, ALU.add).then_inc(summed.sem, 1)
        if jobs[0][2] is not None:
            gated.advance(len(jobs))
        summed.advance(len(jobs))

    def route(l, chunks, wr, logit, aff, pos, msk, af, at_, work, best):
        ntok = chunks * P
        products([dict(mm=[(0, ht[:, k, t * P:(t + 1) * P], wr[:, k, :]) for k in range(KD)],
                       out=out("copy", (0, P, 0, E, logit[:, t, :]))) for t in range(chunks)])
        lg = logit[:, 0:chunks, :]
        a3 = aff[:, 0:chunks, :]
        m1 = af[:, 0:chunks]
        shifted, powered, soft = signal("logits_shifted"), signal("logits_exp"), signal("affinity")
        with nc.Block() as block:
            @block.vector
            def _(dve):
                chain = Chain(dve, "dve_chain")
                chain.link(nc.vector.tensor_reduce(m1, lg, AX.X, ALU.max))
                nc.vector.tensor_tensor(lg, lg, m1.unsqueeze(2).to_broadcast([P, chunks, E]), ALU.subtract).then_inc(shifted.sem, 1)
                dve.wait_ge(powered.sem, powered.upto(0))
                chain.link(nc.vector.tensor_reduce(m1, lg, AX.X, ALU.add))
                chain.link(nc.vector.reciprocal(m1, m1))
                nc.vector.tensor_tensor(a3, lg, m1.unsqueeze(2).to_broadcast([P, chunks, E]), ALU.mult).then_inc(soft.sem, 1)

            @block.scalar
            def _(act):
                act.wait_ge(shifted.sem, shifted.upto(0))
                nc.scalar.activation(lg, lg, ACT.Exp).then_inc(powered.sem, 1)
        shifted.advance(1)
        powered.advance(1)
        soft.advance(1)
        groups = []
        for t0, t1 in ((0, TX), (TX, T))[:1 if chunks == TX else 2]:
            groups.append(dict(mm=[((t - t0) * P, aff[:, t, :], None) for t in range(t0, t1)],
                               out=out("copy", (0, E, 0, (t1 - t0) * P, at_[:, t0 * P:t1 * P]))))
        products(groups)
        picked = signal("picked")
        streams = [(0, SEQ, CAP_X), (SEQ, SEQ + CTX, CAP_C)][:1 if chunks == TX else 2]
        with nc.Block() as block:
            @block.vector
            def _(dve):
                chain = Chain(dve, "dve_chain")
                for a, b, cap in streams:
                    for _ in range(cap // 8):
                        chain.link(nc.vector.max(best, at_[:, a:b]))
                        chain.link(nc.vector.match_replace(at_[:, a:b], best, at_[:, a:b], -1.0))
                nc.vector.tensor_scalar(work, at_[:, 0:ntok], 0.0, None, ALU.is_lt).then_inc(picked.sem, 1)
        picked.advance(1)
        products([dict(mm=[(t * E, work[:, t * P:(t + 1) * P], None) for t in range(chunks)],
                       out=out("copy", (0, P, 0, chunks * E, msk[:, 0:chunks, :])))])
        groups = []
        mm = []
        for t in range(chunks):
            t0 = 0 if t < TX else TX
            for s in range(t0, t + 1):
                mm.append((t * E, cst(at1, "tri" if s == t else "ones"), msk[:, s, :]))
        groups.append(dict(mm=mm, out=out("copy", (0, P, 0, chunks * E, pos[:, 0:chunks, :]))))
        products(groups)
        slot = signal("slots_ready")
        with nc.Block() as block:
            @block.vector
            def _(dve):
                chain = Chain(dve, "dve_chain")
                p3, k3 = pos[:, 0:chunks, :], msk[:, 0:chunks, :]
                chain.link(nc.vector.tensor_tensor(p3, p3, k3, ALU.mult))
                nc.vector.tensor_scalar(p3, p3, -1.0, None, ALU.add).then_inc(slot.sem, 1)
        slot.advance(1)

    def experts(l, chunks, aff, pos, acc, base):
        cx, cc = CAP_X, (CAP_C if chunks > TX else 0)
        S = cx + cc
        a = base
        def take(*dims, parts=P):
            nonlocal a
            v = mem(a, *dims, parts=parts)
            a += int(np.prod(dims))
            return v
        xs, hid, sg = take(KD, S), take(KD, S), take(KD, S)
        y = take(D, parts=S)
        sel = take(TX, cx)
        gat = take(TX, cx)
        selc, gatc = take(TC, 32), take(TC, 96)
        gt = take(TX * P, parts=cx)
        gtc = take(TC * P, parts=96)
        pe_col, ae_col = take(T), take(T)
        assert a <= EXTRA0 + 7 * K1 + 512, a - EXTRA0
        piece = [mem(RING0 + 4 * K1 * i, KD, 512) for i in range(6)]
        src = {}
        for j in range(6):
            w = t_in[("w_gate", "w_up", "w_down")[j // 2]][l]
            src[j] = w.rearrange("e (k p) n -> p e k n", p=P)[:, :, :, (j % 2) * 512:(j % 2) * 512 + 512]
        landed = [signal(f"piece_in{j}") for j in range(6)]
        used = signal("piece_used")
        picks, gathered, xs_ready = signal("picks_ready"), signal("gathered"), signal("tokens_ready")
        gates_turned, gates_sb = signal("gate_turned"), signal("gate_sb")
        silu_ready, hid_ready = signal("silu_ready"), signal("hid_ready")
        y_ready, spread, added = (signal(x) for x in ("down_ready", "spread", "added"))
        cleared, dve_c = signal("sums_cleared"), signal("dve_chain")
        n_out = 2 * chunks
        sc2 = [mod[:, :].rearrange("p (m s) -> p m s", s=2)[:, 32:40, s] for s in range(2)]
        sh2 = [mod[:, :].rearrange("p (m s) -> p m s", s=2)[:, 24:32, s] for s in range(2)]
        xs_ps = [bank[0][:, 0:4 * S].rearrange("p (c s) -> p c s", s=S), bank[1][:, 0:4 * S].rearrange("p (c s) -> p c s", s=S)]
        LINKS = 2
        with nc.Block() as block:
            @block.gpsimd
            def _(pool):
                for t in range(chunks):
                    nc.gpsimd.memset(acc[:, t, :], 0.0).then_inc(cleared.sem, 1)
                nc.gpsimd.memset(gatc, 0.0).then_inc(cleared.sem, 1)

            @block.sync
            def _(sp):
                for j in range(6):
                    sp.dma_start(piece[j], src[j][:, 0, :, :]).then_inc(landed[j].sem, 16)
                with sp.Fori(0, E - 1) as e:
                    for j in range(6):
                        sp.wait_ge(used.sem, e * 6 + (used.base + j + 1))
                        sp.dma_start(piece[j], src[j][:, bass.ds(e + 1, 1), :, :].rearrange("p o k n -> p (o k) n")).then_inc(landed[j].sem, 16)

            @block.vector
            def _(dve):
                dve.wait_ge(cleared.sem, cleared.upto(chunks))
                dve_base = dve_c.base
                def turn(e, first):
                    links = [0]

                    def link(ins):
                        links[0] += 1
                        ins.then_inc(dve_c.sem, 1)
                        dve.wait_ge(dve_c.sem, e * LINKS + (dve_base + links[0]))

                    if not first:
                        dve.wait_ge(gathered.sem, e + gathered.base)
                    nc.vector.tensor_copy(pe_col[:, 0:chunks].unsqueeze(2), pos[:, 0:chunks, bass.ds(e, 1)])
                    link(nc.vector.tensor_copy(ae_col[:, 0:chunks].unsqueeze(2), aff[:, 0:chunks, bass.ds(e, 1)]))
                    if not first:
                        dve.wait_ge(gates_turned.sem, e + gates_turned.base)
                    for t in range(TX):
                        nc.vector.tensor_scalar(sel[:, t, :], cst(at1, "slots"), pe_col[:, t:t + 1], None, ALU.is_equal)
                        ins = nc.vector.tensor_scalar(gat[:, t, :], cst(at1, "slots"), pe_col[:, t:t + 1], ae_col[:, t:t + 1],
                                                      ALU.is_equal, ALU.mult)
                    for t in range(TX, chunks):
                        nc.vector.tensor_scalar(selc[:, t - TX, :], cst(at1, "slots")[:, 0:32], pe_col[:, t:t + 1], None, ALU.is_equal)
                        ins = nc.vector.tensor_scalar(gatc[:, t - TX, 64:96], cst(at1, "slots")[:, 0:32], pe_col[:, t:t + 1],
                                                      ae_col[:, t:t + 1], ALU.is_equal, ALU.mult)
                    ins.then_inc(picks.sem, 1)
                    dve.wait_ge(gathered.sem, e + (gathered.base + 1))
                    cuts = [(0, cx, 0)] + ([(cx, S, 1)] if cc else [])
                    for c0, c1, s in cuts:
                        for h in range(2):
                            b = sc2[s][:, 4 * h:4 * h + 4].unsqueeze(2).to_broadcast([P, 4, c1 - c0])
                            ins = nc.vector.tensor_tensor(xs[:, 4 * h:4 * h + 4, c0:c1], xs_ps[h][:, :, c0:c1], b, ALU.mult)
                    link(ins)
                    for c0, c1, s in cuts:
                        b = sh2[s].unsqueeze(2).to_broadcast([P, KD, c1 - c0])
                        ins = nc.vector.tensor_tensor(xs[:, :, c0:c1], xs[:, :, c0:c1], b, ALU.add)
                    ins.then_inc(xs_ready.sem, 1)
                    dve.wait_ge(silu_ready.sem, e + (silu_ready.base + 1))
                    dve.wait_ge(used.sem, e * 6 + (used.base + 4))
                    for h in range(2):
                        ins = nc.vector.tensor_tensor(hid[:, 4 * h:4 * h + 4, :], sg[:, 4 * h:4 * h + 4, :],
                                                      bank[4 + h][:, 0:4 * S].rearrange("p (c s) -> p c s", s=S), ALU.mult)
                    ins.then_inc(hid_ready.sem, 1)
                    for i in range(n_out):
                        t, h = i // 2, i % 2
                        dve.wait_ge(spread.sem, e * n_out + (spread.base + i + 1))
                        o = acc[:, t, h * 512:(h + 1) * 512]
                        ins = nc.vector.tensor_tensor(o, o, bank[2 + i % 4], ALU.add)
                        ins.then_inc(added.sem, 1)
                    dve.wait_ge(added.sem, e * n_out + (added.base + n_out))

                turn(0, True)
                with dve.Fori(1, E) as e:
                    turn(e, False)

            @block.scalar
            def _(act):
                def turn(e, first):
                    act.wait_ge(gates_turned.sem, e + (gates_turned.base + 1))
                    if not first:
                        act.wait_ge(spread.sem, e * n_out + spread.base)
                    ins = nc.scalar.activation(gt, bank[6][0:cx, :], ACT.Copy)
                    if cc:
                        ins = nc.scalar.activation(gtc, bank[7][0:96, 0:TC * P], ACT.Copy)
                    ins.then_inc(gates_sb.sem, 1)
                    act.wait_ge(used.sem, e * 6 + (used.base + 2))
                    if not first:
                        act.wait_ge(hid_ready.sem, e + hid_ready.base)
                    for h in range(2):
                        ins = nc.scalar.activation(sg[:, 4 * h:4 * h + 4, :],
                                                   bank[2 + h][:, 0:4 * S].rearrange("p (c s) -> p c s", s=S), ACT.Silu)
                    ins.then_inc(silu_ready.sem, 1)
                    for h in range(2):
                        act.wait_ge(used.sem, e * 6 + (used.base + 5 + h))
                        nc.scalar.activation(y[:, h * 512:(h + 1) * 512], bank[6 + h][0:S, :], ACT.Copy).then_inc(y_ready.sem, 1)

                turn(0, True)
                with act.Fori(1, E) as e:
                    turn(e, False)

            @block.tensor
            def _(pe):
                def turn(e, first):
                    if not first:
                        pe.wait_ge(y_ready.sem, e * 2 + y_ready.base)
                    pe.wait_ge(picks.sem, e + (picks.base + 1))
                    for c in range(KD):
                        o = xs_ps[c // 4][:, c % 4, :]
                        for t in range(TX):
                            ins = nc.tensor.matmul(o[:, 0:cx], lhsT=lnx[:, t, c * P:(c + 1) * P], rhs=sel[:, t, :],
                                                   start=t == 0, stop=t == TX - 1)
                        for t in range(TX, chunks):
                            ins = nc.tensor.matmul(o[:, cx:S], lhsT=lnx[:, t, c * P:(c + 1) * P], rhs=selc[:, t - TX, :],
                                                   start=t == TX, stop=t == T - 1)
                    ins.then_inc(gathered.sem, 1)
                    for t in range(TX):
                        ins = nc.tensor.transpose(bank[6][0:cx, t * P:(t + 1) * P], gat[:, t, :], cst(at1, "ident"))
                    for t in range(TX, chunks):
                        ins = nc.tensor.transpose(bank[7][0:96, (t - TX) * P:(t - TX + 1) * P], gatc[:, t - TX, :], cst(at1, "ident"))
                    ins.then_inc(gates_turned.sem, 1)
                    pe.wait_ge(xs_ready.sem, e + (xs_ready.base + 1))
                    if not first:
                        pe.wait_ge(added.sem, e * n_out + added.base)
                    for j in range(4):
                        pe.wait_ge(landed[j].sem, e * 16 + (landed[j].base + 16))
                        for f in range(4):
                            for k in range(KD):
                                ins = nc.tensor.matmul(bank[2 + j][:, f * S:(f + 1) * S], lhsT=piece[j][:, k, f * P:(f + 1) * P],
                                                       rhs=xs[:, k, :], start=k == 0, stop=k == KD - 1)
                        ins.then_inc(used.sem, 1)
                    pe.wait_ge(hid_ready.sem, e + (hid_ready.base + 1))
                    pe.wait_ge(gates_sb.sem, e + (gates_sb.base + 1))
                    for h in range(2):
                        pe.wait_ge(landed[4 + h].sem, e * 16 + (landed[4 + h].base + 16))
                        for f in range(KD):
                            ins = nc.tensor.matmul(bank[6 + h][0:S, :], lhsT=hid[:, f, :], rhs=piece[4 + h][:, f, :],
                                                   start=f == 0, stop=f == KD - 1)
                        ins.then_inc(used.sem, 1)
                    pe.wait_ge(y_ready.sem, e * 2 + (y_ready.base + 2))
                    for i in range(n_out):
                        t, h = i // 2, i % 2
                        if i >= 4:
                            pe.wait_ge(added.sem, e * n_out + (added.base + i - 3))
                        if t < TX:
                            lhs, rhs = gt[:, t * P:(t + 1) * P], y[0:cx, h * 512:(h + 1) * 512]
                        else:
                            lhs, rhs = gtc[:, (t - TX) * P:(t - TX + 1) * P], y[0:96, h * 512:(h + 1) * 512]
                        nc.tensor.matmul(bank[2 + i % 4], lhsT=lhs, rhs=rhs, start=True, stop=True).then_inc(spread.sem, 1)
                turn(0, True)
                with pe.Fori(1, E) as e:
                    turn(e, False)
        cleared.advance(chunks + 1)
        for s in landed:
            s.advance(16 * E)
        used.advance(6 * E)
        for s in (picks, gathered, xs_ready, gates_turned, gates_sb, silu_ready, hid_ready):
            s.advance(E)
        y_ready.advance(2 * E)
        spread.advance(n_out * E)
        added.advance(n_out * E)
        dve_c.advance(LINKS * E)

    def finish_debug(name, v):
        if debug != name:
            return False
        s = signal("debug_out")
        with nc.Block() as block:
            @block.sync
            def _(sp):
                sp.dma_start(out_dbg(v), v).then_inc(s.sem, 16)
                sp.wait_ge(s.sem, s.upto(0, 16))
        s.advance(16)
        return True

    def out_dbg(v):
        return nc.dram_tensor("dbg", list(v.shape), F32, kind="ExternalOutput").ap()

    def head_norms(u2, hx, sq, wt):
        H = A_HEADS + 6
        w_in_, squared, v_ready, v_root, normed = (signal(x) for x in (
            "head_w_in", "squared", "var_ready", "root_ready", "heads_normed"))
        ss, ve, rs = (small[:, 64 * i:64 * i + TX * H].rearrange("p (t h) -> p t h", h=H) for i in range(3))
        qn, kn = t_in["q_norm_w_2"], t_in["k_norm_w_2"]

        def spans(t):
            yield u2[:, t, 0:512], lambda b: b[:, t, 0:8, :].rearrange("p h d -> p (h d)"), (0, 8)
            ks = u2[:, t, 512:1280].rearrange("p (i n) -> p i n", n=256)[:, :, 0:128]
            yield ks, lambda b: b[:, t, 8:14, :].rearrange("p (i g) d -> p i (g d)", g=2), (8, 14)

        with nc.Block() as block:
            @block.sync
            def _(sp):
                sp.dma_start(wt[:, 0:8, :], bass.AP(qn.tensor, qn.offset, [[0, P], [0, 8], [1, HD]])).then_inc(w_in_.sem, 16)
                for i in range(3):
                    sp.dma_start(wt[:, 8 + 2 * i:10 + 2 * i, :],
                                 bass.AP(kn.tensor, kn.offset + i * HD, [[0, P], [0, 2], [1, HD]])).then_inc(w_in_.sem, 16)

            @block.gpsimd
            def _(pool):
                for t in range(TX):
                    for x, at_buf, _ in spans(t):
                        nc.gpsimd.tensor_tensor(at_buf(sq), x, x, ALU.mult).then_inc(squared.sem, 1)

            @block.scalar
            def _(act):
                act.wait_ge(v_ready.sem, v_ready.upto(0))
                nc.scalar.activation(ve, ve, ACT.Sqrt).then_inc(v_root.sem, 1)

            @block.vector
            def _(dve):
                chain = Chain(dve, "dve_chain")
                for t in range(TX):
                    dve.wait_ge(squared.sem, squared.upto(2 * t + 1))
                    ins = nc.vector.tensor_reduce(ss[:, t, :], sq[:, t, :, :], AX.X, ALU.add)
                chain.link(ins)
                nc.vector.tensor_scalar(ve, ss, 1.0 / HD, LN_EPS, ALU.mult, ALU.add).then_inc(v_ready.sem, 1)
                dve.wait_ge(v_root.sem, v_root.upto(0))
                chain.link(nc.vector.reciprocal(rs, ve))
                dve.wait_ge(w_in_.sem, w_in_.upto(3, 16))
                for t in range(TX):
                    for h in range(H):
                        if h < 8:
                            x = u2[:, t, h * HD:(h + 1) * HD]
                        else:
                            a = 512 + 256 * ((h - 8) // 2) + HD * (h % 2)
                            x = u2[:, t, a:a + HD]
                        ins = nc.vector.scalar_tensor_tensor(hx[:, t, h, :], x, rs[:, t, h:h + 1], wt[:, h, :], ALU.mult, ALU.mult)
                    ins.then_inc(normed.sem, 1)
        w_in_.advance(64)
        squared.advance(2 * TX)
        v_ready.advance(1)
        v_root.advance(1)
        normed.advance(TX)

    def retain(u2, rr, kz, rqt, rkt, it, state, mixb):
        units = [(t, h) for t in range(TX) for h in range(4)]
        n = len(units)
        zetad, inner_full, inner_sb, full, taken = (signal(x) for x in (
            "keys_decayed", "inner_full", "inner_decayed", "unit_full", "unit_taken"))

        def place(h):
            return slice(64 * (h % 2), 64 * (h % 2) + 64), h // 2

        with nc.Block() as block:
            @block.gpsimd
            def _(pool):
                for t, h in units:
                    nc.gpsimd.tensor_scalar(kz[:, t, h, :], rr[:, t, 4 + h, :], cst(at2, "zeta")[:, h:h + 1], None,
                                            ALU.mult).then_inc(zetad.sem, 1)

            @block.tensor
            def _(pe):
                for i in range(n + 1):
                    if i < n:
                        t, h = units[i]
                        rows, j = place(h)
                        if i >= 2:
                            pe.wait_ge(inner_sb.sem, inner_sb.upto(i - 2))
                        cols = slice(t * P, (t + 1) * P)
                        nc.tensor.matmul(bank[i % 2][:, 0:P], lhsT=rkt[rows, j, cols], rhs=rqt[rows, j, cols],
                                         start=True, stop=True).then_inc(inner_full.sem, 1)
                    u = i - 1
                    if u >= 0:
                        t, h = units[u]
                        rows, j = place(h)
                        v = u2[:, t, 1816 + h * P:1816 + (h + 1) * P]
                        pe.wait_ge(inner_sb.sem, inner_sb.upto(u))
                        if u >= 2:
                            pe.wait_ge(taken.sem, taken.upto(u - 2))
                        ins = nc.tensor.matmul(bank[2 + u % 2][:, 0:P], lhsT=it[:, u % 2, :], rhs=v, start=True, stop=True)
                        if t > 0:
                            ins = nc.tensor.matmul(bank[4 + u % 2][:, 0:P], lhsT=rqt[rows, j, t * P:(t + 1) * P],
                                                   rhs=state[rows, j, :], start=True, stop=True)
                        if t < TX - 1:
                            pe.wait_ge(zetad.sem, zetad.upto(u))
                            ins = nc.tensor.matmul(bank[6 + u % 2][rows, 0:P], lhsT=kz[:, t, h, :], rhs=v, start=True, stop=True)
                        ins.then_inc(full.sem, 1)

            @block.vector
            def _(dve):
                chain = Chain(dve, "dve_chain")
                for i in range(n + 1):
                    if i < n:
                        t, h = units[i]
                        dve.wait_ge(inner_full.sem, inner_full.upto(i))
                        if i >= 2:
                            dve.wait_ge(full.sem, full.upto(i - 2))
                        nc.vector.tensor_tensor(it[:, i % 2, :], bank[i % 2][:, 0:P],
                                                cst(at2, "decay")[:, h * P:(h + 1) * P], ALU.mult).then_inc(inner_sb.sem, 1)
                    u = i - 1
                    if u >= 0:
                        t, h = units[u]
                        rows, j = place(h)
                        y = mixb[:, t, 512 + h * P:512 + (h + 1) * P]
                        dve.wait_ge(full.sem, full.upto(u))
                        ins = nc.vector.tensor_copy(y, bank[2 + u % 2][:, 0:P])
                        if t > 0:
                            chain.link(ins)
                            ins = nc.vector.scalar_tensor_tensor(y, bank[4 + u % 2][:, 0:P], cst(at2, "xi")[:, h:h + 1], y,
                                                                 ALU.mult, ALU.add)
                        if t == 0:
                            ins = nc.vector.tensor_copy(state[rows, j, :], bank[6 + u % 2][rows, 0:P])
                        elif t < TX - 1:
                            ins = nc.vector.scalar_tensor_tensor(state[rows, j, :], state[rows, j, :], cst(at2, "gc")[rows, h:h + 1],
                                                                 bank[6 + u % 2][rows, 0:P], ALU.mult, ALU.add)
                        ins.then_inc(taken.sem, 1)
        zetad.advance(n)
        for s in (inner_full, inner_sb, full, taken):
            s.advance(n)

    def sparse_attention_block():
        lncol = small[:, 688:704].rearrange("p (i k) -> p i k", k=KD)
        load([(consts[:, 0:c2.shape[1]], t_in["consts2"]), (lncol[:, 0, :], t_in["ln1_w_cols"][0]),
              (lncol[:, 1, :], t_in["ln2_w_cols"][0])], "second_in")
        normalise([(res[:, t, :], lnx[:, t, :]) for t in range(TX)], LN_EPS, mean=False)
        turn_rows(lnx, lambda s, k: lncol[:, 0, k:k + 1], None, TX)
        u2 = mem(LNX0, TX, IN2_W)
        w = mem(RING0, KD, IN2_W)
        w_src = t_in["w_in_2"][0].rearrange("(k p) n -> p k n", p=P)
        cuts = [(a, min(a + 512, IN2_W)) for a in range(0, IN2_W, 512)]
        groups = []
        for i, (a, b) in enumerate(cuts):
            for t in range(TX):
                groups.append(dict(need=i + 1,
                                   mm=[(0, ht[:, k, t * P:(t + 1) * P], w[:, k, a:b]) for k in range(KD)],
                                   out=out("copy", (0, P, 0, b - a, u2[:, t, a:b]))))
        products(groups, [(w[:, :, a:b], w_src[:, :, a:b], 0) for a, b in cuts])
        H = A_HEADS + 6
        hx = mem(RING0, TX * H, HD).rearrange("p (t h) d -> p t h d", h=H)
        sq = mem(RING0 + 3584, TX * H, HD).rearrange("p (t h) d -> p t h d", h=H)
        qr, kr = mem(RING0 + 7168, TX, 512), mem(RING0 + 9216, TX, 384)
        rr = mem(RING0 + 10752, TX, 512)
        wt = mem(RING0 + 12800, H, HD)
        dup = mem(RING0 + 13696, TX, 512)
        head_norms(u2, hx, sq, wt)
        jobs = []
        for t in range(TX):
            for g in range(A_KV):
                jobs.append((hx[:, t, 4 * g:4 * g + 4, :], qr[:, t, :].rearrange("p (j g d) -> p g j d", g=A_KV, d=HD)[:, g], t, 4))
            jobs.append((hx[:, t, 8:14, :], kr[:, t, :].rearrange("p (h d) -> p h d", d=HD), t, 6))
            jobs.append((u2[:, t, 1304:1816].rearrange("p (h d) -> p h d", d=HD), rr[:, t, :].rearrange("p (h d) -> p h d", d=HD), t, 8))
        rotate(jobs, at2, 32)
        gts = mem(RING0 + 23 * K1, TX, 24)
        doubled, gated = signal("rows_doubled"), signal("branch_gates")
        with nc.Block() as block:
            @block.scalar
            def _(act):
                nc.scalar.activation(gts, u2[:, :, 1280:1304], ACT.Sigmoid).then_inc(gated.sem, 1)

            @block.vector
            def _(dve):
                for t in range(TX):
                    for i, src in enumerate((kr[:, t, 0:128], u2[:, t, 640:768])):
                        d = dup[:, t, 256 * i:256 * i + 256].rearrange("p (g c d) -> p g c d", g=2, c=2)
                        x = src.rearrange("p (g d) -> p g d", d=HD)
                        for c in range(2):
                            nc.vector.tensor_copy(d[:, :, c, :], x).then_inc(doubled.sem, 1)
                dve.wait_ge(gated.sem, gated.upto(0))
                some = cst(at2, "some").unsqueeze(2).to_broadcast([P, TX, 8])
                nc.vector.tensor_tensor(gts[:, :, 0:8], gts[:, :, 0:8], some, ALU.mult).then_inc(doubled.sem, 1)
        doubled.advance(4 * TX + 1)
        gated.advance(1)
        qt, kst, kwt = mem(RING0 + 15744, 4, SEQ), mem(RING0 + 17792, SEQ), mem(RING0 + 18304, SEQ)
        rqt, rkt = mem(RING0 + 18816, 2, SEQ), mem(RING0 + 19840, 2, SEQ)
        kc2 = mem(RING0 + 20864, 4, SEQ)
        groups = []

        def turn(src, dst, scale=None):
            mm = [(t * P, src(t), None) for t in range(TX)]
            o = out("copy", (0, P, 0, SEQ, dst)) if scale is None else out("scale", (0, P, 0, SEQ, dst, scale))
            groups.append(dict(mm=mm, out=o))

        for j in range(4):
            turn(lambda t: qr[:, t, j * P:(j + 1) * P], qt[:, j, :])
        turn(lambda t: kr[:, t, 128:256], kst)
        turn(lambda t: kr[:, t, 256:384], kwt)
        for j in range(2):
            turn(lambda t: rr[:, t, j * P:(j + 1) * P], rqt[:, j, :])
            turn(lambda t: rr[:, t, 256 + j * P:256 + (j + 1) * P], rkt[:, j, :], SCALE)
        for i in range(4):
            groups.append(dict(mm=[(t * P, dup[:, t, i * P:(i + 1) * P], None) for t in range(TX)],
                               out=out("copy", (0, 64, 0, SEQ, kc2[0:64, i, :]), (64, P, 1, SEQ, kc2[64:P, i, 0:SEQ - 1]))))
        products(groups)
        w1 = [mem(RING0 + 4096 * i, 16, CMP_HID) for i in range(2)]
        w2 = [mem(RING0 + 8192 + 128 * i, 2, HD) for i in range(2)]
        pe_ = [mem(RING0 + 8448 + 16 * i, 16) for i in range(2)]
        hraw = mem(RING0 + 8480, 4, 65)
        hc = mem(RING0 + 8740, 4, 2 * N_CMP)
        kcmp, vcmp = mem(RING0 + 8988, N_CMP + 1), mem(RING0 + 9020, 2, HD, parts=N_CMP)
        loads = []
        for i, kind in enumerate(("k", "v")):
            loads.append((w1[i], t_in[f"cmp_w{kind}1_2"][0].rearrange("(j p) n -> p j n", p=P), 0))
            loads.append((w2[i], t_in[f"cmp_w{kind}2_2"][0].rearrange("(j p) n -> p j n", p=P), 0))
            loads.append((pe_[i], t_in[f"cmp_pe_{kind}_cols"][0], 0))
        groups = []
        for i in range(2):
            for half in range(2):
                lhs = [w1[i][:, j, half * P:(half + 1) * P] for j in range(16)]
                mm = [(0, lhs[j], kc2[:, 2 * i:2 * i + 2, 2 * j:2 * j + 16 * (N_CMP - 1) + 1:16]) for j in range(16)]
                mm += [(2 * N_CMP, lhs[j], pe_[i][:, j:j + 1]) for j in range(16)]
                groups.append(dict(need=3 * i + 3, mm=mm, out=out("copy", (0, P, 0, 2 * N_CMP + 1, hraw[:, 2 * i + half, 0:2 * N_CMP + 1]))))
        products(groups, loads)
        silued = signal("hidden_silu")
        with nc.Block() as block:
            @block.scalar
            def _(act):
                for i in range(4):
                    nc.scalar.activation(hc[:, i, :], hraw[:, i, 0:2 * N_CMP], ACT.Silu,
                                         bias=hraw[:, i, 2 * N_CMP:2 * N_CMP + 1]).then_inc(silued.sem, 1)
        silued.advance(4)
        groups = []
        for g in range(2):
            cols = slice(g * N_CMP, (g + 1) * N_CMP)
            groups.append(dict(p0=64 * g, mm=[(0, w2[0][:, h, :], hc[:, h, cols]) for h in range(2)],
                               out=out("copy", (64 * g, 64 * g + 64, 0, N_CMP, kcmp[64 * g:64 * g + 64, 0:N_CMP]))))
            groups.append(dict(mm=[(0, hc[:, 2 + h, cols], w2[1][:, h, :]) for h in range(2)],
                               out=out("copy", (0, N_CMP, 0, HD, vcmp[:, g, :]))))
        products(groups)
        mixb = mem(HT0, TX, D)
        units = []
        for branch in range(3):
            for h in range(A_HEADS):
                g, j = h // 4, h % 4
                rows = slice(64 * g, 64 * g + 64)
                for t in range(TX):
                    u = dict(q=qt[rows, j, t * P:(t + 1) * P], out=mixb[:, t, h * HD:(h + 1) * HD],
                             gate=gts[:, t, branch * 8 + h:branch * 8 + h + 1], add=branch > 0)
                    if branch == 0:
                        seen = cst(at2, "seen")[:, t * 32:t * 32 + N_CMP]
                        u.update(keys=[(0, kcmp[rows, 0:N_CMP])], evac=[(0, 0, N_CMP, seen)], n=N_CMP, v=[vcmp[:, g, :]])
                    else:
                        s0 = 0 if branch == 1 else max(0, t - 2)
                        kT = kst if branch == 1 else kwt
                        m = t - s0
                        vcol = slice((896 if branch == 1 else 1152) + g * HD, (896 if branch == 1 else 1152) + (g + 1) * HD)
                        evac = []
                        for s in range(s0, t + 1):
                            bias = cst(at2, "lower") if s == t else cst(at2, "above") if branch == 2 and s == t - 2 else None
                            if bias is None and evac and evac[-1][3] is None:
                                evac[-1] = (evac[-1][0], evac[-1][1], evac[-1][2] + P, None)
                            else:
                                evac.append(((s - s0) * P, (s - s0) * P, P, bias))
                        u.update(keys=[(0, kT[rows, s0 * P:(t + 1) * P])], evac=evac, n=(t + 1 - s0) * P,
                                 v=[u2[:, s, vcol] for s in range(s0, t + 1)])
                    units.append(u)
        attend(units, RING0, at2)
        kz = mem(RING0, TX * 4, HD).rearrange("p (t h) d -> p t h d", h=4)
        it, state = mem(RING0 + 1024, 2, P), mem(RING0 + 1280, 2, P)
        retain(u2, rr.rearrange("p t (h d) -> p t h d", d=HD), kz, rqt, rkt, it, state, mixb)
        normalise([(mixb[:, t, 512 + h * P:512 + (h + 1) * P],) * 2 for t in range(TX) for h in range(4)], LN_EPS, width=P)
        rw = mem(RING0 + 2048, 512)
        load([(rw, t_in["ret_norm_w_2"][0].rearrange("h d -> (h d)").partition_broadcast(P))], "ret_norm_in")
        weighted, gate_silu, gated = signal("rows_weighted"), signal("ret_gate_silu"), signal("rows_gated")
        with nc.Block() as block:
            @block.gpsimd
            def _(pool):
                for t in range(TX):
                    nc.gpsimd.tensor_tensor(mixb[:, t, 512:D], mixb[:, t, 512:D], rw, ALU.mult).then_inc(weighted.sem, 1)

            @block.scalar
            def _(act):
                for t in range(TX):
                    nc.scalar.activation(u2[:, t, 2328:2840], u2[:, t, 2328:2840], ACT.Silu).then_inc(gate_silu.sem, 1)

            @block.vector
            def _(dve):
                for t in range(TX):
                    dve.wait_ge(weighted.sem, weighted.upto(t))
                    dve.wait_ge(gate_silu.sem, gate_silu.upto(t))
                    nc.vector.tensor_tensor(mixb[:, t, 512:D], mixb[:, t, 512:D], u2[:, t, 2328:2840], ALU.mult).then_inc(gated.sem, 1)
        for s in (weighted, gate_silu, gated):
            s.advance(TX)
        if finish_debug("mix2", mixb):
            return
        wo = mem(RING0, KD, D)
        mixt = mem(RING0 + 8 * K1, KD, SEQ)
        products([dict(mm=[(t * P, mixb[:, t, k * P:(k + 1) * P], None) for t in range(TX)],
                       out=out("copy", (0, P, 0, SEQ, mixt[:, k, :]))) for k in range(KD)])
        branch = lnx
        products([dict(need=1, mm=[(0, mixt[:, k, t * P:(t + 1) * P], wo[:, k, n * 512:(n + 1) * 512]) for k in range(KD)],
                       out=out("copy", (0, P, 0, 512, branch[:, t, n * 512:(n + 1) * 512]))) for t in range(TX) for n in range(2)],
                 [(wo, t_in["w_out_2"][0].rearrange("(k p) n -> p k n", p=P), 0)])
        gate_rows([(res[:, t, :], branch[:, t, :], None) for t in range(TX)], 1.0)
        normalise([(res[:, t, :], lnx[:, t, :]) for t in range(TX)], LN_EPS, mean=False)
        turn_rows(lnx, lambda s, k: lncol[:, 1, k:k + 1], None, TX)
        NF = FF2 // P
        hid = [mem(LNX0 + 512 * c, 512) if c < 27 else mem(RING0 + 20 * K1 + 512 * (c - 27), 512) for c in range(NF)]
        slot = [mem(RING0 + 4 * K1 * i, KD, 512) for i in range(4)]
        wu = t_in["w_up_2"][0].rearrange("(k p) n -> p k n", p=P)
        products([dict(need=c // 4 + 1, mm=[(0, slot[c // 4 % 4][:, k, (c % 4) * P:(c % 4 + 1) * P], ht[:, k, 0:SEQ]) for k in range(KD)],
                       out=out("relu2", (0, P, 0, SEQ, hid[c]))) for c in range(NF)],
                 [(slot[n % 4], wu[:, :, n * 512:(n + 1) * 512], 4 * (n - 3) if n >= 4 else 0) for n in range(8)])
        wd = t_in["w_down_2"][0].rearrange("(c p) n -> p c n", p=P)
        slot = [mem(RING0 + 4 * K1 * i, 4, D) for i in range(5)]
        down_in = [signal(f"down_in{i}") for i in range(5)]
        used, finished, stored = signal("down_used"), signal("out_ready"), signal("stored")
        with nc.Block() as block:
            @block.sync
            def _(sp):
                for n in range(8):
                    if n >= 5:
                        sp.wait_ge(used.sem, used.upto(n - 5))
                    sp.dma_start(slot[n % 5], wd[:, 4 * n:4 * n + 4, :]).then_inc(down_in[n % 5].sem, 16)
                for t in range(TX):
                    sp.wait_ge(finished.sem, finished.upto(2 * t + 1))
                    sp.dma_start(final.rearrange("o (t p) d -> p (o t) d", p=P)[:, t, :], res[:, t, :]).then_inc(stored.sem, 16)
                sp.wait_ge(stored.sem, stored.upto(TX - 1, 16))

            @block.tensor
            def _(pe):
                for n in range(8):
                    pe.wait_ge(down_in[n % 5].sem, down_in[n % 5].upto(n // 5, 16))
                    for c in range(4 * n, 4 * n + 4):
                        for t in range(TX):
                            for m in range(2):
                                ins = nc.tensor.matmul(bank[2 * t + m], lhsT=hid[c][:, t * P:(t + 1) * P],
                                                       rhs=slot[n % 5][:, c % 4, m * 512:(m + 1) * 512],
                                                       start=c == 0, stop=c == NF - 1)
                    ins.then_inc(used.sem, 1)

            @block.vector
            def _(dve):
                dve.wait_ge(used.sem, used.upto(7))
                for i in range(8):
                    o = res[:, i // 2, (i % 2) * 512:(i % 2 + 1) * 512]
                    nc.vector.tensor_tensor(o, o, bank[i], ALU.add).then_inc(finished.sem, 1)


    final = out_ap
    with ctx:
        load([(consts[:, 0:c1.shape[1]], t_in["consts1"]),
              (res[:, 0:TX, :], t_in["x"][0].rearrange("(t p) d -> p t d", p=P)),
              (res[:, TX:T, :], t_in["ctx"][0].rearrange("(t p) d -> p t d", p=P))]
             + [(bias_rows[l].rearrange("(c n) -> c n", c=64),
                 t_in["nat_bias"][l].rearrange("h r c -> (h r c)").partition_broadcast(64)) for l in range(LAYERS)],
             "start_in")
        m3 = mod[:, :].rearrange("p (m s) -> p m s", s=2)
        for l in range(LAYERS):
            last = l == LAYERS - 1
            nt = TX if last else T
            adaln(l)
            if finish_debug(f"mod{l}", mod[:, :]):
                return
            normalise([(res[:, t, :], lnx[:, t, :]) for t in range(T)], LN_EPS)
            turn_rows(lnx, lambda s, k: m3[:, 8 + k, s:s + 1], lambda s, k: m3[:, k, s:s + 1], T)
            if finish_debug(f"ht{l}", ht[:, :, :]):
                return
            w = mem(RING0, KD, IN_W)
            qkv = mem(LNX0, T, QKV_W)
            glu = mem(LNX0 + T * QKV_W, 4, SEQ + CTX)
            w_src = t_in["w_in"][l].rearrange("(k p) n -> p k n", p=P)
            loads = [(w[:, :, n * 512:(n + 1) * 512], w_src[:, :, n * 512:(n + 1) * 512], 0) for n in range(4)]
            wo = mem(RING0 + 16 * K1, KD, D)
            groups = []
            for n in range(3):
                for t in range(T):
                    groups.append(dict(need=n + 1,
                                       mm=[(0, ht[:, k, t * P:(t + 1) * P], w[:, k, n * 512:(n + 1) * 512]) for k in range(KD)],
                                       out=out("copy", (0, P, 0, 512, qkv[:, t, n * 512:(n + 1) * 512]))))
            for c in range(4):
                for c0, c1_ in ((0, SEQ), (SEQ, SEQ + CTX))[:1 if last else 2]:
                    groups.append(dict(need=4,
                                       mm=[(0, w[:, k, 3 * 512 + c * P:3 * 512 + (c + 1) * P], ht[:, k, c0:c1_]) for k in range(KD)],
                                       out=out("copy", (0, P, 0, c1_ - c0, glu[:, c, c0:c1_]))))
            products(groups, loads)
            qr = mem(HT0, T, 512)
            kr = mem(HT0 + T * 512, T, P)
            jobs = []
            for t in range(TX):
                for g in range(A_KV):
                    srcq = qkv[:, t, g * 256:(g + 1) * 256].rearrange("p (j d) -> p j d", d=HD)
                    dstq = qr[:, t, :].rearrange("p (j g d) -> p g j d", g=A_KV, d=HD)[:, g]
                    jobs.append((srcq, dstq, t, A_GROUP))
                jobs.append((qkv[:, t, 512:640].rearrange("p (j d) -> p j d", d=HD),
                             kr[:, t, :].rearrange("p (j d) -> p j d", d=HD), t, A_KV))
            rotate(jobs, at1, 16)
            if not last:
                moved = signal("queries_moved")
                with nc.Block() as block:
                    @block.vector
                    def _(dve):
                        for t in range(TX, T):
                            for g in range(A_KV):
                                nc.vector.tensor_copy(
                                    qr[:, t, :].rearrange("p (j g d) -> p g j d", g=A_KV, d=HD)[:, g],
                                    qkv[:, t, g * 256:(g + 1) * 256].rearrange("p (j d) -> p j d", d=HD)).then_inc(moved.sem, 1)
                moved.advance(2 * TC)
            QT0 = RING0
            qta, kta = mem(QT0, A_GROUP, 768), mem(QT0 + 4 * 768, 768)
            qtb, ktb = mem(QT0 + 5 * 768, 2, 768), mem(QT0 + 7 * 768, 2, 768)
            groups = []
            for c0, c1_ in ((0, TX), (TX, T)):
                n = (c1_ - c0) * P
                cols = slice(c0 * P, c1_ * P)
                latent = c0 == 0
                if latent or not last:
                    for j in range(A_GROUP):
                        mm = [((t - c0) * P, qr[:, t, j * P:(j + 1) * P], None) for t in range(c0, c1_)]
                        groups.append(dict(mm=mm, out=out("copy", (0, P, 0, n, qta[:, j, cols]))))
                    for j in range(2):
                        groups.append(dict(mm=[((t - c0) * P, qkv[:, t, 768 + j * P:768 + (j + 1) * P], None) for t in range(c0, c1_)],
                                           out=out("copy", (0, P, 0, n, qtb[:, j, cols]))))
                groups.append(dict(mm=[((t - c0) * P, kr[:, t, :] if latent else qkv[:, t, 512:640], None) for t in range(c0, c1_)],
                                   out=out("copy", (0, P, 0, n, kta[:, cols]))))
                for j in range(2):
                    groups.append(dict(mm=[((t - c0) * P, qkv[:, t, 1024 + j * P:1024 + (j + 1) * P], None) for t in range(c0, c1_)],
                                       out=out("copy", (0, P, 0, n, ktb[:, j, cols]))))
            products(groups)
            sink, nsink = small[:, 32:40], small[:, 40:48]
            load([(sink, t_in["a_sink"][l].partition_broadcast(P)),
                  (wo, t_in["w_out"][l].rearrange("(k p) n -> p k n", p=P))], "sinks_in")
            negated = signal("sinks_negated")
            with nc.Block() as block:
                @block.vector
                def _(dve):
                    nc.vector.tensor_scalar(nsink, sink, -1.0, None, ALU.mult).then_inc(negated.sem, 1)
            negated.advance(1)
            mix = mem(HT0, T, D)
            units = []
            for h in range(A_HEADS):
                g, j = h // A_GROUP, h % A_GROUP
                rows = slice(64 * g, 64 * g + 64)
                sk = dict(sink=sink[:, h:h + 1], nsink=nsink[:, h:h + 1])
                for t in range(nt):
                    u = dict(q=qta[rows, j, t * P:(t + 1) * P], out=mix[:, t, h * HD:(h + 1) * HD], **sk)
                    vcol = slice(640 + g * HD, 640 + (g + 1) * HD)
                    u["keys"] = [(0, kta[rows, SEQ:SEQ + CTX])]
                    u["evac"] = [(0, 0, CTX, None)]
                    u["v"] = [qkv[:, s, vcol] for s in range(TX, T)]
                    u["n"] = CTX
                    if t < TX:
                        s0, s1 = max(0, t - 1), min(TX - 1, t + 1)
                        u["keys"].append((512, kta[rows, s0 * P:(s1 + 1) * P]))
                        for s in range(s0, s1 + 1):
                            bias = cst(at1, "upper") if s < t else cst(at1, "lower") if s > t else None
                            u["evac"].append((512 + (s - s0) * P, u["n"], P, bias))
                            u["v"].append(qkv[:, s, vcol])
                            u["n"] += P
                    units.append(u)
            biases = {}
            for h in range(B_HEADS):
                j, p0 = h // 2, 64 * (h % 2)
                rows = slice(p0, p0 + 64)
                for t in range(nt):
                    vcol = slice(1280 + h * HD, 1280 + (h + 1) * HD)
                    u = dict(q=qtb[rows, j, t * P:(t + 1) * P], out=mix[:, t, 512 + h * HD:512 + (h + 1) * HD])
                    if t < TX:
                        u["keys"] = [(0, ktb[rows, j, 0:SEQ]), (512, ktb[rows, j, SEQ:SEQ + CTX])]
                        u["evac"] = [(0, 0, SEQ, True), (512, SEQ, CTX, None)]
                        u["v"] = [qkv[:, s, vcol] for s in range(T)]
                        u["n"] = SEQ + CTX
                        biases[len(units)] = [
                            bass.AP(bias_rows.tensor, bias_rows[l].offset + h * RB_R * RB_C + (7 - r) * RB_C + RB_C // 2,
                                    [[B_HEADS * RB_R * RB_C - 1, 64], [RB_C, ROWS], [1, GRID]])
                            for r in (2 * t, 2 * t + 1)]
                    else:
                        u["keys"] = [(0, ktb[rows, j, SEQ:SEQ + CTX])]
                        u["evac"] = [(0, 0, CTX, None)]
                        u["v"] = [qkv[:, s, vcol] for s in range(TX, T)]
                        u["n"] = CTX
                    units.append(u)
            attend(units, RING0 + 9 * 768, at1, biases)
            PAD = 4 * HALF + SEQ + CTX
            padded = mem(RING0, 2, PAD)
            y = mem(RING0 + 2 * PAD, 2, PAD)
            wcol, bcol = mem(RING0 + 4 * PAD, 2, TAPS), mem(RING0 + 4 * PAD + 64, 2)
            convolve(l, glu, padded, y, wcol, bcol, nt)
            cg, cb = mem(RING0 + 4 * PAD + 128, C_CH), mem(RING0 + 4 * PAD + 128 + C_CH, C_CH)
            load([(cg, t_in["conv_ln_g"][l].partition_broadcast(P)), (cb, t_in["conv_ln_b"][l].partition_broadcast(P))], "conv_ln_in")
            groups = []
            for t in range(nt):
                a = t * P if t < TX else SEQ + 2 * HALF + (t - TX) * P
                groups.append(dict(mm=[(c * P, y[:, c, a:a + P], None) for c in range(2)],
                                   out=out("copy", (0, P, 0, C_CH, mix[:, t, 768:1024]))))
            products(groups)
            rows = [(mix[:, t, 768:1024], mix[:, t, 768:1024]) for t in range(nt)]
            normalise(rows, LN_EPS, post=[(cg, cb)] * nt, width=C_CH)
            silu_rows(rows)
            if finish_debug(f"mix{l}", mix[:, 0:nt, :]):
                return
            mixt = mem(RING0, KD, 768)
            groups = []
            for k in range(KD):
                for c0, c1_ in ((0, TX), (TX, T))[:1 if last else 2]:
                    groups.append(dict(mm=[((t - c0) * P, mix[:, t, k * P:(k + 1) * P], None) for t in range(c0, c1_)],
                                       out=out("copy", (0, P, 0, (c1_ - c0) * P, mixt[:, k, c0 * P:c1_ * P]))))
            products(groups)
            groups = []
            for t in range(nt):
                for n in range(2):
                    groups.append(dict(mm=[(0, mixt[:, k, t * P:(t + 1) * P], wo[:, k, n * 512:(n + 1) * 512]) for k in range(KD)],
                                       out=out("copy", (0, P, 0, 512, mix[:, t, n * 512:(n + 1) * 512]))))
            gtile = [mem(RING0 + 7 * K1 + K1 * i, D) for i in range(2)]
            gain, shift_ = mem(RING0 + 9 * K1, D), mem(RING0 + 10 * K1, D)
            wr = small[:, 576:704].rearrange("p (k e) -> p k e", e=E)
            products(groups)
            load([(gtile[s], mod_rows[s, 0].partition_broadcast(P)) for s in range(2)]
                 + [(gain, t_in["ln1_g"][l].partition_broadcast(P)), (shift_, t_in["ln1_b"][l].partition_broadcast(P)),
                    (wr, t_in["w_router"][l].rearrange("(k p) e -> p k e", p=P))], "gates_in")
            gate_rows([(res[:, t, :], mix[:, t, :], gtile[0 if t < TX else 1]) for t in range(nt)], ALPHA)
            normalise([(res[:, t, :], res[:, t, :]) for t in range(nt)], LN_EPS, post=[(gain, shift_)] * nt)
            if finish_debug(f"res1_{l}", res[:, 0:nt, :]):
                return
            normalise([(res[:, t, :], lnx[:, t, :]) for t in range(nt)], LN_EPS)
            turn_rows(lnx, lambda s, k: m3[:, 32 + k, s:s + 1], lambda s, k: m3[:, 24 + k, s:s + 1], nt)
            X0 = EXTRA0
            aff, pos = mem(X0, T, E), mem(X0 + T * E, T, E)
            msk, logit = mem(X0 + 2 * T * E, T, E), mem(X0 + 3 * T * E, T, E)
            af = small[:, 16:24]
            at_ = mem(X0 + 4 * T * E, 768, parts=E)
            work = mem(X0 + 4 * T * E + 768, nt * P, parts=E)
            best = small[0:E, 0:8]
            route(l, nt, wr, logit, aff, pos, msk, af, at_, work, best)
            if finish_debug(f"pos{l}", pos[:, 0:nt, :]):
                return
            acc = mem(HT0, T, D)
            experts(l, nt, aff, pos, acc, X0 + 2 * T * E)
            if finish_debug(f"moe{l}", acc[:, 0:nt, :]):
                return
            load([(gtile[s], mod_rows[s, 1].partition_broadcast(P)) for s in range(2)]
                 + [(gain, t_in["ln2_g"][l].partition_broadcast(P)), (shift_, t_in["ln2_b"][l].partition_broadcast(P))], "gates_in")
            gate_rows([(res[:, t, :], acc[:, t, :], gtile[0 if t < TX else 1]) for t in range(nt)], ALPHA)
            normalise([(res[:, t, :], res[:, t, :]) for t in range(nt)], LN_EPS, post=[(gain, shift_)] * nt)
            if finish_debug(f"res2_{l}", res[:, 0:nt, :]):
                return
        sparse_attention_block()


_INPUTS = ["x", "c", "ctx", "c_ctx", "w_mod", "b_mod", "w_in", "a_sink", "nat_bias", "conv_w", "conv_b", "conv_ln_g",
           "conv_ln_b", "w_out", "ln1_g", "ln1_b", "w_router", "w_gate", "w_up", "w_down", "ln2_g", "ln2_b", "ln1_w_2",
           "w_in_2", "q_norm_w_2", "k_norm_w_2", "cmp_pe_k_2", "cmp_pe_v_2", "cmp_wk1_2", "cmp_wk2_2", "cmp_wv1_2",
           "cmp_wv2_2", "ret_norm_w_2", "w_out_2", "ln2_w_2", "w_up_2", "w_down_2"]


def extra_layout(inputs):
    def cols(a):
        a = np.asarray(a)
        a = a.reshape(a.shape[:-1] + (a.shape[-1] // P, P))
        return np.ascontiguousarray(np.swapaxes(a, -1, -2))

    cond = np.stack([cols(inputs["c"][0]), cols(inputs["c_ctx"])], -1).reshape(P, 2 * KD)
    taps = np.asarray(inputs["conv_w"]).transpose(0, 2, 1).reshape(LAYERS, 2, P, TAPS).transpose(0, 2, 1, 3)
    return {"cond_cols": cond, "b_mod_cols": cols(inputs["b_mod"]),
            "ln1_w_cols": cols(inputs["ln1_w_2"]), "ln2_w_cols": cols(inputs["ln2_w_2"]),
            "cmp_pe_k_cols": cols(np.asarray(inputs["cmp_pe_k_2"]).reshape(1, -1)),
            "cmp_pe_v_cols": cols(np.asarray(inputs["cmp_pe_v_2"]).reshape(1, -1)),
            "conv_w_cols": np.ascontiguousarray(taps), "conv_b_cols": cols(inputs["conv_b"])}


def kernel(**inputs):
    import concourse.bacc as bacc
    from concourse.bass_utils import run_bass_kernel_spmd

    nc = bacc.Bacc("TRN2", target_bir_lowering=False, num_devices=1)
    (c1, _), (c2, _) = shape_constants()
    arrays = {name: np.ascontiguousarray(inputs[name]) for name in _INPUTS}
    arrays |= {"consts1": c1, "consts2": c2} | extra_layout(inputs)
    t_in = {name: nc.dram_tensor(f"in_{name}", a.shape, mybir.dt.from_np(a.dtype), kind="ExternalInput").ap()
            for name, a in arrays.items()}
    out = nc.dram_tensor("out", [1, SEQ, D], F32, kind="ExternalOutput").ap()
    build(nc, t_in, out)
    r = run_bass_kernel_spmd(nc, [{f"in_{name}": a for name, a in arrays.items()}], core_ids=[0])
    return r.results[0]["out"]
```

```python
from contextlib import ExitStack

import numpy as np

import concourse.bass as bass
from concourse import mybir
from concourse.alu_op_type import AluOpType as ALU

F32 = mybir.dt.float32
ACT = mybir.ActivationFunctionType
AX = mybir.AxisListType

P = 128
D = 1024
KD = D // P
SEQ, CTX = 512, 256
TX, TC = SEQ // P, CTX // P
T = TX + TC
LAYERS = 2
HD = 64
SCALE = HD ** -0.5
NEG = -1e30
A_HEADS, A_KV = 8, 2
A_GROUP = A_HEADS // A_KV
B_HEADS = 4
GRID = 64
ROWS = SEQ // GRID
RB_R, RB_C = 15, 31
C_CH, TAPS = 256, 31
HALF = TAPS // 2
IN_W = 2048
QKV_W = IN_W - 2 * C_CH
E = 16
CAP_X, CAP_C = 2 * SEQ // E, 2 * CTX // E
ALPHA = (2 * LAYERS) ** 0.25
LN_EPS = 1e-6
IN2_W = 2840
FF2 = 4096
N_CMP = (SEQ - 32) // 16 + 1
CMP_HID = 256
K1 = 1024


def shape_constants():
    q = np.arange(P)[:, None]
    k = np.arange(P)[None, :]
    eye = np.eye(P)
    lower = np.where(k <= q, 0.0, NEG)
    upper = np.where(k >= q, 0.0, NEG)
    above = np.where(k > q, 0.0, NEG)
    pos = np.arange(SEQ, dtype=np.float32)

    def tile(a):
        return a.reshape(TX, P, HD).transpose(1, 0, 2).reshape(P, TX * HD)

    inv = (10000.0 ** (-np.arange(16, dtype=np.float32) / np.float32(16))).astype(np.float32)
    ar = (pos // GRID)[:, None].astype(np.float32) * inv
    ac = (pos % GRID)[:, None].astype(np.float32) * inv
    cos1 = np.concatenate([np.cos(ar), np.cos(ar), np.cos(ac), np.cos(ac)], 1)
    sin1 = np.concatenate([-np.sin(ar), np.sin(ar), -np.sin(ac), np.sin(ac)], 1)
    inv = (10000.0 ** (-np.arange(32, dtype=np.float32) / np.float32(32))).astype(np.float32)
    an = pos[:, None] * inv
    cos2 = np.concatenate([np.cos(an), np.cos(an)], 1)
    sin2 = np.concatenate([-np.sin(an), np.sin(an)], 1)

    c = np.arange(P) % GRID
    start = np.clip(c - 8, 0, GRID - 16)[:, None]
    kc = np.arange(GRID)[None, :]
    near = np.where((kc >= start) & (kc < start + 16), 0.0, NEG)
    slots = np.broadcast_to(np.arange(64)[None, :], (P, 64))
    tri = np.where(q <= k, 1.0, 0.0)
    first = dict(ident=eye, lower=lower, upper=upper, near=near, slots=slots, tri=tri,
                 ones=np.ones((P, P)), cos=tile(cos1), sin=tile(sin1))

    cend = np.arange(32) * 16 + 31
    seen = np.zeros((P, TX, 32))
    some = np.zeros((P, TX))
    for t in range(TX):
        at = t * P + np.arange(P)
        seen[:, t] = np.where(cend[None, :] <= at[:, None], 0.0, NEG)
        some[:, t] = at >= 31
    lg = np.log(1.0 - 2.0 ** (-5.0 - np.arange(4)))
    decay = np.zeros((P, 4, P))
    for h in range(4):
        decay[:, h] = np.where(q <= k, np.exp(lg[h] * np.maximum(k - q, 0)), 0.0)
    i = np.arange(P)[:, None]
    xi = np.exp(lg[None, :] * (i + 1))
    zeta = np.exp(lg[None, :] * (P - 1 - i)) * SCALE
    gc = np.broadcast_to(np.exp(lg * P)[None, :], (P, 4))
    second = dict(ident=eye, lower=lower, above=above, seen=seen.reshape(P, -1), some=some,
                  decay=decay.reshape(P, -1), xi=xi, zeta=zeta, gc=gc,
                  cos=tile(cos2), sin=tile(sin2))

    def pack(parts):
        at, where = 0, {}
        for name, a in parts.items():
            where[name] = (at, at + a.shape[1])
            at += a.shape[1]
        return np.concatenate([np.asarray(a, np.float32) for a in parts.values()], 1), where

    return pack(first), pack(second)


def build(nc, t_in, out_ap, debug=None):
    (c1, at1), (c2, at2) = shape_constants()
    NC = max(c1.shape[1], c2.shape[1])
    ctx = ExitStack()

    def sb(name, n):
        return ctx.enter_context(nc.sbuf_tensor(name, [P, n], F32))

    arena = sb("arena", 49 * K1 + 512)
    at = [0]

    def region(n):
        a = at[0]
        at[0] += n
        return a

    RES0, HT0, LNX0 = region(6 * K1), region(6 * K1), region(6 * K1)
    EXTRA0 = region(7 * K1 + 512)
    RING0 = region(24 * K1)

    def mem(start, *dims, parts=P, p0=0):
        n = int(np.prod(dims))
        v = arena[p0:p0 + parts, start:start + n]
        if len(dims) == 2:
            v = v.rearrange("p (a b) -> p a b", b=dims[1])
        if len(dims) == 3:
            v = v.rearrange("p (a b c) -> p a b c", b=dims[1], c=dims[2])
        return v

    consts = sb("consts", NC)
    small = sb("small", 704)
    mod = sb("mod", 96)
    res = mem(RES0, T, D)
    ht = mem(HT0, KD, SEQ + CTX)
    lnx = mem(LNX0, T, D)

    pair = [ctx.enter_context(nc.psum_tensor(f"pair{i}", [P, 1024], F32)) for i in range(4)]
    bank = [pair[i // 2][:, (i % 2) * 512:(i % 2) * 512 + 512] for i in range(8)]

    mod_rows = nc.dram_tensor("mod_rows", [2, 2, D], F32, kind="Internal").ap()
    bias_rows = nc.dram_tensor("bias_rows", [LAYERS, 64 * B_HEADS * RB_R * RB_C], F32, kind="Internal").ap()

    class Signal:
        def __init__(self, name):
            self.sem = ctx.enter_context(nc.semaphore(name))
            self.base = 0

        def upto(self, i, each=1):
            return self.base + (i + 1) * each

        def advance(self, total):
            self.base += total

    known = {}

    def signal(name):
        if name not in known:
            known[name] = Signal(name)
        return known[name]

    class Chain:

        def __init__(self, eng, name):
            self.eng, self.s = eng, signal(name)

        def link(self, ins):
            self.s.advance(1)
            ins.then_inc(self.s.sem, 1)
            self.eng.wait_ge(self.s.sem, self.s.base)

    def cst(where, name):
        a, b = where[name]
        return consts[:, a:b]

    def load(pairs, name):
        s = signal(name)
        with nc.Block() as block:
            @block.sync
            def _(sp):
                for dst, src in pairs:
                    sp.dma_start(dst, src).then_inc(s.sem, 16)
                sp.wait_ge(s.sem, s.upto(len(pairs) - 1, 16))
        s.advance(16 * len(pairs))

    def products(groups, loads=(), frees=True):
        full, taken, landed = signal("bank_full"), signal("bank_taken"), [signal(f"landed{i}") for i in range(8)]
        takers = [g % 2 for g in range(len(groups))]
        base_landed = [s.base for s in landed]

        def value(n):
            return base_landed[n % 8] + 16 * (n // 8 + 1)

        counts = {0: [], 1: []}
        for g in range(len(groups)):
            counts[g % 2].append(g)
        taken = [signal("bank_taken_act"), signal("bank_taken_dve")]

        with nc.Block() as block:
            @block.sync
            def _(sp):
                for n, (dst, src, after) in enumerate(loads):
                    if after > 0:
                        sp.wait_ge(full.sem, full.upto(after - 1))
                    sp.dma_start(dst, src).then_inc(landed[n % 8].sem, 16)

            @block.tensor
            def _(pe):
                seen = 0
                for g, group in enumerate(groups):
                    for n in range(seen, group.get("need", 0)):
                        pe.wait_ge(landed[n % 8].sem, value(n))
                    seen = max(seen, group.get("need", 0))
                    if g >= 8:
                        pe.wait_ge(taken[g % 2].sem, taken[g % 2].upto((g - 8) // 2))
                    ps = bank[g % 8]
                    mm = group["mm"]
                    for i, (col, lhs, rhs) in enumerate(mm):
                        p0 = group.get("p0", 0)
                        if rhs is None:
                            k, m = lhs.shape[0], lhs.shape[-1]
                            ins = nc.tensor.transpose(ps[0:m, col:col + k], lhs, cst(at1, "ident")[0:k, 0:k])
                        else:
                            m = lhs.shape[-1]
                            n = int(np.prod(rhs.shape[1:]))
                            o = ps[p0:p0 + m, col:col + n]
                            if len(rhs.shape) == 3:
                                o = o.rearrange("p (a b) -> p a b", b=rhs.shape[2])
                            ins = nc.tensor.matmul(
                                o, lhsT=lhs, rhs=rhs,
                                start=i == 0 or mm[i - 1][0] != col,
                                stop=i == len(mm) - 1 or mm[i + 1][0] != col)
                    ins.then_inc(full.sem, 1)

            @block.scalar
            def _(act):
                chain = Chain(act, "act_chain")
                for i, g in enumerate(counts[0]):
                    act.wait_ge(full.sem, full.upto(g))
                    o = groups[g]["out"]
                    for j, (psv, dst, *more) in enumerate(o["parts"](bank[g % 8])):
                        if o["kind"] == "copy":
                            ins = nc.scalar.activation(dst, psv, ACT.Copy)
                        elif o["kind"] == "affine":
                            ins = nc.scalar.activation(dst, psv, ACT.Identity, bias=more[1], scale=more[0])
                        elif o["kind"] == "scale":
                            ins = nc.scalar.activation(dst, psv, ACT.Copy, scale=more[0])
                        elif o["kind"] == "relu2":
                            chain.link(nc.scalar.activation(dst, psv, ACT.Relu))
                            ins = nc.scalar.activation(dst, dst, ACT.Square)
                    ins.then_inc(taken[0].sem, 1)

            @block.vector
            def _(dve):
                chain = Chain(dve, "dve_chain")
                for i, g in enumerate(counts[1]):
                    dve.wait_ge(full.sem, full.upto(g))
                    o = groups[g]["out"]
                    for j, (psv, dst, *more) in enumerate(o["parts"](bank[g % 8])):
                        if o["kind"] == "copy":
                            ins = nc.vector.tensor_copy(dst, psv)
                        elif o["kind"] == "affine":
                            ins = nc.vector.tensor_scalar(dst, psv, more[0], more[1], ALU.mult, ALU.add)
                        elif o["kind"] == "scale":
                            ins = nc.vector.tensor_scalar(dst, psv, more[0], None, ALU.mult)
                        elif o["kind"] == "relu2":
                            chain.link(nc.vector.tensor_scalar(dst, psv, 0.0, None, ALU.max))
                            ins = nc.vector.tensor_tensor(dst, dst, dst, ALU.mult)
                    ins.then_inc(taken[1].sem, 1)
        full.advance(len(groups))
        taken[0].advance(len(counts[0]))
        taken[1].advance(len(counts[1]))
        for n in range(len(loads)):
            landed[n % 8].advance(16)

    def out(kind, *parts):
        def views(ps):
            for (r0, r1, c0, c1, dst, *more) in parts:
                v = ps[r0:r1, c0:c1]
                if len(dst.shape) == 3:
                    v = v.rearrange("p (a b) -> p a b", b=dst.shape[2])
                yield (v, dst, *more)
        return dict(kind=kind, parts=views)

    def normalise(rows, eps, post=(), mean=True, width=D):
        n = len(rows)
        halves = (width + 511) // 512
        hw = width // halves
        stats = small[:, 0:n * halves * 6].rearrange("p (n k) -> p n k", k=6 * halves)
        mv = small[:, 288:288 + 2 * n].rearrange("p (n k) -> p n k", k=2)
        ve, sd, rs = (small[:, 352 + 32 * i:352 + 32 * i + n] for i in range(3))
        v_ready, v_root, gained = signal("var_ready"), signal("root_ready"), signal("row_normal")
        finished = signal("row_finished")
        with nc.Block() as block:
            @block.vector
            def _(dve):
                chain = Chain(dve, "dve_chain")
                for i, (src, _) in enumerate(rows):
                    for h in range(halves):
                        ins = nc.vector.bn_stats(stats[:, i, 6 * h:6 * h + 6], src[:, h * hw:(h + 1) * hw])
                chain.link(ins)
                for i in range(n):
                    ins = nc.vector.bn_aggr(mv[:, i, :], stats[:, i, :])
                chain.link(ins)
                if mean:
                    nc.vector.tensor_scalar(ve, mv[:, :, 1], eps, None, ALU.add).then_inc(v_ready.sem, 1)
                else:
                    chain.link(nc.vector.tensor_tensor(ve, mv[:, :, 0], mv[:, :, 0], ALU.mult))
                    nc.vector.scalar_tensor_tensor(ve, ve, eps, mv[:, :, 1], ALU.add, ALU.add).then_inc(v_ready.sem, 1)
                dve.wait_ge(v_root.sem, v_root.upto(0))
                chain.link(nc.vector.reciprocal(rs, sd))
                for i, (src, dst) in enumerate(rows):
                    if mean:
                        ins = nc.vector.tensor_scalar(dst, src, mv[:, i, 0:1], rs[:, i:i + 1], ALU.subtract, ALU.mult)
                    else:
                        ins = nc.vector.tensor_scalar(dst, src, rs[:, i:i + 1], None, ALU.mult)
                    if post:
                        chain.link(ins)
                        ins = nc.vector.tensor_tensor(dst, dst, post[i][0], ALU.mult)
                    ins.then_inc(gained.sem, 1)

            @block.scalar
            def _(act):
                act.wait_ge(v_ready.sem, v_ready.upto(0))
                nc.scalar.activation(sd, ve, ACT.Sqrt).then_inc(v_root.sem, 1)

            @block.gpsimd
            def _(pool):
                if post:
                    for i, (_, dst) in enumerate(rows):
                        pool.wait_ge(gained.sem, gained.upto(i))
                        nc.gpsimd.tensor_tensor(dst, dst, post[i][1], ALU.add).then_inc(finished.sem, 1)
        v_ready.advance(1)
        v_root.advance(1)
        gained.advance(n)
        if post:
            finished.advance(n)

    def turn_rows(src, scale, shift, chunks):
        groups = []
        for k in range(KD):
            for stream, (t0, t1) in enumerate(((0, TX), (TX, T))):
                if t0 >= chunks:
                    continue
                mm = [((t - t0) * P, src[:, t, k * P:(k + 1) * P], None) for t in range(t0, t1)]
                n = (t1 - t0) * P
                dst = ht[:, k, t0 * P:t1 * P]
                if shift is None:
                    o = out("scale", (0, P, 0, n, dst, scale(stream, k)))
                else:
                    o = out("affine", (0, P, 0, n, dst, scale(stream, k), shift(stream, k)))
                groups.append(dict(mm=mm, out=o))
        products(groups)

    def rotate(jobs, where, seg):
        done, half_done = signal("rotated"), signal("swapped")
        tmp = mem(RING0 + 23 * K1, 2, 512)
        with nc.Block() as block:
            @block.gpsimd
            def _(pool):
                for i, (src, dst, t, heads) in enumerate(jobs):
                    if i >= 2:
                        pool.wait_ge(done.sem, done.upto(i - 2))
                    cosv = cst(where, "cos")[:, t * HD:(t + 1) * HD].unsqueeze(1).to_broadcast([P, heads, HD])
                    tv = tmp[:, i % 2, 0:heads * HD].rearrange("p (h d) -> p h d", d=HD)
                    nc.gpsimd.tensor_tensor(tv, src, cosv, ALU.mult).then_inc(half_done.sem, 1)

            @block.vector
            def _(dve):
                chain = Chain(dve, "dve_chain")
                for i, (src, dst, t, heads) in enumerate(jobs):
                    for a in range(0, HD, 2 * seg):
                        for s in range(2):
                            o, x = a + s * seg, a + (1 - s) * seg
                            sinv = cst(where, "sin")[:, t * HD + o:t * HD + o + seg].unsqueeze(1).to_broadcast([P, heads, seg])
                            ins = nc.vector.tensor_tensor(dst[:, :, o:o + seg], src[:, :, x:x + seg], sinv, ALU.mult)
                    chain.link(ins)
                    dve.wait_ge(half_done.sem, half_done.upto(i))
                    tv = tmp[:, i % 2, 0:heads * HD].rearrange("p (h d) -> p h d", d=HD)
                    nc.vector.tensor_tensor(dst, dst, tv, ALU.add).then_inc(done.sem, 1)
        done.advance(len(jobs))
        half_done.advance(len(jobs))

    def attend(units, work, where, biases=()):
        n = len(units)
        sc = mem(work, 2, 768)
        pt = mem(work + 1536, 2, 768)
        bt = mem(work + 3072, 2, 512)
        mx = small[:, 0:4]
        nm = small[:, 4:8]
        rs = small[:, 8:12]
        es = small[:, 12:16]
        den = small[:, 16:20]
        rc = small[:, 20:24]
        scored, maxed, probs = signal("scored"), signal("maxed"), signal("probs")
        turned, turned_sb, valued, written = (signal(x) for x in ("turned", "turned_sb", "valued", "written"))
        tile_in, tile_ready = [signal("bias_in0"), signal("bias_in1")], signal("bias_ready")
        kb = {u: i for i, u in enumerate(sorted(biases))} if biases else {}
        order = sorted(kb)
        ident = cst(where, "ident")
        wide = pair[2]
        po = [pair[3][:, 0:512], pair[3][:, 512:1024]]

        with nc.Block() as block:
            @block.sync
            def _(sp):
                for i, u in enumerate(order):
                    if i >= 2:
                        sp.wait_ge(maxed.sem, maxed.upto(order[i - 2]))
                    for r in range(2):
                        sp.dma_start(bt[64 * r:64 * r + 64, i % 2, :].rearrange("p (a b) -> p a b", b=GRID),
                                     biases[u][r]).then_inc(tile_in[i % 2].sem, 16)

            @block.gpsimd
            def _(pool):
                chain = Chain(pool, "pool_chain")
                for i, u in enumerate(order):
                    pool.wait_ge(tile_in[i % 2].sem, tile_in[i % 2].upto(i // 2, 32))
                    chain.link(nc.gpsimd.tensor_scalar(bt[:, i % 2, :], bt[:, i % 2, :], 1.0 / SCALE, None, ALU.mult))
                    tv = bt[:, i % 2, :].rearrange("p (a b) -> p a b", b=GRID)
                    near = cst(where, "near").unsqueeze(1).to_broadcast([P, ROWS, GRID])
                    nc.gpsimd.tensor_tensor(tv, tv, near, ALU.add).then_inc(tile_ready.sem, 1)

            @block.tensor
            def _(pe):
                for i in range(n + 2):
                    if i < n:
                        if i >= 2:
                            pe.wait_ge(maxed.sem, maxed.upto(i - 2))
                        for col, kT in units[i]["keys"]:
                            m = kT.shape[-1]
                            ins = nc.tensor.matmul(pair[i % 2][:, col:col + m], lhsT=units[i]["q"], rhs=kT,
                                                   start=True, stop=True)
                        ins.then_inc(scored.sem, 1)
                    j = i - 1
                    if 0 <= j < n:
                        pe.wait_ge(probs.sem, probs.upto(j))
                        if j >= 1:
                            pe.wait_ge(turned_sb.sem, turned_sb.upto(j - 1))
                        nk = units[j]["n"]
                        for c in range(0, nk, P):
                            w = min(P, nk - c)
                            ins = nc.tensor.transpose(wide[0:w, c:c + P], sc[:, j % 2, c:c + w], ident)
                        ins.then_inc(turned.sem, 1)
                    j = i - 2
                    if 0 <= j < n:
                        pe.wait_ge(turned_sb.sem, turned_sb.upto(j))
                        if j >= 2:
                            pe.wait_ge(written.sem, written.upto(j - 2))
                        v = units[j]["v"]
                        for c, vc in enumerate(v):
                            w = vc.shape[0]
                            ins = nc.tensor.matmul(po[j % 2][:, 0:HD], lhsT=pt[0:w, j % 2, c * P:(c + 1) * P], rhs=vc,
                                                   start=c == 0, stop=c == len(v) - 1)
                        ins.then_inc(valued.sem, 1)

            @block.vector
            def _(dve):
                chain = Chain(dve, "dve_chain")
                for i in range(n + 2):
                    if i < n:
                        u = units[i]
                        dve.wait_ge(scored.sem, scored.upto(i))
                        if i >= 2:
                            dve.wait_ge(turned.sem, turned.upto(i - 2))
                        if i in kb:
                            dve.wait_ge(tile_ready.sem, tile_ready.upto(kb[i]))
                        for pc, c, m, bias in u["evac"]:
                            if bias is None:
                                ins = nc.vector.tensor_copy(sc[:, i % 2, c:c + m], pair[i % 2][:, pc:pc + m])
                            else:
                                if i in kb:
                                    bias = bt[:, kb[i] % 2, :]
                                ins = nc.vector.tensor_tensor(sc[:, i % 2, c:c + m], pair[i % 2][:, pc:pc + m], bias, ALU.add)
                        chain.link(ins)
                        k = i % 4
                        chain.link(nc.vector.tensor_reduce(mx[:, k:k + 1], sc[:, i % 2, 0:u["n"]], AX.X, ALU.max))
                        if u.get("sink") is None:
                            nc.vector.tensor_scalar(nm[:, k:k + 1], mx[:, k:k + 1], -SCALE, None, ALU.mult).then_inc(maxed.sem, 1)
                        else:
                            chain.link(nc.vector.tensor_scalar(nm[:, k:k + 1], mx[:, k:k + 1], -SCALE, None, ALU.mult))
                            nc.vector.tensor_scalar(nm[:, k:k + 1], nm[:, k:k + 1], u["nsink"], None, ALU.min).then_inc(maxed.sem, 1)
                    j = i - 2
                    if 0 <= j < n:
                        u = units[j]
                        k = j % 4
                        dve.wait_ge(valued.sem, valued.upto(j))
                        total = rs[:, k:k + 1]
                        if u.get("sink") is not None:
                            chain.link(nc.vector.tensor_tensor(den[:, k:k + 1], rs[:, k:k + 1], es[:, k:k + 1], ALU.add))
                            total = den[:, k:k + 1]
                        chain.link(nc.vector.reciprocal(rc[:, k:k + 1], total))
                        if u.get("gate") is not None:
                            chain.link(nc.vector.tensor_tensor(rc[:, k:k + 1], rc[:, k:k + 1], u["gate"], ALU.mult))
                        if u.get("add"):
                            ins = nc.vector.scalar_tensor_tensor(u["out"], po[j % 2][:, 0:HD], rc[:, k:k + 1], u["out"],
                                                                 ALU.mult, ALU.add)
                        else:
                            ins = nc.vector.tensor_scalar(u["out"], po[j % 2][:, 0:HD], rc[:, k:k + 1], None, ALU.mult)
                        ins.then_inc(written.sem, 1)

            @block.scalar
            def _(act):
                for i in range(n + 1):
                    if i < n:
                        u = units[i]
                        k = i % 4
                        act.wait_ge(maxed.sem, maxed.upto(i))
                        if i >= 4:
                            act.wait_ge(written.sem, written.upto(i - 4))
                        if u.get("sink") is not None:
                            nc.scalar.activation(es[:, k:k + 1], u["sink"], ACT.Exp, bias=nm[:, k:k + 1])
                        nc.scalar.activation(sc[:, i % 2, 0:u["n"]], sc[:, i % 2, 0:u["n"]], ACT.Exp,
                                             bias=nm[:, k:k + 1], scale=SCALE, accum_out=rs[:, k:k + 1]).then_inc(probs.sem, 1)
                    j = i - 1
                    if 0 <= j < n:
                        act.wait_ge(turned.sem, turned.upto(j))
                        if j >= 2:
                            act.wait_ge(valued.sem, valued.upto(j - 2))
                        nk = units[j]["n"]
                        cols = (nk + P - 1) // P * P
                        rows = P if nk >= P else nk
                        for c in range(0, cols, 512):
                            m = min(512, cols - c)
                            ins = nc.scalar.activation(pt[0:rows, j % 2, c:c + m], wide[0:rows, c:c + m], ACT.Copy)
                        ins.then_inc(turned_sb.sem, 1)
        for s in (scored, maxed, probs, turned, turned_sb, valued, written):
            s.advance(n)
        tile_in[0].advance(32 * ((len(order) + 1) // 2))
        tile_in[1].advance(32 * (len(order) // 2))
        tile_ready.advance(len(order))

    def adaln(l):
        cond = small[:, 0:16].rearrange("p (k s) -> p k s", s=2)
        cs = small[:, 16:32].rearrange("p (k s) -> p k s", s=2)
        bm = small[:, 32:80]
        rows = small[0:8, 128:640].rearrange("p (s g d) -> p s g d", s=2, g=2)
        m3 = mod[:, :].rearrange("p (m s) -> p m s", s=2)
        panel = [mem(RING0 + 8 * K1 * i, KD, 1024) for i in range(3)]
        n_panels = 6
        cond_in, cond_silu = signal("cond_in"), signal("cond_silu")
        panel_in = [signal(f"panel_in{i}") for i in range(3)]
        panel_full, panel_taken = signal("panel_full"), signal("panel_taken")
        gates_turned, gates_sb, gates_out = signal("gates_turned"), signal("gates_sb"), signal("gates_out")
        wm = t_in["w_mod"][l].rearrange("(k p) n -> p k n", p=P)
        with nc.Block() as block:
            @block.sync
            def _(sp):
                sp.dma_start(small[:, 0:16], t_in["cond_cols"]).then_inc(cond_in.sem, 16)
                sp.dma_start(bm, t_in["b_mod_cols"][l]).then_inc(cond_in.sem, 16)
                for m in range(n_panels):
                    if m >= 3:
                        sp.wait_ge(panel_full.sem, panel_full.upto(m - 3))
                    sp.dma_start(panel[m % 3], wm[:, :, m * 1024:(m + 1) * 1024]).then_inc(panel_in[m % 3].sem, 16)
                sp.wait_ge(gates_sb.sem, gates_sb.upto(0))
                for s in range(2):
                    for g in range(2):
                        sp.dma_start(mod_rows[s, g].rearrange("(k d) -> k d", d=P), rows[:, s, g, :]).then_inc(gates_out.sem, 16)
                sp.wait_ge(gates_out.sem, gates_out.upto(3, 16))

            @block.scalar
            def _(act):
                act.wait_ge(cond_in.sem, cond_in.upto(1, 16))
                nc.scalar.activation(cs, cond, ACT.Silu).then_inc(cond_silu.sem, 1)

            @block.tensor
            def _(pe):
                pe.wait_ge(cond_silu.sem, cond_silu.upto(0))
                for m in range(n_panels):
                    pe.wait_ge(panel_in[m % 3].sem, panel_in[m % 3].upto(m // 3, 16))
                    if m >= 2:
                        pe.wait_ge(panel_taken.sem, panel_taken.upto(m - 2))
                    for j in range(8):
                        for k in range(KD):
                            ins = nc.tensor.matmul(bank[m % 2][:, 2 * j:2 * j + 2], lhsT=panel[m % 3][:, k, j * P:(j + 1) * P],
                                                   rhs=cs[:, k, :], start=k == 0, stop=k == KD - 1)
                    ins.then_inc(panel_full.sem, 1)
                pe.wait_ge(panel_taken.sem, panel_taken.upto(n_panels - 1))
                for s in range(2):
                    for g in range(2):
                        a = 16 + 24 * g
                        ins = nc.tensor.transpose(bank[2][0:8, (2 * s + g) * P:(2 * s + g + 1) * P],
                                                  m3[:, a:a + 8, s], cst(at1, "ident"))
                ins.then_inc(gates_turned.sem, 1)

            @block.vector
            def _(dve):
                for m in range(n_panels):
                    dve.wait_ge(panel_full.sem, panel_full.upto(m))
                    b = bm[:, 8 * m:8 * m + 8].unsqueeze(2).to_broadcast([P, 8, 2])
                    o = m3[:, 8 * m:8 * m + 8, :]
                    v = bank[m % 2][:, 0:16].rearrange("p (a b) -> p a b", b=2)
                    one = 1.0 if m in (1, 4) else 0.0
                    nc.vector.scalar_tensor_tensor(o, v, one, b, ALU.add, ALU.add).then_inc(panel_taken.sem, 1)
                dve.wait_ge(gates_turned.sem, gates_turned.upto(0))
                nc.vector.tensor_copy(small[0:8, 128:640], bank[2][0:8, :]).then_inc(gates_sb.sem, 1)
        cond_in.advance(32)
        cond_silu.advance(1)
        for s in panel_in:
            s.advance(32)
        panel_full.advance(6)
        panel_taken.advance(6)
        gates_turned.advance(1)
        gates_sb.advance(1)
        gates_out.advance(64)

    def convolve(l, glu, padded, y, wcol, bcol, chunks):
        width = 2 * HALF + SEQ + (2 * HALF + CTX if chunks > TX else 0)
        span = width - 2 * HALF
        w_in_, cleared, sig, ready = signal("taps_in"), signal("pads_cleared"), signal("gate_sigmoid"), signal("glu_ready")
        with nc.Block() as block:
            @block.sync
            def _(sp):
                sp.dma_start(wcol, t_in["conv_w_cols"][l]).then_inc(w_in_.sem, 16)
                sp.dma_start(bcol, t_in["conv_b_cols"][l]).then_inc(w_in_.sem, 16)

            @block.gpsimd
            def _(pool):
                nc.gpsimd.memset(padded[:, :, 0:width], 0.0).then_inc(cleared.sem, 1)

            @block.scalar
            def _(act):
                nc.scalar.activation(glu[:, 2:4, 0:chunks * P], glu[:, 2:4, 0:chunks * P], ACT.Sigmoid).then_inc(sig.sem, 1)

            @block.vector
            def _(dve):
                chain = Chain(dve, "dve_chain")
                dve.wait_ge(cleared.sem, cleared.upto(0))
                dve.wait_ge(sig.sem, sig.upto(0))
                ins = nc.vector.tensor_tensor(padded[:, :, HALF:HALF + SEQ], glu[:, 0:2, 0:SEQ], glu[:, 2:4, 0:SEQ], ALU.mult)
                if chunks > TX:
                    a = 3 * HALF + SEQ
                    ins = nc.vector.tensor_tensor(padded[:, :, a:a + CTX], glu[:, 0:2, SEQ:], glu[:, 2:4, SEQ:], ALU.mult)
                chain.link(ins)
                dve.wait_ge(w_in_.sem, w_in_.upto(1, 16))
                for j in range(TAPS):
                    for c in range(2):
                        x = padded[:, c, j:j + span]
                        o = y[:, c, 0:span]
                        if j == 0:
                            ins = nc.vector.tensor_scalar(o, x, wcol[:, c, 0:1], bcol[:, c:c + 1], ALU.mult, ALU.add)
                        else:
                            ins = nc.vector.scalar_tensor_tensor(o, x, wcol[:, c, j:j + 1], o, ALU.mult, ALU.add)
                    chain.link(ins)
        w_in_.advance(32)
        cleared.advance(1)
        sig.advance(1)
        return span

    def silu_rows(rows):
        s = signal("row_silu")
        with nc.Block() as block:
            @block.scalar
            def _(act):
                for dst, src in rows:
                    nc.scalar.activation(dst, src, ACT.Silu).then_inc(s.sem, 1)
        s.advance(len(rows))

    def gate_rows(jobs, alpha):
        gated, summed = signal("branch_gated"), signal("branch_added")
        with nc.Block() as block:
            @block.gpsimd
            def _(pool):
                for i, (r, b, g) in enumerate(jobs):
                    if g is not None:
                        nc.gpsimd.tensor_tensor(b, b, g, ALU.mult).then_inc(gated.sem, 1)

            @block.vector
            def _(dve):
                for i, (r, b, g) in enumerate(jobs):
                    if g is not None:
                        dve.wait_ge(gated.sem, gated.upto(i))
                    nc.vector.scalar_tensor_tensor(r, r, alpha, b, ALU.mult, ALU.add).then_inc(summed.sem, 1)
        if jobs[0][2] is not None:
            gated.advance(len(jobs))
        summed.advance(len(jobs))

    def route(l, chunks, wr, logit, aff, pos, msk, af, at_, work, best):
        ntok = chunks * P
        products([dict(mm=[(0, ht[:, k, t * P:(t + 1) * P], wr[:, k, :]) for k in range(KD)],
                       out=out("copy", (0, P, 0, E, logit[:, t, :]))) for t in range(chunks)])
        lg = logit[:, 0:chunks, :]
        a3 = aff[:, 0:chunks, :]
        m1 = af[:, 0:chunks]
        shifted, powered, soft = signal("logits_shifted"), signal("logits_exp"), signal("affinity")
        with nc.Block() as block:
            @block.vector
            def _(dve):
                chain = Chain(dve, "dve_chain")
                chain.link(nc.vector.tensor_reduce(m1, lg, AX.X, ALU.max))
                nc.vector.tensor_tensor(lg, lg, m1.unsqueeze(2).to_broadcast([P, chunks, E]), ALU.subtract).then_inc(shifted.sem, 1)
                dve.wait_ge(powered.sem, powered.upto(0))
                chain.link(nc.vector.tensor_reduce(m1, lg, AX.X, ALU.add))
                chain.link(nc.vector.reciprocal(m1, m1))
                nc.vector.tensor_tensor(a3, lg, m1.unsqueeze(2).to_broadcast([P, chunks, E]), ALU.mult).then_inc(soft.sem, 1)

            @block.scalar
            def _(act):
                act.wait_ge(shifted.sem, shifted.upto(0))
                nc.scalar.activation(lg, lg, ACT.Exp).then_inc(powered.sem, 1)
        shifted.advance(1)
        powered.advance(1)
        soft.advance(1)
        groups = []
        for t0, t1 in ((0, TX), (TX, T))[:1 if chunks == TX else 2]:
            groups.append(dict(mm=[((t - t0) * P, aff[:, t, :], None) for t in range(t0, t1)],
                               out=out("copy", (0, E, 0, (t1 - t0) * P, at_[:, t0 * P:t1 * P]))))
        products(groups)
        picked = signal("picked")
        streams = [(0, SEQ, CAP_X), (SEQ, SEQ + CTX, CAP_C)][:1 if chunks == TX else 2]
        with nc.Block() as block:
            @block.vector
            def _(dve):
                chain = Chain(dve, "dve_chain")
                for a, b, cap in streams:
                    for _ in range(cap // 8):
                        chain.link(nc.vector.max(best, at_[:, a:b]))
                        chain.link(nc.vector.match_replace(at_[:, a:b], best, at_[:, a:b], -1.0))
                nc.vector.tensor_scalar(work, at_[:, 0:ntok], 0.0, None, ALU.is_lt).then_inc(picked.sem, 1)
        picked.advance(1)
        products([dict(mm=[(t * E, work[:, t * P:(t + 1) * P], None) for t in range(chunks)],
                       out=out("copy", (0, P, 0, chunks * E, msk[:, 0:chunks, :])))])
        groups = []
        mm = []
        for t in range(chunks):
            t0 = 0 if t < TX else TX
            for s in range(t0, t + 1):
                mm.append((t * E, cst(at1, "tri" if s == t else "ones"), msk[:, s, :]))
        groups.append(dict(mm=mm, out=out("copy", (0, P, 0, chunks * E, pos[:, 0:chunks, :]))))
        products(groups)
        slot = signal("slots_ready")
        with nc.Block() as block:
            @block.vector
            def _(dve):
                chain = Chain(dve, "dve_chain")
                p3, k3 = pos[:, 0:chunks, :], msk[:, 0:chunks, :]
                chain.link(nc.vector.tensor_tensor(p3, p3, k3, ALU.mult))
                nc.vector.tensor_scalar(p3, p3, -1.0, None, ALU.add).then_inc(slot.sem, 1)
        slot.advance(1)

    def experts(l, chunks, aff, pos, acc, base):
        ctx_too = chunks > TX
        a = base

        def take(*dims):
            nonlocal a
            v = mem(a, *dims)
            a += int(np.prod(dims))
            return v

        raw_x, raw_c = take(512), take(256)
        tok_x, tok_c = take(4, 2, CAP_X), take(2, 4, CAP_C)
        hid_x, hid_c = take(512), take(256)
        turn_x, turn_c = take(4, 2, CAP_X), take(2, 4, CAP_C)
        y_x, y_c = take(D), take(D)
        sel_x, sel_c = take(TX, CAP_X), take(TC, CAP_C)
        gat_x, gat_c = take(TX, P), take(TC, P)
        gt_x, gt_c = take(TX * P), take(TC * P)
        slot_col, aff_col = take(T), take(T)
        assert a <= EXTRA0 + 7 * K1 + 512, a - EXTRA0
        piece = [mem(RING0 + 4 * K1 * i, 4, D) for i in range(6)]
        src = [t_in[("w_gate", "w_up", "w_down")[j // 2]][l].rearrange("e (k p) n -> p e k n", p=P)
               [:, :, 4 * (j % 2):4 * (j % 2) + 4, :] for j in range(6)]
        landed = [signal(f"piece_in{j}") for j in range(6)]
        (used, cols_copied, picks, raw_full, raw_sb, tok_turned, tok_scaled, tok_ready, silu_ready, hid_ready, hid_turned,
         hid_sb, y_sb, gates_ready, gates_turned, gates_sb, spread, added, cleared) = (signal(x) for x in (
             "piece_used", "cols_copied", "picks_ready", "raw_full", "raw_sb", "tok_turned", "tok_scaled", "tok_ready",
             "silu_ready", "hid_ready", "hid_turned", "hid_sb", "y_sb", "gates_ready", "pair_gates_turned",
             "pair_gates_sb", "spread", "added", "sums_cleared"))
        n_out = 2 * chunks
        m3 = mod[:, :].rearrange("p (m s) -> p m s", s=2)

        def per_feature(m0, s):
            if s == 0:
                v = m3[:, m0:m0 + 8, 0].rearrange("p (h b) -> p b h", b=4)
                return v.unsqueeze(3).to_broadcast([P, 4, 2, CAP_X])
            v = m3[:, m0:m0 + 8, 1].rearrange("p (q b) -> p b q", b=2)
            return v.unsqueeze(3).to_broadcast([P, 2, 4, CAP_C])

        def count(s, turn, each, j):
            i, par = turn
            return i * (2 * each) + (s.base + par * each + j)

        def pair(s, turn, each, j):
            return turn[0] * each + (s.base + j)

        def pairs(eng, prologue, step):
            prologue()
            step((0, 0), True, False)
            step((0, 1), True, False)
            with eng.Fori(1, E // 2 - 1) as i:
                step((i, 0), False, False)
                step((i, 1), False, False)
            step((E // 2 - 1, 0), False, False)
            step((E // 2 - 1, 1), False, True)

        with nc.Block() as block:
            @block.gpsimd
            def _(pool):
                for t in range(chunks):
                    nc.gpsimd.memset(acc[:, t, :], 0.0).then_inc(cleared.sem, 1)
                nc.gpsimd.memset(gat_c, 0.0).then_inc(cleared.sem, 1)
                nc.gpsimd.memset(y_c, 0.0).then_inc(cleared.sem, 1)

            @block.sync
            def _(sp):
                for j in range(6):
                    sp.dma_start(piece[j], src[j][:, 0, :, :]).then_inc(landed[j].sem, 16)
                with sp.Fori(0, E - 1) as e:
                    for j in range(6):
                        sp.wait_ge(used.sem, e * 6 + (used.base + j + 1))
                        sp.dma_start(piece[j], src[j][:, bass.ds(e + 1, 1), :, :].rearrange("p o k n -> p (o k) n")).then_inc(landed[j].sem, 16)

            @block.vector
            def _(dve):
                def pick(turn, ahead):
                    i, par = turn
                    e = i * 2 + (par + ahead)
                    nc.vector.tensor_copy(slot_col[:, 0:chunks].unsqueeze(2), pos[:, 0:chunks, bass.ds(e, 1)])
                    nc.vector.tensor_copy(aff_col[:, 0:chunks].unsqueeze(2), aff[:, 0:chunks, bass.ds(e, 1)]).then_inc(cols_copied.sem, 1)
                    dve.wait_ge(cols_copied.sem, count(cols_copied, turn, 1, 1 + ahead))
                    for t in range(chunks):
                        cap, sel = (CAP_X, sel_x[:, t, :]) if t < TX else (CAP_C, sel_c[:, t - TX, :])
                        ins = nc.vector.tensor_scalar(sel, cst(at1, "slots")[:, 0:cap], slot_col[:, t:t + 1], None, ALU.is_equal)
                    ins.then_inc(picks.sem, 1)

                def modulate(turn, ahead):
                    dve.wait_ge(tok_turned.sem, count(tok_turned, turn, 1, 1 + ahead))
                    x4 = bank[4].rearrange("p (b h s) -> p b h s", b=4, h=2)
                    c4 = bank[5][:, 0:256].rearrange("p (b q s) -> p b q s", b=2, q=4)
                    ins = nc.vector.tensor_tensor(tok_x, x4, per_feature(32, 0), ALU.mult)
                    if ctx_too:
                        ins = nc.vector.tensor_tensor(tok_c, c4, per_feature(32, 1), ALU.mult)
                    ins.then_inc(tok_scaled.sem, 1)
                    dve.wait_ge(tok_scaled.sem, count(tok_scaled, turn, 1, 1 + ahead))
                    ins = nc.vector.tensor_tensor(tok_x, tok_x, per_feature(24, 0), ALU.add)
                    if ctx_too:
                        ins = nc.vector.tensor_tensor(tok_c, tok_c, per_feature(24, 1), ALU.add)
                    ins.then_inc(tok_ready.sem, 1)

                def gates(par):
                    for t in range(chunks):
                        cap, gat = (CAP_X, gat_x[:, t, :]) if t < TX else (CAP_C, gat_c[:, t - TX, :])
                        ins = nc.vector.tensor_scalar(gat[:, par * cap:(par + 1) * cap], cst(at1, "slots")[:, 0:cap],
                                                      slot_col[:, t:t + 1], aff_col[:, t:t + 1], ALU.is_equal, ALU.mult)
                    ins.then_inc(gates_ready.sem, 1)

                def prologue():
                    dve.wait_ge(cleared.sem, cleared.upto(chunks + 1))
                    pick((0, 0), 0)
                    modulate((0, 0), 0)
                    gates(0)

                def step(turn, first, last):
                    i, par = turn
                    if not last:
                        dve.wait_ge(raw_full.sem, count(raw_full, turn, 1, 1))
                        dve.wait_ge(gates_ready.sem, count(gates_ready, turn, 1, 1))
                        pick(turn, 1)
                    dve.wait_ge(silu_ready.sem, count(silu_ready, turn, 1, 1))
                    dve.wait_ge(used.sem, count(used, turn, 6, 4))
                    ins = nc.vector.tensor_tensor(hid_x, hid_x, bank[2], ALU.mult)
                    if ctx_too:
                        ins = nc.vector.tensor_tensor(hid_c, hid_c, bank[3][:, 0:256], ALU.mult)
                    ins.then_inc(hid_ready.sem, 1)
                    if not last:
                        modulate(turn, 1)
                        if par == 1:
                            dve.wait_ge(gates_turned.sem, pair(gates_turned, turn, 1, 1))
                        gates(1 - par)
                    if par == 1:
                        for n in range(n_out):
                            dve.wait_ge(spread.sem, pair(spread, turn, n_out, n + 1))
                            o = acc[:, n // 2, (n % 2) * 512:(n % 2) * 512 + 512]
                            nc.vector.tensor_tensor(o, o, bank[n % 4], ALU.add).then_inc(added.sem, 1)
                        dve.wait_ge(added.sem, pair(added, turn, n_out, n_out))

                pairs(dve, prologue, step)

            @block.scalar
            def _(act):
                def copy_raw(turn, ahead):
                    act.wait_ge(raw_full.sem, count(raw_full, turn, 1, 1 + ahead))
                    ins = nc.scalar.activation(raw_x, bank[4], ACT.Copy)
                    if ctx_too:
                        ins = nc.scalar.activation(raw_c, bank[5][:, 0:256], ACT.Copy)
                    ins.then_inc(raw_sb.sem, 1)

                def step(turn, first, last):
                    i, par = turn
                    act.wait_ge(used.sem, count(used, turn, 6, 2))
                    if par or not first:
                        act.wait_ge(hid_turned.sem, count(hid_turned, turn, 1, 0))
                    ins = nc.scalar.activation(hid_x, bank[0], ACT.Silu)
                    if ctx_too:
                        ins = nc.scalar.activation(hid_c, bank[1][:, 0:256], ACT.Silu)
                    ins.then_inc(silu_ready.sem, 1)
                    if not last:
                        act.wait_ge(tok_turned.sem, count(tok_turned, turn, 1, 1))
                        copy_raw(turn, 1)
                    if par == 1:
                        act.wait_ge(gates_turned.sem, pair(gates_turned, turn, 1, 1))
                        if not first:
                            act.wait_ge(spread.sem, pair(spread, turn, n_out, 0))
                        ins = nc.scalar.activation(gt_x, bank[6], ACT.Copy)
                        if ctx_too:
                            ins = nc.scalar.activation(gt_c, bank[7][:, 0:256], ACT.Copy)
                        ins.then_inc(gates_sb.sem, 1)
                    act.wait_ge(hid_turned.sem, count(hid_turned, turn, 1, 1))
                    if par or not first:
                        act.wait_ge(used.sem, count(used, turn, 6, 0))
                    ins = nc.scalar.activation(turn_x.rearrange("p b h s -> p (b h s)"), bank[6], ACT.Copy)
                    if ctx_too:
                        ins = nc.scalar.activation(turn_c.rearrange("p b q s -> p (b q s)"), bank[7][:, 0:256], ACT.Copy)
                    ins.then_inc(hid_sb.sem, 1)
                    act.wait_ge(used.sem, count(used, turn, 6, 6))
                    if par == 0 and not first:
                        act.wait_ge(spread.sem, pair(spread, turn, n_out, 0))
                    for h in range(2):
                        ins = nc.scalar.activation(y_x[64 * par:64 * par + 64, h * 512:(h + 1) * 512],
                                                   bank[6][64 * h:64 * h + 64, :], ACT.Copy)
                    if ctx_too:
                        if first and par == 0:
                            act.wait_ge(cleared.sem, cleared.upto(chunks + 1))
                        for q in range(4):
                            ins = nc.scalar.activation(y_c[32 * par:32 * par + 32, q * 256:(q + 1) * 256],
                                                       bank[7][32 * q:32 * q + 32, 0:256], ACT.Copy)
                    ins.then_inc(y_sb.sem, 1)

                pairs(act, lambda: copy_raw((0, 0), 0), step)

            @block.tensor
            def _(pe):
                ident = cst(at1, "ident")

                def gather(turn, ahead):
                    pe.wait_ge(picks.sem, count(picks, turn, 1, 1 + ahead))
                    for t in range(TX):
                        for h in range(2):
                            ins = nc.tensor.matmul(bank[4][64 * h:64 * h + 64, :], lhsT=sel_x[:, t, :],
                                                   rhs=lnx[:, t, h * 512:(h + 1) * 512], start=t == 0, stop=t == TX - 1)
                    for t in range(TX, chunks):
                        for q in range(4):
                            ins = nc.tensor.matmul(bank[5][32 * q:32 * q + 32, 0:256], lhsT=sel_c[:, t - TX, :],
                                                   rhs=lnx[:, t, q * 256:(q + 1) * 256], start=t == TX, stop=t == T - 1)
                    ins.then_inc(raw_full.sem, 1)

                def turn_tokens():
                    for b in range(4):
                        ins = nc.tensor.transpose(bank[4][:, b * P:(b + 1) * P], raw_x[:, b * P:(b + 1) * P], ident)
                    if ctx_too:
                        for b in range(2):
                            ins = nc.tensor.transpose(bank[5][:, b * P:(b + 1) * P], raw_c[:, b * P:(b + 1) * P], ident)
                    ins.then_inc(tok_turned.sem, 1)

                def stream(turn, j0, lhs_x, lhs_c, out_x, out_c):
                    for k in range(KD):
                        w = piece[j0 + k // 4]
                        if k % 4 == 0:
                            pe.wait_ge(landed[j0 + k // 4].sem, count(landed[j0 + k // 4], turn, 16, 16))
                        for h in range(2):
                            ins = nc.tensor.matmul(out_x[64 * h:64 * h + 64, :], lhsT=lhs_x[:, k % 4, k // 4, :],
                                                   rhs=w[:, k % 4, h * 512:(h + 1) * 512], start=k == 0, stop=k == KD - 1)
                        if ctx_too:
                            for q in range(4):
                                ins = nc.tensor.matmul(out_c[32 * q:32 * q + 32, 0:256], lhsT=lhs_c[:, k % 2, k // 2, :],
                                                       rhs=w[:, k % 4, q * 256:(q + 1) * 256], start=k == 0, stop=k == KD - 1)
                        if k % 4 == 3:
                            ins.then_inc(used.sem, 1)

                def prologue():
                    gather((0, 0), 0)
                    pe.wait_ge(raw_sb.sem, count(raw_sb, (0, 0), 1, 1))
                    turn_tokens()

                def step(turn, first, last):
                    i, par = turn
                    pe.wait_ge(tok_ready.sem, count(tok_ready, turn, 1, 1))
                    if par or not first:
                        pe.wait_ge(hid_ready.sem, count(hid_ready, turn, 1, 0))
                    if par == 0 and not first:
                        pe.wait_ge(added.sem, pair(added, turn, n_out, 0))
                    stream(turn, 0, tok_x, tok_c, bank[0], bank[1])
                    stream(turn, 2, tok_x, tok_c, bank[2], bank[3])
                    if par or not first:
                        pe.wait_ge(y_sb.sem, count(y_sb, turn, 1, 0))
                    if not last:
                        gather(turn, 1)
                    if par == 1:
                        pe.wait_ge(gates_ready.sem, count(gates_ready, turn, 1, 1))
                        for t in range(chunks):
                            o = bank[6][:, t * P:(t + 1) * P] if t < TX else bank[7][:, (t - TX) * P:(t - TX + 1) * P]
                            ins = nc.tensor.transpose(o, gat_x[:, t, :] if t < TX else gat_c[:, t - TX, :], ident)
                        ins.then_inc(gates_turned.sem, 1)
                    if not last:
                        pe.wait_ge(raw_sb.sem, count(raw_sb, turn, 1, 2))
                        turn_tokens()
                    pe.wait_ge(hid_ready.sem, count(hid_ready, turn, 1, 1))
                    if par == 1:
                        pe.wait_ge(gates_sb.sem, pair(gates_sb, turn, 1, 1))
                    for b in range(4):
                        ins = nc.tensor.transpose(bank[6][:, b * P:(b + 1) * P], hid_x[:, b * P:(b + 1) * P], ident)
                    if ctx_too:
                        for b in range(2):
                            ins = nc.tensor.transpose(bank[7][:, b * P:(b + 1) * P], hid_c[:, b * P:(b + 1) * P], ident)
                    ins.then_inc(hid_turned.sem, 1)
                    pe.wait_ge(hid_sb.sem, count(hid_sb, turn, 1, 1))
                    stream(turn, 4, turn_x, turn_c, bank[6], bank[7])
                    if par == 1:
                        pe.wait_ge(y_sb.sem, count(y_sb, turn, 1, 1))
                        for n in range(n_out):
                            t, h = n // 2, n % 2
                            if n >= 4:
                                pe.wait_ge(added.sem, pair(added, turn, n_out, n - 3))
                            gt, y = (gt_x[:, t * P:(t + 1) * P], y_x) if t < TX else (gt_c[:, (t - TX) * P:(t - TX + 1) * P], y_c)
                            nc.tensor.matmul(bank[n % 4], lhsT=gt, rhs=y[:, h * 512:(h + 1) * 512],
                                             start=True, stop=True).then_inc(spread.sem, 1)

                pairs(pe, prologue, step)
        cleared.advance(chunks + 2)
        for s in landed:
            s.advance(16 * E)
        used.advance(6 * E)
        for s in (cols_copied, picks, raw_full, raw_sb, tok_turned, tok_scaled, tok_ready, silu_ready, hid_ready,
                  hid_turned, hid_sb, y_sb, gates_ready):
            s.advance(E)
        gates_turned.advance(E // 2)
        gates_sb.advance(E // 2)
        spread.advance(n_out * E // 2)
        added.advance(n_out * E // 2)

    def finish_debug(name, v):
        if debug != name:
            return False
        s = signal("debug_out")
        with nc.Block() as block:
            @block.sync
            def _(sp):
                sp.dma_start(out_dbg(v), v).then_inc(s.sem, 16)
                sp.wait_ge(s.sem, s.upto(0, 16))
        s.advance(16)
        return True

    def out_dbg(v):
        return nc.dram_tensor("dbg", list(v.shape), F32, kind="ExternalOutput").ap()

    def head_norms(u2, hx, sq, wt):
        H = A_HEADS + 6
        w_in_, squared, v_ready, v_root, normed = (signal(x) for x in (
            "head_w_in", "squared", "var_ready", "root_ready", "heads_normed"))
        ss, ve, rs = (small[:, 64 * i:64 * i + TX * H].rearrange("p (t h) -> p t h", h=H) for i in range(3))
        qn, kn = t_in["q_norm_w_2"], t_in["k_norm_w_2"]

        def spans(t):
            yield u2[:, t, 0:512], lambda b: b[:, t, 0:8, :].rearrange("p h d -> p (h d)"), (0, 8)
            ks = u2[:, t, 512:1280].rearrange("p (i n) -> p i n", n=256)[:, :, 0:128]
            yield ks, lambda b: b[:, t, 8:14, :].rearrange("p (i g) d -> p i (g d)", g=2), (8, 14)

        with nc.Block() as block:
            @block.sync
            def _(sp):
                sp.dma_start(wt[:, 0:8, :], bass.AP(qn.tensor, qn.offset, [[0, P], [0, 8], [1, HD]])).then_inc(w_in_.sem, 16)
                for i in range(3):
                    sp.dma_start(wt[:, 8 + 2 * i:10 + 2 * i, :],
                                 bass.AP(kn.tensor, kn.offset + i * HD, [[0, P], [0, 2], [1, HD]])).then_inc(w_in_.sem, 16)

            @block.gpsimd
            def _(pool):
                for t in range(TX):
                    for x, at_buf, _ in spans(t):
                        nc.gpsimd.tensor_tensor(at_buf(sq), x, x, ALU.mult).then_inc(squared.sem, 1)

            @block.scalar
            def _(act):
                act.wait_ge(v_ready.sem, v_ready.upto(0))
                nc.scalar.activation(ve, ve, ACT.Sqrt).then_inc(v_root.sem, 1)

            @block.vector
            def _(dve):
                chain = Chain(dve, "dve_chain")
                for t in range(TX):
                    dve.wait_ge(squared.sem, squared.upto(2 * t + 1))
                    ins = nc.vector.tensor_reduce(ss[:, t, :], sq[:, t, :, :], AX.X, ALU.add)
                chain.link(ins)
                nc.vector.tensor_scalar(ve, ss, 1.0 / HD, LN_EPS, ALU.mult, ALU.add).then_inc(v_ready.sem, 1)
                dve.wait_ge(v_root.sem, v_root.upto(0))
                chain.link(nc.vector.reciprocal(rs, ve))
                dve.wait_ge(w_in_.sem, w_in_.upto(3, 16))
                for t in range(TX):
                    for h in range(H):
                        if h < 8:
                            x = u2[:, t, h * HD:(h + 1) * HD]
                        else:
                            a = 512 + 256 * ((h - 8) // 2) + HD * (h % 2)
                            x = u2[:, t, a:a + HD]
                        ins = nc.vector.scalar_tensor_tensor(hx[:, t, h, :], x, rs[:, t, h:h + 1], wt[:, h, :], ALU.mult, ALU.mult)
                    ins.then_inc(normed.sem, 1)
        w_in_.advance(64)
        squared.advance(2 * TX)
        v_ready.advance(1)
        v_root.advance(1)
        normed.advance(TX)

    def retain(u2, rr, kz, rqt, rkt, it, state, mixb):
        units = [(t, h) for t in range(TX) for h in range(4)]
        n = len(units)
        zetad, inner_full, inner_sb, full, taken = (signal(x) for x in (
            "keys_decayed", "inner_full", "inner_decayed", "unit_full", "unit_taken"))

        def place(h):
            return slice(64 * (h % 2), 64 * (h % 2) + 64), h // 2

        with nc.Block() as block:
            @block.gpsimd
            def _(pool):
                for t, h in units:
                    nc.gpsimd.tensor_scalar(kz[:, t, h, :], rr[:, t, 4 + h, :], cst(at2, "zeta")[:, h:h + 1], None,
                                            ALU.mult).then_inc(zetad.sem, 1)

            @block.tensor
            def _(pe):
                for i in range(n + 1):
                    if i < n:
                        t, h = units[i]
                        rows, j = place(h)
                        if i >= 2:
                            pe.wait_ge(inner_sb.sem, inner_sb.upto(i - 2))
                        cols = slice(t * P, (t + 1) * P)
                        nc.tensor.matmul(bank[i % 2][:, 0:P], lhsT=rkt[rows, j, cols], rhs=rqt[rows, j, cols],
                                         start=True, stop=True).then_inc(inner_full.sem, 1)
                    u = i - 1
                    if u >= 0:
                        t, h = units[u]
                        rows, j = place(h)
                        v = u2[:, t, 1816 + h * P:1816 + (h + 1) * P]
                        pe.wait_ge(inner_sb.sem, inner_sb.upto(u))
                        if u >= 2:
                            pe.wait_ge(taken.sem, taken.upto(u - 2))
                        ins = nc.tensor.matmul(bank[2 + u % 2][:, 0:P], lhsT=it[:, u % 2, :], rhs=v, start=True, stop=True)
                        if t > 0:
                            ins = nc.tensor.matmul(bank[4 + u % 2][:, 0:P], lhsT=rqt[rows, j, t * P:(t + 1) * P],
                                                   rhs=state[rows, j, :], start=True, stop=True)
                        if t < TX - 1:
                            pe.wait_ge(zetad.sem, zetad.upto(u))
                            ins = nc.tensor.matmul(bank[6 + u % 2][rows, 0:P], lhsT=kz[:, t, h, :], rhs=v, start=True, stop=True)
                        ins.then_inc(full.sem, 1)

            @block.vector
            def _(dve):
                chain = Chain(dve, "dve_chain")
                for i in range(n + 1):
                    if i < n:
                        t, h = units[i]
                        dve.wait_ge(inner_full.sem, inner_full.upto(i))
                        if i >= 2:
                            dve.wait_ge(full.sem, full.upto(i - 2))
                        nc.vector.tensor_tensor(it[:, i % 2, :], bank[i % 2][:, 0:P],
                                                cst(at2, "decay")[:, h * P:(h + 1) * P], ALU.mult).then_inc(inner_sb.sem, 1)
                    u = i - 1
                    if u >= 0:
                        t, h = units[u]
                        rows, j = place(h)
                        y = mixb[:, t, 512 + h * P:512 + (h + 1) * P]
                        dve.wait_ge(full.sem, full.upto(u))
                        ins = nc.vector.tensor_copy(y, bank[2 + u % 2][:, 0:P])
                        if t > 0:
                            chain.link(ins)
                            ins = nc.vector.scalar_tensor_tensor(y, bank[4 + u % 2][:, 0:P], cst(at2, "xi")[:, h:h + 1], y,
                                                                 ALU.mult, ALU.add)
                        if t == 0:
                            ins = nc.vector.tensor_copy(state[rows, j, :], bank[6 + u % 2][rows, 0:P])
                        elif t < TX - 1:
                            ins = nc.vector.scalar_tensor_tensor(state[rows, j, :], state[rows, j, :], cst(at2, "gc")[rows, h:h + 1],
                                                                 bank[6 + u % 2][rows, 0:P], ALU.mult, ALU.add)
                        ins.then_inc(taken.sem, 1)
        zetad.advance(n)
        for s in (inner_full, inner_sb, full, taken):
            s.advance(n)

    def sparse_attention_block():
        lncol = small[:, 688:704].rearrange("p (i k) -> p i k", k=KD)
        load([(consts[:, 0:c2.shape[1]], t_in["consts2"]), (lncol[:, 0, :], t_in["ln1_w_cols"][0]),
              (lncol[:, 1, :], t_in["ln2_w_cols"][0])], "second_in")
        normalise([(res[:, t, :], lnx[:, t, :]) for t in range(TX)], LN_EPS, mean=False)
        turn_rows(lnx, lambda s, k: lncol[:, 0, k:k + 1], None, TX)
        u2 = mem(LNX0, TX, IN2_W)
        w = mem(RING0, KD, IN2_W)
        w_src = t_in["w_in_2"][0].rearrange("(k p) n -> p k n", p=P)
        cuts = [(a, min(a + 512, IN2_W)) for a in range(0, IN2_W, 512)]
        groups = []
        for i, (a, b) in enumerate(cuts):
            for t in range(TX):
                groups.append(dict(need=i + 1,
                                   mm=[(0, ht[:, k, t * P:(t + 1) * P], w[:, k, a:b]) for k in range(KD)],
                                   out=out("copy", (0, P, 0, b - a, u2[:, t, a:b]))))
        products(groups, [(w[:, :, a:b], w_src[:, :, a:b], 0) for a, b in cuts])
        H = A_HEADS + 6
        hx = mem(RING0, TX * H, HD).rearrange("p (t h) d -> p t h d", h=H)
        sq = mem(RING0 + 3584, TX * H, HD).rearrange("p (t h) d -> p t h d", h=H)
        qr, kr = mem(RING0 + 7168, TX, 512), mem(RING0 + 9216, TX, 384)
        rr = mem(RING0 + 10752, TX, 512)
        wt = mem(RING0 + 12800, H, HD)
        dup = mem(RING0 + 13696, TX, 512)
        head_norms(u2, hx, sq, wt)
        jobs = []
        for t in range(TX):
            for g in range(A_KV):
                jobs.append((hx[:, t, 4 * g:4 * g + 4, :], qr[:, t, :].rearrange("p (j g d) -> p g j d", g=A_KV, d=HD)[:, g], t, 4))
            jobs.append((hx[:, t, 8:14, :], kr[:, t, :].rearrange("p (h d) -> p h d", d=HD), t, 6))
            jobs.append((u2[:, t, 1304:1816].rearrange("p (h d) -> p h d", d=HD), rr[:, t, :].rearrange("p (h d) -> p h d", d=HD), t, 8))
        rotate(jobs, at2, 32)
        gts = mem(RING0 + 23 * K1, TX, 24)
        doubled, gated = signal("rows_doubled"), signal("branch_gates")
        with nc.Block() as block:
            @block.scalar
            def _(act):
                nc.scalar.activation(gts, u2[:, :, 1280:1304], ACT.Sigmoid).then_inc(gated.sem, 1)

            @block.vector
            def _(dve):
                for t in range(TX):
                    for i, src in enumerate((kr[:, t, 0:128], u2[:, t, 640:768])):
                        d = dup[:, t, 256 * i:256 * i + 256].rearrange("p (g c d) -> p g c d", g=2, c=2)
                        x = src.rearrange("p (g d) -> p g d", d=HD)
                        for c in range(2):
                            nc.vector.tensor_copy(d[:, :, c, :], x).then_inc(doubled.sem, 1)
                dve.wait_ge(gated.sem, gated.upto(0))
                some = cst(at2, "some").unsqueeze(2).to_broadcast([P, TX, 8])
                nc.vector.tensor_tensor(gts[:, :, 0:8], gts[:, :, 0:8], some, ALU.mult).then_inc(doubled.sem, 1)
        doubled.advance(4 * TX + 1)
        gated.advance(1)
        qt, kst, kwt = mem(RING0 + 15744, 4, SEQ), mem(RING0 + 17792, SEQ), mem(RING0 + 18304, SEQ)
        rqt, rkt = mem(RING0 + 18816, 2, SEQ), mem(RING0 + 19840, 2, SEQ)
        kc2 = mem(RING0 + 20864, 4, SEQ)
        groups = []

        def turn(src, dst, scale=None):
            mm = [(t * P, src(t), None) for t in range(TX)]
            o = out("copy", (0, P, 0, SEQ, dst)) if scale is None else out("scale", (0, P, 0, SEQ, dst, scale))
            groups.append(dict(mm=mm, out=o))

        for j in range(4):
            turn(lambda t: qr[:, t, j * P:(j + 1) * P], qt[:, j, :])
        turn(lambda t: kr[:, t, 128:256], kst)
        turn(lambda t: kr[:, t, 256:384], kwt)
        for j in range(2):
            turn(lambda t: rr[:, t, j * P:(j + 1) * P], rqt[:, j, :])
            turn(lambda t: rr[:, t, 256 + j * P:256 + (j + 1) * P], rkt[:, j, :], SCALE)
        for i in range(4):
            groups.append(dict(mm=[(t * P, dup[:, t, i * P:(i + 1) * P], None) for t in range(TX)],
                               out=out("copy", (0, 64, 0, SEQ, kc2[0:64, i, :]), (64, P, 1, SEQ, kc2[64:P, i, 0:SEQ - 1]))))
        products(groups)
        w1 = [mem(RING0 + 4096 * i, 16, CMP_HID) for i in range(2)]
        w2 = [mem(RING0 + 8192 + 128 * i, 2, HD) for i in range(2)]
        pe_ = [mem(RING0 + 8448 + 16 * i, 16) for i in range(2)]
        hraw = mem(RING0 + 8480, 4, 65)
        hc = mem(RING0 + 8740, 4, 2 * N_CMP)
        kcmp, vcmp = mem(RING0 + 8988, N_CMP + 1), mem(RING0 + 9020, 2, HD, parts=N_CMP)
        loads = []
        for i, kind in enumerate(("k", "v")):
            loads.append((w1[i], t_in[f"cmp_w{kind}1_2"][0].rearrange("(j p) n -> p j n", p=P), 0))
            loads.append((w2[i], t_in[f"cmp_w{kind}2_2"][0].rearrange("(j p) n -> p j n", p=P), 0))
            loads.append((pe_[i], t_in[f"cmp_pe_{kind}_cols"][0], 0))
        groups = []
        for i in range(2):
            for half in range(2):
                lhs = [w1[i][:, j, half * P:(half + 1) * P] for j in range(16)]
                mm = [(0, lhs[j], kc2[:, 2 * i:2 * i + 2, 2 * j:2 * j + 16 * (N_CMP - 1) + 1:16]) for j in range(16)]
                mm += [(2 * N_CMP, lhs[j], pe_[i][:, j:j + 1]) for j in range(16)]
                groups.append(dict(need=3 * i + 3, mm=mm, out=out("copy", (0, P, 0, 2 * N_CMP + 1, hraw[:, 2 * i + half, 0:2 * N_CMP + 1]))))
        products(groups, loads)
        silued = signal("hidden_silu")
        with nc.Block() as block:
            @block.scalar
            def _(act):
                for i in range(4):
                    nc.scalar.activation(hc[:, i, :], hraw[:, i, 0:2 * N_CMP], ACT.Silu,
                                         bias=hraw[:, i, 2 * N_CMP:2 * N_CMP + 1]).then_inc(silued.sem, 1)
        silued.advance(4)
        groups = []
        for g in range(2):
            cols = slice(g * N_CMP, (g + 1) * N_CMP)
            groups.append(dict(p0=64 * g, mm=[(0, w2[0][:, h, :], hc[:, h, cols]) for h in range(2)],
                               out=out("copy", (64 * g, 64 * g + 64, 0, N_CMP, kcmp[64 * g:64 * g + 64, 0:N_CMP]))))
            groups.append(dict(mm=[(0, hc[:, 2 + h, cols], w2[1][:, h, :]) for h in range(2)],
                               out=out("copy", (0, N_CMP, 0, HD, vcmp[:, g, :]))))
        products(groups)
        mixb = mem(HT0, TX, D)
        units = []
        for branch in range(3):
            for h in range(A_HEADS):
                g, j = h // 4, h % 4
                rows = slice(64 * g, 64 * g + 64)
                for t in range(TX):
                    u = dict(q=qt[rows, j, t * P:(t + 1) * P], out=mixb[:, t, h * HD:(h + 1) * HD],
                             gate=gts[:, t, branch * 8 + h:branch * 8 + h + 1], add=branch > 0)
                    if branch == 0:
                        seen = cst(at2, "seen")[:, t * 32:t * 32 + N_CMP]
                        u.update(keys=[(0, kcmp[rows, 0:N_CMP])], evac=[(0, 0, N_CMP, seen)], n=N_CMP, v=[vcmp[:, g, :]])
                    else:
                        s0 = 0 if branch == 1 else max(0, t - 2)
                        kT = kst if branch == 1 else kwt
                        m = t - s0
                        vcol = slice((896 if branch == 1 else 1152) + g * HD, (896 if branch == 1 else 1152) + (g + 1) * HD)
                        evac = []
                        for s in range(s0, t + 1):
                            bias = cst(at2, "lower") if s == t else cst(at2, "above") if branch == 2 and s == t - 2 else None
                            if bias is None and evac and evac[-1][3] is None:
                                evac[-1] = (evac[-1][0], evac[-1][1], evac[-1][2] + P, None)
                            else:
                                evac.append(((s - s0) * P, (s - s0) * P, P, bias))
                        u.update(keys=[(0, kT[rows, s0 * P:(t + 1) * P])], evac=evac, n=(t + 1 - s0) * P,
                                 v=[u2[:, s, vcol] for s in range(s0, t + 1)])
                    units.append(u)
        attend(units, RING0, at2)
        kz = mem(RING0, TX * 4, HD).rearrange("p (t h) d -> p t h d", h=4)
        it, state = mem(RING0 + 1024, 2, P), mem(RING0 + 1280, 2, P)
        retain(u2, rr.rearrange("p t (h d) -> p t h d", d=HD), kz, rqt, rkt, it, state, mixb)
        normalise([(mixb[:, t, 512 + h * P:512 + (h + 1) * P],) * 2 for t in range(TX) for h in range(4)], LN_EPS, width=P)
        rw = mem(RING0 + 2048, 512)
        load([(rw, t_in["ret_norm_w_2"][0].rearrange("h d -> (h d)").partition_broadcast(P))], "ret_norm_in")
        weighted, gate_silu, gated = signal("rows_weighted"), signal("ret_gate_silu"), signal("rows_gated")
        with nc.Block() as block:
            @block.gpsimd
            def _(pool):
                for t in range(TX):
                    nc.gpsimd.tensor_tensor(mixb[:, t, 512:D], mixb[:, t, 512:D], rw, ALU.mult).then_inc(weighted.sem, 1)

            @block.scalar
            def _(act):
                for t in range(TX):
                    nc.scalar.activation(u2[:, t, 2328:2840], u2[:, t, 2328:2840], ACT.Silu).then_inc(gate_silu.sem, 1)

            @block.vector
            def _(dve):
                for t in range(TX):
                    dve.wait_ge(weighted.sem, weighted.upto(t))
                    dve.wait_ge(gate_silu.sem, gate_silu.upto(t))
                    nc.vector.tensor_tensor(mixb[:, t, 512:D], mixb[:, t, 512:D], u2[:, t, 2328:2840], ALU.mult).then_inc(gated.sem, 1)
        for s in (weighted, gate_silu, gated):
            s.advance(TX)
        if finish_debug("mix2", mixb):
            return
        wo = mem(RING0, KD, D)
        mixt = mem(RING0 + 8 * K1, KD, SEQ)
        products([dict(mm=[(t * P, mixb[:, t, k * P:(k + 1) * P], None) for t in range(TX)],
                       out=out("copy", (0, P, 0, SEQ, mixt[:, k, :]))) for k in range(KD)])
        branch = lnx
        products([dict(need=1, mm=[(0, mixt[:, k, t * P:(t + 1) * P], wo[:, k, n * 512:(n + 1) * 512]) for k in range(KD)],
                       out=out("copy", (0, P, 0, 512, branch[:, t, n * 512:(n + 1) * 512]))) for t in range(TX) for n in range(2)],
                 [(wo, t_in["w_out_2"][0].rearrange("(k p) n -> p k n", p=P), 0)])
        gate_rows([(res[:, t, :], branch[:, t, :], None) for t in range(TX)], 1.0)
        normalise([(res[:, t, :], lnx[:, t, :]) for t in range(TX)], LN_EPS, mean=False)
        turn_rows(lnx, lambda s, k: lncol[:, 1, k:k + 1], None, TX)
        NF = FF2 // P
        hid = [mem(LNX0 + 512 * c, 512) if c < 27 else mem(RING0 + 20 * K1 + 512 * (c - 27), 512) for c in range(NF)]
        slot = [mem(RING0 + 4 * K1 * i, KD, 512) for i in range(4)]
        wu = t_in["w_up_2"][0].rearrange("(k p) n -> p k n", p=P)
        products([dict(need=c // 4 + 1, mm=[(0, slot[c // 4 % 4][:, k, (c % 4) * P:(c % 4 + 1) * P], ht[:, k, 0:SEQ]) for k in range(KD)],
                       out=out("relu2", (0, P, 0, SEQ, hid[c]))) for c in range(NF)],
                 [(slot[n % 4], wu[:, :, n * 512:(n + 1) * 512], 4 * (n - 3) if n >= 4 else 0) for n in range(8)])
        wd = t_in["w_down_2"][0].rearrange("(c p) n -> p c n", p=P)
        slot = [mem(RING0 + 4 * K1 * i, 4, D) for i in range(5)]
        down_in = [signal(f"down_in{i}") for i in range(5)]
        used, finished, stored = signal("down_used"), signal("out_ready"), signal("stored")
        with nc.Block() as block:
            @block.sync
            def _(sp):
                for n in range(8):
                    if n >= 5:
                        sp.wait_ge(used.sem, used.upto(n - 5))
                    sp.dma_start(slot[n % 5], wd[:, 4 * n:4 * n + 4, :]).then_inc(down_in[n % 5].sem, 16)
                for t in range(TX):
                    sp.wait_ge(finished.sem, finished.upto(2 * t + 1))
                    sp.dma_start(final.rearrange("o (t p) d -> p (o t) d", p=P)[:, t, :], res[:, t, :]).then_inc(stored.sem, 16)
                sp.wait_ge(stored.sem, stored.upto(TX - 1, 16))

            @block.tensor
            def _(pe):
                for n in range(8):
                    pe.wait_ge(down_in[n % 5].sem, down_in[n % 5].upto(n // 5, 16))
                    for c in range(4 * n, 4 * n + 4):
                        for t in range(TX):
                            for m in range(2):
                                ins = nc.tensor.matmul(bank[2 * t + m], lhsT=hid[c][:, t * P:(t + 1) * P],
                                                       rhs=slot[n % 5][:, c % 4, m * 512:(m + 1) * 512],
                                                       start=c == 0, stop=c == NF - 1)
                    ins.then_inc(used.sem, 1)

            @block.vector
            def _(dve):
                dve.wait_ge(used.sem, used.upto(7))
                for i in range(8):
                    o = res[:, i // 2, (i % 2) * 512:(i % 2 + 1) * 512]
                    nc.vector.tensor_tensor(o, o, bank[i], ALU.add).then_inc(finished.sem, 1)


    final = out_ap
    with ctx:
        load([(consts[:, 0:c1.shape[1]], t_in["consts1"]),
              (res[:, 0:TX, :], t_in["x"][0].rearrange("(t p) d -> p t d", p=P)),
              (res[:, TX:T, :], t_in["ctx"][0].rearrange("(t p) d -> p t d", p=P))]
             + [(bias_rows[l].rearrange("(c n) -> c n", c=64),
                 t_in["nat_bias"][l].rearrange("h r c -> (h r c)").partition_broadcast(64)) for l in range(LAYERS)],
             "start_in")
        m3 = mod[:, :].rearrange("p (m s) -> p m s", s=2)
        for l in range(LAYERS):
            last = l == LAYERS - 1
            nt = TX if last else T
            adaln(l)
            if finish_debug(f"mod{l}", mod[:, :]):
                return
            normalise([(res[:, t, :], lnx[:, t, :]) for t in range(T)], LN_EPS)
            turn_rows(lnx, lambda s, k: m3[:, 8 + k, s:s + 1], lambda s, k: m3[:, k, s:s + 1], T)
            if finish_debug(f"ht{l}", ht[:, :, :]):
                return
            w = mem(RING0, KD, IN_W)
            qkv = mem(LNX0, T, QKV_W)
            glu = mem(LNX0 + T * QKV_W, 4, SEQ + CTX)
            w_src = t_in["w_in"][l].rearrange("(k p) n -> p k n", p=P)
            loads = [(w[:, :, n * 512:(n + 1) * 512], w_src[:, :, n * 512:(n + 1) * 512], 0) for n in range(4)]
            wo = mem(RING0 + 16 * K1, KD, D)
            groups = []
            for n in range(3):
                for t in range(T):
                    groups.append(dict(need=n + 1,
                                       mm=[(0, ht[:, k, t * P:(t + 1) * P], w[:, k, n * 512:(n + 1) * 512]) for k in range(KD)],
                                       out=out("copy", (0, P, 0, 512, qkv[:, t, n * 512:(n + 1) * 512]))))
            for c in range(4):
                for c0, c1_ in ((0, SEQ), (SEQ, SEQ + CTX))[:1 if last else 2]:
                    groups.append(dict(need=4,
                                       mm=[(0, w[:, k, 3 * 512 + c * P:3 * 512 + (c + 1) * P], ht[:, k, c0:c1_]) for k in range(KD)],
                                       out=out("copy", (0, P, 0, c1_ - c0, glu[:, c, c0:c1_]))))
            products(groups, loads)
            qr = mem(HT0, T, 512)
            kr = mem(HT0 + T * 512, T, P)
            jobs = []
            for t in range(TX):
                for g in range(A_KV):
                    srcq = qkv[:, t, g * 256:(g + 1) * 256].rearrange("p (j d) -> p j d", d=HD)
                    dstq = qr[:, t, :].rearrange("p (j g d) -> p g j d", g=A_KV, d=HD)[:, g]
                    jobs.append((srcq, dstq, t, A_GROUP))
                jobs.append((qkv[:, t, 512:640].rearrange("p (j d) -> p j d", d=HD),
                             kr[:, t, :].rearrange("p (j d) -> p j d", d=HD), t, A_KV))
            rotate(jobs, at1, 16)
            if not last:
                moved = signal("queries_moved")
                with nc.Block() as block:
                    @block.vector
                    def _(dve):
                        for t in range(TX, T):
                            for g in range(A_KV):
                                nc.vector.tensor_copy(
                                    qr[:, t, :].rearrange("p (j g d) -> p g j d", g=A_KV, d=HD)[:, g],
                                    qkv[:, t, g * 256:(g + 1) * 256].rearrange("p (j d) -> p j d", d=HD)).then_inc(moved.sem, 1)
                moved.advance(2 * TC)
            QT0 = RING0
            qta, kta = mem(QT0, A_GROUP, 768), mem(QT0 + 4 * 768, 768)
            qtb, ktb = mem(QT0 + 5 * 768, 2, 768), mem(QT0 + 7 * 768, 2, 768)
            groups = []
            for c0, c1_ in ((0, TX), (TX, T)):
                n = (c1_ - c0) * P
                cols = slice(c0 * P, c1_ * P)
                latent = c0 == 0
                if latent or not last:
                    for j in range(A_GROUP):
                        mm = [((t - c0) * P, qr[:, t, j * P:(j + 1) * P], None) for t in range(c0, c1_)]
                        groups.append(dict(mm=mm, out=out("copy", (0, P, 0, n, qta[:, j, cols]))))
                    for j in range(2):
                        groups.append(dict(mm=[((t - c0) * P, qkv[:, t, 768 + j * P:768 + (j + 1) * P], None) for t in range(c0, c1_)],
                                           out=out("copy", (0, P, 0, n, qtb[:, j, cols]))))
                groups.append(dict(mm=[((t - c0) * P, kr[:, t, :] if latent else qkv[:, t, 512:640], None) for t in range(c0, c1_)],
                                   out=out("copy", (0, P, 0, n, kta[:, cols]))))
                for j in range(2):
                    groups.append(dict(mm=[((t - c0) * P, qkv[:, t, 1024 + j * P:1024 + (j + 1) * P], None) for t in range(c0, c1_)],
                                       out=out("copy", (0, P, 0, n, ktb[:, j, cols]))))
            products(groups)
            sink, nsink = small[:, 32:40], small[:, 40:48]
            load([(sink, t_in["a_sink"][l].partition_broadcast(P)),
                  (wo, t_in["w_out"][l].rearrange("(k p) n -> p k n", p=P))], "sinks_in")
            negated = signal("sinks_negated")
            with nc.Block() as block:
                @block.vector
                def _(dve):
                    nc.vector.tensor_scalar(nsink, sink, -1.0, None, ALU.mult).then_inc(negated.sem, 1)
            negated.advance(1)
            mix = mem(HT0, T, D)
            units = []
            for h in range(A_HEADS):
                g, j = h // A_GROUP, h % A_GROUP
                rows = slice(64 * g, 64 * g + 64)
                sk = dict(sink=sink[:, h:h + 1], nsink=nsink[:, h:h + 1])
                for t in range(nt):
                    u = dict(q=qta[rows, j, t * P:(t + 1) * P], out=mix[:, t, h * HD:(h + 1) * HD], **sk)
                    vcol = slice(640 + g * HD, 640 + (g + 1) * HD)
                    u["keys"] = [(0, kta[rows, SEQ:SEQ + CTX])]
                    u["evac"] = [(0, 0, CTX, None)]
                    u["v"] = [qkv[:, s, vcol] for s in range(TX, T)]
                    u["n"] = CTX
                    if t < TX:
                        s0, s1 = max(0, t - 1), min(TX - 1, t + 1)
                        u["keys"].append((512, kta[rows, s0 * P:(s1 + 1) * P]))
                        for s in range(s0, s1 + 1):
                            bias = cst(at1, "upper") if s < t else cst(at1, "lower") if s > t else None
                            u["evac"].append((512 + (s - s0) * P, u["n"], P, bias))
                            u["v"].append(qkv[:, s, vcol])
                            u["n"] += P
                    units.append(u)
            biases = {}
            for h in range(B_HEADS):
                j, p0 = h // 2, 64 * (h % 2)
                rows = slice(p0, p0 + 64)
                for t in range(nt):
                    vcol = slice(1280 + h * HD, 1280 + (h + 1) * HD)
                    u = dict(q=qtb[rows, j, t * P:(t + 1) * P], out=mix[:, t, 512 + h * HD:512 + (h + 1) * HD])
                    if t < TX:
                        u["keys"] = [(0, ktb[rows, j, 0:SEQ]), (512, ktb[rows, j, SEQ:SEQ + CTX])]
                        u["evac"] = [(0, 0, SEQ, True), (512, SEQ, CTX, None)]
                        u["v"] = [qkv[:, s, vcol] for s in range(T)]
                        u["n"] = SEQ + CTX
                        biases[len(units)] = [
                            bass.AP(bias_rows.tensor, bias_rows[l].offset + h * RB_R * RB_C + (7 - r) * RB_C + RB_C // 2,
                                    [[B_HEADS * RB_R * RB_C - 1, 64], [RB_C, ROWS], [1, GRID]])
                            for r in (2 * t, 2 * t + 1)]
                    else:
                        u["keys"] = [(0, ktb[rows, j, SEQ:SEQ + CTX])]
                        u["evac"] = [(0, 0, CTX, None)]
                        u["v"] = [qkv[:, s, vcol] for s in range(TX, T)]
                        u["n"] = CTX
                    units.append(u)
            attend(units, RING0 + 9 * 768, at1, biases)
            PAD = 4 * HALF + SEQ + CTX
            padded = mem(RING0, 2, PAD)
            y = mem(RING0 + 2 * PAD, 2, PAD)
            wcol, bcol = mem(RING0 + 4 * PAD, 2, TAPS), mem(RING0 + 4 * PAD + 64, 2)
            convolve(l, glu, padded, y, wcol, bcol, nt)
            cg, cb = mem(RING0 + 4 * PAD + 128, C_CH), mem(RING0 + 4 * PAD + 128 + C_CH, C_CH)
            load([(cg, t_in["conv_ln_g"][l].partition_broadcast(P)), (cb, t_in["conv_ln_b"][l].partition_broadcast(P))], "conv_ln_in")
            groups = []
            for t in range(nt):
                a = t * P if t < TX else SEQ + 2 * HALF + (t - TX) * P
                groups.append(dict(mm=[(c * P, y[:, c, a:a + P], None) for c in range(2)],
                                   out=out("copy", (0, P, 0, C_CH, mix[:, t, 768:1024]))))
            products(groups)
            rows = [(mix[:, t, 768:1024], mix[:, t, 768:1024]) for t in range(nt)]
            normalise(rows, LN_EPS, post=[(cg, cb)] * nt, width=C_CH)
            silu_rows(rows)
            if finish_debug(f"mix{l}", mix[:, 0:nt, :]):
                return
            mixt = mem(RING0, KD, 768)
            groups = []
            for k in range(KD):
                for c0, c1_ in ((0, TX), (TX, T))[:1 if last else 2]:
                    groups.append(dict(mm=[((t - c0) * P, mix[:, t, k * P:(k + 1) * P], None) for t in range(c0, c1_)],
                                       out=out("copy", (0, P, 0, (c1_ - c0) * P, mixt[:, k, c0 * P:c1_ * P]))))
            products(groups)
            groups = []
            for t in range(nt):
                for n in range(2):
                    groups.append(dict(mm=[(0, mixt[:, k, t * P:(t + 1) * P], wo[:, k, n * 512:(n + 1) * 512]) for k in range(KD)],
                                       out=out("copy", (0, P, 0, 512, mix[:, t, n * 512:(n + 1) * 512]))))
            gtile = [mem(RING0 + 7 * K1 + K1 * i, D) for i in range(2)]
            gain, shift_ = mem(RING0 + 9 * K1, D), mem(RING0 + 10 * K1, D)
            wr = small[:, 576:704].rearrange("p (k e) -> p k e", e=E)
            products(groups)
            load([(gtile[s], mod_rows[s, 0].partition_broadcast(P)) for s in range(2)]
                 + [(gain, t_in["ln1_g"][l].partition_broadcast(P)), (shift_, t_in["ln1_b"][l].partition_broadcast(P)),
                    (wr, t_in["w_router"][l].rearrange("(k p) e -> p k e", p=P))], "gates_in")
            gate_rows([(res[:, t, :], mix[:, t, :], gtile[0 if t < TX else 1]) for t in range(nt)], ALPHA)
            normalise([(res[:, t, :], res[:, t, :]) for t in range(nt)], LN_EPS, post=[(gain, shift_)] * nt)
            if finish_debug(f"res1_{l}", res[:, 0:nt, :]):
                return
            normalise([(res[:, t, :], lnx[:, t, :]) for t in range(nt)], LN_EPS)
            turn_rows(lnx, lambda s, k: m3[:, 32 + k, s:s + 1], lambda s, k: m3[:, 24 + k, s:s + 1], nt)
            X0 = EXTRA0
            aff, pos = mem(X0, T, E), mem(X0 + T * E, T, E)
            msk, logit = mem(X0 + 2 * T * E, T, E), mem(X0 + 3 * T * E, T, E)
            af = small[:, 16:24]
            at_ = mem(X0 + 4 * T * E, 768, parts=E)
            work = mem(X0 + 4 * T * E + 768, nt * P, parts=E)
            best = small[0:E, 0:8]
            route(l, nt, wr, logit, aff, pos, msk, af, at_, work, best)
            if finish_debug(f"pos{l}", pos[:, 0:nt, :]):
                return
            acc = mem(HT0, T, D)
            experts(l, nt, aff, pos, acc, X0 + 2 * T * E)
            if finish_debug(f"moe{l}", acc[:, 0:nt, :]):
                return
            load([(gtile[s], mod_rows[s, 1].partition_broadcast(P)) for s in range(2)]
                 + [(gain, t_in["ln2_g"][l].partition_broadcast(P)), (shift_, t_in["ln2_b"][l].partition_broadcast(P))], "gates_in")
            gate_rows([(res[:, t, :], acc[:, t, :], gtile[0 if t < TX else 1]) for t in range(nt)], ALPHA)
            normalise([(res[:, t, :], res[:, t, :]) for t in range(nt)], LN_EPS, post=[(gain, shift_)] * nt)
            if finish_debug(f"res2_{l}", res[:, 0:nt, :]):
                return
        sparse_attention_block()


_INPUTS = ["x", "c", "ctx", "c_ctx", "w_mod", "b_mod", "w_in", "a_sink", "nat_bias", "conv_w", "conv_b", "conv_ln_g",
           "conv_ln_b", "w_out", "ln1_g", "ln1_b", "w_router", "w_gate", "w_up", "w_down", "ln2_g", "ln2_b", "ln1_w_2",
           "w_in_2", "q_norm_w_2", "k_norm_w_2", "cmp_pe_k_2", "cmp_pe_v_2", "cmp_wk1_2", "cmp_wk2_2", "cmp_wv1_2",
           "cmp_wv2_2", "ret_norm_w_2", "w_out_2", "ln2_w_2", "w_up_2", "w_down_2"]


def extra_layout(inputs):
    def cols(a):
        a = np.asarray(a)
        a = a.reshape(a.shape[:-1] + (a.shape[-1] // P, P))
        return np.ascontiguousarray(np.swapaxes(a, -1, -2))

    cond = np.stack([cols(inputs["c"][0]), cols(inputs["c_ctx"])], -1).reshape(P, 2 * KD)
    taps = np.asarray(inputs["conv_w"]).transpose(0, 2, 1).reshape(LAYERS, 2, P, TAPS).transpose(0, 2, 1, 3)
    return {"cond_cols": cond, "b_mod_cols": cols(inputs["b_mod"]),
            "ln1_w_cols": cols(inputs["ln1_w_2"]), "ln2_w_cols": cols(inputs["ln2_w_2"]),
            "cmp_pe_k_cols": cols(np.asarray(inputs["cmp_pe_k_2"]).reshape(1, -1)),
            "cmp_pe_v_cols": cols(np.asarray(inputs["cmp_pe_v_2"]).reshape(1, -1)),
            "conv_w_cols": np.ascontiguousarray(taps), "conv_b_cols": cols(inputs["conv_b"])}


def kernel(**inputs):
    import concourse.bacc as bacc
    from concourse.bass_utils import run_bass_kernel_spmd

    nc = bacc.Bacc("TRN2", target_bir_lowering=False, num_devices=1)
    (c1, _), (c2, _) = shape_constants()
    arrays = {name: np.ascontiguousarray(inputs[name]) for name in _INPUTS}
    arrays |= {"consts1": c1, "consts2": c2} | extra_layout(inputs)
    t_in = {name: nc.dram_tensor(f"in_{name}", a.shape, mybir.dt.from_np(a.dtype), kind="ExternalInput").ap()
            for name, a in arrays.items()}
    out = nc.dram_tensor("out", [1, SEQ, D], F32, kind="ExternalOutput").ap()
    build(nc, t_in, out)
    r = run_bass_kernel_spmd(nc, [{f"in_{name}": a for name, a in arrays.items()}], core_ids=[0])
    return r.results[0]["out"]
```

```python
from contextlib import ExitStack

import numpy as np

import concourse.bass as bass
from concourse import mybir
from concourse.alu_op_type import AluOpType as ALU

F32 = mybir.dt.float32
ACT = mybir.ActivationFunctionType
AX = mybir.AxisListType

P = 128
D = 1024
KD = D // P
SEQ, CTX = 512, 256
TX, TC = SEQ // P, CTX // P
T = TX + TC
LAYERS = 2
HD = 64
SCALE = HD ** -0.5
NEG = -1e30
A_HEADS, A_KV = 8, 2
A_GROUP = A_HEADS // A_KV
B_HEADS = 4
GRID = 64
ROWS = SEQ // GRID
RB_R, RB_C = 15, 31
C_CH, TAPS = 256, 31
HALF = TAPS // 2
IN_W = 2048
QKV_W = IN_W - 2 * C_CH
E = 16
CAP_X, CAP_C = 2 * SEQ // E, 2 * CTX // E
ALPHA = (2 * LAYERS) ** 0.25
LN_EPS = 1e-6
IN2_W = 2840
FF2 = 4096
N_CMP = (SEQ - 32) // 16 + 1
CMP_HID = 256
K1 = 1024
BIASED = 0.3


def shape_constants():
    q = np.arange(P)[:, None]
    k = np.arange(P)[None, :]
    eye = np.eye(P)
    lower = np.where(k <= q, 0.0, NEG)
    upper = np.where(k >= q, 0.0, NEG)
    above = np.where(k > q, 0.0, NEG)
    pos = np.arange(SEQ, dtype=np.float32)

    def tile(a):
        return a.reshape(TX, P, HD).transpose(1, 0, 2).reshape(P, TX * HD)

    inv = (10000.0 ** (-np.arange(16, dtype=np.float32) / np.float32(16))).astype(np.float32)
    ar = (pos // GRID)[:, None].astype(np.float32) * inv
    ac = (pos % GRID)[:, None].astype(np.float32) * inv
    cos1 = np.concatenate([np.cos(ar), np.cos(ar), np.cos(ac), np.cos(ac)], 1)
    sin1 = np.concatenate([-np.sin(ar), np.sin(ar), -np.sin(ac), np.sin(ac)], 1)
    inv = (10000.0 ** (-np.arange(32, dtype=np.float32) / np.float32(32))).astype(np.float32)
    an = pos[:, None] * inv
    cos2 = np.concatenate([np.cos(an), np.cos(an)], 1)
    sin2 = np.concatenate([-np.sin(an), np.sin(an)], 1)

    c = np.arange(P) % GRID
    start = np.clip(c - 8, 0, GRID - 16)[:, None]
    kc = np.arange(GRID)[None, :]
    near = np.where((kc >= start) & (kc < start + 16), 0.0, NEG)
    slots = np.broadcast_to(np.arange(64)[None, :], (P, 64))
    tri = np.where(q <= k, 1.0, 0.0)
    pick2 = (q % 32 == np.arange(2)[None, :]) * 1.0
    first = dict(ident=eye, lower=lower, upper=upper, near=near, slots=slots, tri=tri, pick2=pick2,
                 ones=np.ones((P, P)), cos=tile(cos1), sin=tile(sin1))

    cend = np.arange(32) * 16 + 31
    seen = np.zeros((P, TX, 32))
    some = np.zeros((P, TX))
    for t in range(TX):
        at = t * P + np.arange(P)
        seen[:, t] = np.where(cend[None, :] <= at[:, None], 0.0, NEG)
        some[:, t] = at >= 31
    lg = np.log(1.0 - 2.0 ** (-5.0 - np.arange(4)))
    decay = np.zeros((P, 4, P))
    for h in range(4):
        decay[:, h] = np.where(q <= k, np.exp(lg[h] * np.maximum(k - q, 0)), 0.0)
    i = np.arange(P)[:, None]
    xi = np.exp(lg[None, :] * (i + 1))
    zeta = np.exp(lg[None, :] * (P - 1 - i)) * SCALE
    gc = np.broadcast_to(np.exp(lg * P)[None, :], (P, 4))
    second = dict(ident=eye, lower=lower, above=above, seen=seen.reshape(P, -1), some=some,
                  decay=decay.reshape(P, -1), xi=xi, zeta=zeta, gc=gc,
                  cos=tile(cos2), sin=tile(sin2))

    def pack(parts):
        at, where = 0, {}
        for name, a in parts.items():
            where[name] = (at, at + a.shape[1])
            at += a.shape[1]
        return np.concatenate([np.asarray(a, np.float32) for a in parts.values()], 1), where

    return pack(first), pack(second)


def build(nc, t_in, out_ap, debug=None):
    (c1, at1), (c2, at2) = shape_constants()
    NC = max(c1.shape[1], c2.shape[1])
    ctx = ExitStack()

    def sb(name, n):
        return ctx.enter_context(nc.sbuf_tensor(name, [P, n], F32))

    arena = sb("arena", 49 * K1 + 512)
    at = [0]

    def region(n):
        a = at[0]
        at[0] += n
        return a

    RES0, HT0, LNX0 = region(6 * K1), region(6 * K1), region(6 * K1)
    EXTRA0 = region(7 * K1 + 512)
    RING0 = region(24 * K1)

    def mem(start, *dims, parts=P, p0=0):
        n = int(np.prod(dims))
        v = arena[p0:p0 + parts, start:start + n]
        if len(dims) == 2:
            v = v.rearrange("p (a b) -> p a b", b=dims[1])
        if len(dims) == 3:
            v = v.rearrange("p (a b c) -> p a b c", b=dims[1], c=dims[2])
        return v

    consts = sb("consts", NC)
    small = sb("small", 704)
    mod = sb("mod", 96)
    res = mem(RES0, T, D)
    ht = mem(HT0, KD, SEQ + CTX)
    lnx = mem(LNX0, T, D)

    pair = [ctx.enter_context(nc.psum_tensor(f"pair{i}", [P, 1024], F32))[:, :] for i in range(4)]
    bank = [pair[i // 2][:, (i % 2) * 512:(i % 2) * 512 + 512] for i in range(8)]

    mod_rows = nc.dram_tensor("mod_rows", [2, 2, D], F32, kind="Internal").ap()
    bias_rows = nc.dram_tensor("bias_rows", [LAYERS, 64 * B_HEADS * RB_R * RB_C], F32, kind="Internal").ap()

    class Signal:
        def __init__(self, name):
            self.sem = ctx.enter_context(nc.semaphore(name))
            self.base = 0

        def upto(self, i, each=1):
            return self.base + (i + 1) * each

        def advance(self, total):
            self.base += total

    known = {}

    def signal(name):
        if name not in known:
            known[name] = Signal(name)
        return known[name]

    class Chain:

        def __init__(self, eng, name):
            self.eng, self.s = eng, signal(name)

        def link(self, ins):
            self.s.advance(1)
            ins.then_inc(self.s.sem, 1)
            self.eng.wait_ge(self.s.sem, self.s.base)

    def cst(where, name):
        a, b = where[name]
        return consts[:, a:b]

    def load(pairs, name):
        s = signal(name)
        with nc.Block() as block:
            @block.sync
            def _(sp):
                for dst, src in pairs:
                    sp.dma_start(dst, src).then_inc(s.sem, 16)
                sp.wait_ge(s.sem, s.upto(len(pairs) - 1, 16))
        s.advance(16 * len(pairs))

    class Ahead:

        def __init__(self, pairs, name):
            self.s, self.n = signal(name), len(pairs)
            with nc.Block() as block:
                @block.sync
                def _(sp):
                    for dst, src in pairs:
                        sp.dma_start(dst, src).then_inc(self.s.sem, 16)

        def wait(self, eng):
            eng.wait_ge(self.s.sem, self.s.upto(self.n - 1, 16))

        def wait_now(self):
            with nc.Block() as block:
                @block.sync
                def _(sp):
                    self.wait(sp)
            self.done()

        def done(self):
            self.s.advance(16 * self.n)

    def products(groups, loads=(), ahead=()):
        full, taken, landed = signal("bank_full"), signal("bank_taken"), [signal(f"landed{i}") for i in range(8)]
        takers = [g % 2 for g in range(len(groups))]
        base_landed = [s.base for s in landed]

        def value(n):
            return base_landed[n % 8] + 16 * len(range(n % 8, n + 1, 8)) - 16 * len(range(n % 8, len(ahead), 8))

        counts = {0: [], 1: []}
        for g in range(len(groups)):
            counts[g % 2].append(g)
        taken = [signal("bank_taken_act"), signal("bank_taken_dve")]

        with nc.Block() as block:
            @block.sync
            def _(sp):
                for n, (dst, src, after) in enumerate(loads, len(ahead)):
                    if after > 0:
                        sp.wait_ge(full.sem, full.upto(after - 1))
                    sp.dma_start(dst, src).then_inc(landed[n % 8].sem, 16)

            @block.tensor
            def _(pe):
                seen = 0
                for g, group in enumerate(groups):
                    for n in range(seen, group.get("need", 0)):
                        if n < len(ahead):
                            ahead[n].wait(pe)
                        else:
                            pe.wait_ge(landed[n % 8].sem, value(n))
                    seen = max(seen, group.get("need", 0))
                    if g >= 8:
                        pe.wait_ge(taken[g % 2].sem, taken[g % 2].upto((g - 8) // 2))
                    ps = bank[g % 8]
                    mm = group["mm"]
                    for i, (col, lhs, rhs) in enumerate(mm):
                        p0 = group.get("p0", 0)
                        if rhs is None:
                            k, m = lhs.shape[0], lhs.shape[-1]
                            ins = nc.tensor.transpose(ps[0:m, col:col + k], lhs, cst(at1, "ident")[0:k, 0:k])
                        else:
                            m = lhs.shape[-1]
                            n = int(np.prod(rhs.shape[1:]))
                            o = ps[p0:p0 + m, col:col + n]
                            if len(rhs.shape) == 3:
                                o = o.rearrange("p (a b) -> p a b", b=rhs.shape[2])
                            ins = nc.tensor.matmul(
                                o, lhsT=lhs, rhs=rhs,
                                start=i == 0 or mm[i - 1][0] != col,
                                stop=i == len(mm) - 1 or mm[i + 1][0] != col)
                    ins.then_inc(full.sem, 1)

            @block.scalar
            def _(act):
                chain = Chain(act, "act_chain")
                for i, g in enumerate(counts[0]):
                    act.wait_ge(full.sem, full.upto(g))
                    o = groups[g]["out"]
                    for j, (psv, dst, *more) in enumerate(o["parts"](bank[g % 8])):
                        if o["kind"] == "copy":
                            ins = nc.scalar.activation(dst, psv, ACT.Copy)
                        elif o["kind"] == "affine":
                            ins = nc.scalar.activation(dst, psv, ACT.Identity, bias=more[1], scale=more[0])
                        elif o["kind"] == "scale":
                            ins = nc.scalar.activation(dst, psv, ACT.Copy, scale=more[0])
                        elif o["kind"] == "relu2":
                            chain.link(nc.scalar.activation(dst, psv, ACT.Relu))
                            ins = nc.scalar.activation(dst, dst, ACT.Square)
                    ins.then_inc(taken[0].sem, 1)

            @block.vector
            def _(dve):
                chain = Chain(dve, "dve_chain")
                for i, g in enumerate(counts[1]):
                    dve.wait_ge(full.sem, full.upto(g))
                    o = groups[g]["out"]
                    for j, (psv, dst, *more) in enumerate(o["parts"](bank[g % 8])):
                        if o["kind"] == "copy":
                            ins = nc.vector.tensor_copy(dst, psv)
                        elif o["kind"] == "affine":
                            ins = nc.vector.tensor_scalar(dst, psv, more[0], more[1], ALU.mult, ALU.add)
                        elif o["kind"] == "scale":
                            ins = nc.vector.tensor_scalar(dst, psv, more[0], None, ALU.mult)
                        elif o["kind"] == "relu2":
                            chain.link(nc.vector.tensor_scalar(dst, psv, 0.0, None, ALU.max))
                            ins = nc.vector.tensor_tensor(dst, dst, dst, ALU.mult)
                    ins.then_inc(taken[1].sem, 1)
        full.advance(len(groups))
        taken[0].advance(len(counts[0]))
        taken[1].advance(len(counts[1]))
        for a in ahead:
            a.done()
        for n in range(len(ahead), len(ahead) + len(loads)):
            landed[n % 8].advance(16)

    def out(kind, *parts):
        def views(ps):
            for (r0, r1, c0, c1, dst, *more) in parts:
                v = ps[r0:r1, c0:c1]
                if len(dst.shape) == 3:
                    v = v.rearrange("p (a b) -> p a b", b=dst.shape[2])
                yield (v, dst, *more)
        return dict(kind=kind, parts=views)

    def row_stats(n, halves):
        return small[:, 0:n * halves * 6].rearrange("p (n k) -> p n k", k=6 * halves)

    def normalise(rows, eps, **more):
        vector, scalar, gpsimd, finish = normalise_parts(rows, eps, **more)
        with nc.Block() as block:
            block.vector(vector)
            block.scalar(scalar)
            block.gpsimd(gpsimd)
        finish()

    def normalise_parts(rows, eps, post=(), mean=True, width=D, ahead=None, counted=False, beside=False, loaded=None):
        n = len(rows)
        halves = (width + 511) // 512
        hw = width // halves
        stats = row_stats(n, halves)
        mv0, ve0, each = (288, 352, 32) if not beside else (584, 600, 8)
        if beside:
            stats = small[:, 512:512 + 12 * n].rearrange("p (n k) -> p n k", k=12)
        mv = small[:, mv0:mv0 + 2 * n].rearrange("p (n k) -> p n k", k=2)
        ve, sd, rs, nb = (small[:, ve0 + each * i:ve0 + each * i + n] for i in range(4))
        v_ready, v_root, scales, applied, gained, finished = (signal(x) for x in (
            "var_ready", "root_ready", "row_scales", "row_normal", "row_gained", "row_finished"))
        on_act = [i for i in range(n) if post or i % 2 == 0]
        on_pool = [i for i in range(n) if post and i % 3 < 2]
        def vector(dve):
            chain = Chain(dve, "dve_chain")
            if loaded:
                loaded.wait(dve)
            if not counted:
                for i, (src, _) in enumerate(rows):
                    for h in range(halves):
                        ins = nc.vector.bn_stats(stats[:, i, 6 * h:6 * h + 6], src[:, h * hw:(h + 1) * hw])
                chain.link(ins)
            for i in range(n):
                ins = nc.vector.bn_aggr(mv[:, i, :], stats[:, i, :])
            chain.link(ins)
            if mean:
                nc.vector.tensor_scalar(ve, mv[:, :, 1], eps, None, ALU.add).then_inc(v_ready.sem, 1)
            else:
                chain.link(nc.vector.tensor_tensor(ve, mv[:, :, 0], mv[:, :, 0], ALU.mult))
                nc.vector.scalar_tensor_tensor(ve, ve, eps, mv[:, :, 1], ALU.add, ALU.add).then_inc(v_ready.sem, 1)
            dve.wait_ge(v_root.sem, v_root.upto(0))
            ins = nc.vector.reciprocal(rs, sd)
            if mean:
                chain.link(ins)
                ins = nc.vector.scalar_tensor_tensor(nb, mv[:, :, 0], -1.0, rs, ALU.mult, ALU.mult)
            ins.then_inc(scales.sem, 1)
            dve.wait_ge(scales.sem, scales.upto(0))
            if post and ahead:
                ahead.wait(dve)
            for i, (src, dst) in enumerate(rows):
                if post:
                    dve.wait_ge(applied.sem, applied.upto(i))
                    ins = nc.vector.tensor_tensor(dst, dst, post[i][0], ALU.mult)
                    if i in on_pool:
                        ins.then_inc(gained.sem, 1)
                    else:
                        chain.link(ins)
                        nc.vector.tensor_tensor(dst, dst, post[i][1], ALU.add).then_inc(finished.sem, 1)
                elif i not in on_act:
                    if mean:
                        ins = nc.vector.tensor_scalar(dst, src, mv[:, i, 0:1], rs[:, i:i + 1], ALU.subtract, ALU.mult)
                    else:
                        ins = nc.vector.tensor_scalar(dst, src, rs[:, i:i + 1], None, ALU.mult)
                    ins.then_inc(finished.sem, 1)

        def scalar(act):
            act.wait_ge(v_ready.sem, v_ready.upto(0))
            nc.scalar.activation(sd, ve, ACT.Sqrt).then_inc(v_root.sem, 1)
            act.wait_ge(scales.sem, scales.upto(0))
            for i in on_act:
                src, dst = rows[i]
                if mean:
                    ins = nc.scalar.activation(dst, src, ACT.Identity, bias=nb[:, i:i + 1], scale=rs[:, i:i + 1])
                else:
                    ins = nc.scalar.activation(dst, src, ACT.Copy, scale=rs[:, i:i + 1])
                ins.then_inc(applied.sem, 1)

        def gpsimd(pool):
            if on_pool and ahead:
                ahead.wait(pool)
            for k, i in enumerate(on_pool):
                pool.wait_ge(gained.sem, gained.upto(k))
                nc.gpsimd.tensor_tensor(rows[i][1], rows[i][1], post[i][1], ALU.add).then_inc(finished.sem, 1)
        def finish():
            for x in (v_ready, v_root, scales):
                x.advance(1)
            applied.advance(len(on_act))
            gained.advance(len(on_pool))
            finished.advance(n if post else n - len(on_act))
            if ahead:
                ahead.done()

        return vector, scalar, gpsimd, finish

    def turn_rows(src, scale, shift, chunks, ahead=None):
        groups = []
        for k in range(KD):
            for stream, (t0, t1) in enumerate(((0, TX), (TX, T))):
                if t0 >= chunks:
                    continue
                mm = [((t - t0) * P, src[:, t, k * P:(k + 1) * P], None) for t in range(t0, t1)]
                n = (t1 - t0) * P
                dst = ht[:, k, t0 * P:t1 * P]
                if shift is None:
                    o = out("scale", (0, P, 0, n, dst, scale(stream, k)))
                else:
                    o = out("affine", (0, P, 0, n, dst, scale(stream, k), shift(stream, k)))
                groups.append(dict(mm=mm, out=o, need=1 if ahead else 0))
        products(groups, ahead=[ahead] if ahead else ())

    def rotate(jobs, where, seg):
        done, half_done = signal("rotated"), signal("swapped")
        tmp = mem(RING0 + 23 * K1, 2, 512)
        with nc.Block() as block:
            @block.gpsimd
            def _(pool):
                for i, (src, dst, t, heads) in enumerate(jobs):
                    if i >= 2:
                        pool.wait_ge(done.sem, done.upto(i - 2))
                    cosv = cst(where, "cos")[:, t * HD:(t + 1) * HD].unsqueeze(1).to_broadcast([P, heads, HD])
                    tv = tmp[:, i % 2, 0:heads * HD].rearrange("p (h d) -> p h d", d=HD)
                    nc.gpsimd.tensor_tensor(tv, src, cosv, ALU.mult).then_inc(half_done.sem, 1)

            @block.vector
            def _(dve):
                chain = Chain(dve, "dve_chain")
                for i, (src, dst, t, heads) in enumerate(jobs):
                    for a in range(0, HD, 2 * seg):
                        for s in range(2):
                            o, x = a + s * seg, a + (1 - s) * seg
                            sinv = cst(where, "sin")[:, t * HD + o:t * HD + o + seg].unsqueeze(1).to_broadcast([P, heads, seg])
                            ins = nc.vector.tensor_tensor(dst[:, :, o:o + seg], src[:, :, x:x + seg], sinv, ALU.mult)
                    chain.link(ins)
                    dve.wait_ge(half_done.sem, half_done.upto(i))
                    tv = tmp[:, i % 2, 0:heads * HD].rearrange("p (h d) -> p h d", d=HD)
                    nc.vector.tensor_tensor(dst, dst, tv, ALU.add).then_inc(done.sem, 1)
        done.advance(len(jobs))
        half_done.advance(len(jobs))

    def attend(units, work, where, biases=(), conv=None):
        n = len(units)
        LT, LV = 2, 3
        sc = mem(work, 3, 768)
        pt = mem(work + 2304, 2, 768)
        bt = mem(work + 3840, 2, 512)
        tapped, summed = signal("tap_product"), signal("tap_added")
        taps = [(j, c) for j in range(TAPS) for c in range(2)] if conv else []
        weight = np.cumsum([0] + [u["n"] * (BIASED if i in biases else 1) for i, u in enumerate(units)])
        cut = [int(len(taps) * w / weight[-1]) for w in weight]
        share = [range(cut[i], cut[i + 1]) for i in range(n)]
        turn_banks = 2 if max(u["n"] for u in units) <= 512 else 1
        nm = small[:, 4:8]
        rs = small[:, 8:12]
        es = small[:, 12:16]
        den = small[:, 16:20]
        rc = small[:, 20:24]
        scored, maxed, probs = signal("scored"), signal("maxed"), signal("probs")
        turned, turned_sb, valued, written = (signal(x) for x in ("turned", "turned_sb", "valued", "written"))
        tile_in, tile_ready = [signal("bias_in0"), signal("bias_in1")], signal("bias_ready")
        kb = {u: i for i, u in enumerate(sorted(biases))} if biases else {}
        order = sorted(kb)
        ident = cst(where, "ident")
        wide = [pair[2], pair[2][:, 512:]] if turn_banks == 2 else [pair[2]] * 2
        po = [pair[3][:, 0:512], pair[3][:, 512:1024]]

        with nc.Block() as block:
            @block.sync
            def _(sp):
                for i, u in enumerate(order):
                    if i >= 2:
                        sp.wait_ge(maxed.sem, maxed.upto(order[i - 2]))
                    for r in range(2):
                        sp.dma_start(bt[64 * r:64 * r + 64, i % 2, :].rearrange("p (a b) -> p a b", b=GRID),
                                     biases[u][r]).then_inc(tile_in[i % 2].sem, 16)

            @block.gpsimd
            def _(pool):
                def tile(i):
                    pool.wait_ge(tile_in[i % 2].sem, tile_in[i % 2].upto(i // 2, 32))
                    tv = bt[:, i % 2, :].rearrange("p (a b) -> p a b", b=GRID)
                    near = cst(where, "near").unsqueeze(1).to_broadcast([P, ROWS, GRID])
                    nc.gpsimd.tensor_tensor(tv, tv, near, ALU.add).then_inc(tile_ready.sem, 1)

                if 0 in kb:
                    tile(0)
                for u in range(n):
                    if u + 1 in kb:
                        tile(kb[u + 1])
                    for k in share[u]:
                        j, c = taps[k]
                        if j > 0:
                            _, y, _, _, span, buf = conv
                            pool.wait_ge(tapped.sem, tapped.upto(k))
                            if k >= 4:
                                pool.wait_ge(summed.sem, summed.upto(k - 4))
                            nc.gpsimd.tensor_tensor(y[:, c, 0:span], y[:, c, 0:span], buf[k % 2][:, 0:span],
                                                    ALU.add).then_inc(summed.sem, 1)

            @block.tensor
            def _(pe):
                for i in range(n + LV):
                    if i < n:
                        if i >= 2:
                            pe.wait_ge(maxed.sem, maxed.upto(i - 2))
                        for col, kT in units[i]["keys"]:
                            m = kT.shape[-1]
                            ins = nc.tensor.matmul(pair[i % 2][:, col:col + m], lhsT=units[i]["q"], rhs=kT,
                                                   start=True, stop=True)
                        ins.then_inc(scored.sem, 1)
                    j = i - LT
                    if 0 <= j < n:
                        pe.wait_ge(probs.sem, probs.upto(j))
                        if j >= turn_banks:
                            pe.wait_ge(turned_sb.sem, turned_sb.upto(j - turn_banks))
                        nk = units[j]["n"]
                        for c in range(0, nk, P):
                            w = min(P, nk - c)
                            ins = nc.tensor.transpose(wide[j % 2][0:w, c:c + P], sc[:, j % 3, c:c + w], ident)
                        ins.then_inc(turned.sem, 1)
                    j = i - LV
                    if 0 <= j < n:
                        pe.wait_ge(turned_sb.sem, turned_sb.upto(j))
                        if j >= 2:
                            pe.wait_ge(written.sem, written.upto(j - 2))
                        v = units[j]["v"]
                        for c, vc in enumerate(v):
                            w = vc.shape[0]
                            ins = nc.tensor.matmul(po[j % 2][:, 0:2 * HD], lhsT=pt[0:w, j % 2, c * P:(c + 1) * P], rhs=vc,
                                                   start=c == 0, stop=c == len(v) - 1)
                        ins.then_inc(valued.sem, 1)

            @block.vector
            def _(dve):
                chain = Chain(dve, "dve_chain")
                for i in range(n + LV):
                    if i < n:
                        u = units[i]
                        dve.wait_ge(scored.sem, scored.upto(i))
                        if i >= 3:
                            dve.wait_ge(turned.sem, turned.upto(i - 3))
                        if i in kb:
                            dve.wait_ge(tile_ready.sem, tile_ready.upto(kb[i]))
                        for pc, c, m, bias in u["evac"]:
                            if bias is None:
                                ins = nc.vector.tensor_copy(sc[:, i % 3, c:c + m], pair[i % 2][:, pc:pc + m])
                            else:
                                if i in kb:
                                    bias = bt[:, kb[i] % 2, :]
                                ins = nc.vector.tensor_tensor(sc[:, i % 3, c:c + m], pair[i % 2][:, pc:pc + m], bias, ALU.add)
                        chain.link(ins)
                        k = i % 4
                        ins = nc.vector.tensor_reduce(nm[:, k:k + 1], sc[:, i % 3, 0:u["n"]], AX.X, ALU.max, negate=True)
                        if u.get("sink") is None:
                            ins.then_inc(maxed.sem, 1)
                        else:
                            chain.link(ins)
                            nc.vector.tensor_scalar(nm[:, k:k + 1], nm[:, k:k + 1], u["nsink"], None, ALU.min).then_inc(maxed.sem, 1)
                    j = i - LV
                    if 0 <= j < n:
                        u = units[j]
                        k = j % 4
                        v0 = u["v0"]
                        dve.wait_ge(valued.sem, valued.upto(j))
                        total = rs[:, k:k + 1]
                        if u.get("sink") is not None:
                            chain.link(nc.vector.tensor_tensor(den[:, k:k + 1], rs[:, k:k + 1], es[:, k:k + 1], ALU.add))
                            total = den[:, k:k + 1]
                        chain.link(nc.vector.reciprocal(rc[:, k:k + 1], total))
                        if u.get("gate") is not None:
                            chain.link(nc.vector.tensor_tensor(rc[:, k:k + 1], rc[:, k:k + 1], u["gate"], ALU.mult))
                        if u.get("add"):
                            ins = nc.vector.scalar_tensor_tensor(u["out"], po[j % 2][:, v0:v0 + HD], rc[:, k:k + 1], u["out"],
                                                                 ALU.mult, ALU.add)
                        else:
                            ins = nc.vector.tensor_scalar(u["out"], po[j % 2][:, v0:v0 + HD], rc[:, k:k + 1], None, ALU.mult)
                        ins.then_inc(written.sem, 1)

            @block.scalar
            def _(act):
                for i in range(n + LT):
                    j = i - LT
                    if 0 <= j < n:
                        act.wait_ge(turned.sem, turned.upto(j))
                        if j >= 2:
                            act.wait_ge(valued.sem, valued.upto(j - 2))
                        nk = units[j]["n"]
                        cols = (nk + P - 1) // P * P
                        rows = P if nk >= P else nk
                        for c in range(0, cols, 512):
                            m = min(512, cols - c)
                            ins = nc.scalar.activation(pt[0:rows, j % 2, c:c + m], wide[j % 2][0:rows, c:c + m], ACT.Copy)
                        ins.then_inc(turned_sb.sem, 1)
                    if i < n:
                        u = units[i]
                        k = i % 4
                        act.wait_ge(maxed.sem, maxed.upto(i))
                        if i >= 4:
                            act.wait_ge(written.sem, written.upto(i - 4))
                        if u.get("sink") is not None:
                            nc.scalar.activation(es[:, k:k + 1], u["sink"], ACT.Exp, bias=nm[:, k:k + 1])
                        nc.scalar.activation(sc[:, i % 3, 0:u["n"]], sc[:, i % 3, 0:u["n"]], ACT.Exp,
                                             bias=nm[:, k:k + 1], accum_out=rs[:, k:k + 1]).then_inc(probs.sem, 1)
                        for q in share[i]:
                            tj, c = taps[q]
                            padded, y, wcol, bcol, span, buf = conv
                            x = padded[:, c, tj:tj + span]
                            if tj == 0:
                                ins = nc.scalar.activation(y[:, c, 0:span], x, ACT.Identity, bias=bcol[:, c:c + 1], scale=wcol[:, c, 0:1])
                            else:
                                if q >= 4:
                                    act.wait_ge(summed.sem, summed.upto(q - 4))
                                ins = nc.scalar.activation(buf[q % 2][:, 0:span], x, ACT.Copy, scale=wcol[:, c, tj:tj + 1])
                            ins.then_inc(tapped.sem, 1)
        for s in (scored, maxed, probs, turned, turned_sb, valued, written):
            s.advance(n)
        if conv:
            tapped.advance(len(taps))
            summed.advance(len(taps) - 2)
        tile_in[0].advance(32 * ((len(order) + 1) // 2))
        tile_in[1].advance(32 * (len(order) // 2))
        tile_ready.advance(len(order))

    mod_panels = 6

    def adaln_panels(l):
        return ([mem(RING0 + 8 * K1 * i, KD, 1024) for i in range(3)],
                t_in["w_mod"][l].rearrange("(k p) n -> p k n", p=P), [signal(f"panel_in{i}") for i in range(3)])

    cond = small[:, 640:656].rearrange("p (k s) -> p k s", s=2)
    bm = small[:, 656:704]

    def start_adaln(l):
        panel, wm, panel_in = adaln_panels(l)
        with nc.Block() as block:
            @block.sync
            def _(sp):
                sp.dma_start(small[:, 640:656], t_in["cond_cols"]).then_inc(signal("cond_in").sem, 16)
                sp.dma_start(bm, t_in["b_mod_cols"][l]).then_inc(signal("cond_in").sem, 16)
                for m in range(3):
                    sp.dma_start(panel[m], wm[:, :, m * 1024:(m + 1) * 1024]).then_inc(panel_in[m].sem, 16)

    def adaln(l, beside, tables=None):
        wide = small[:, 80:80 + 32 * KD].rearrange("p (k s) -> p k s", s=32)
        gate_rows_sb = small[0:8, 0:512]
        m3 = mod[:, :].rearrange("p (m s) -> p m s", s=2)
        panel, wm, panel_in = adaln_panels(l)
        row = mem(HT0, 2, 1024)
        n_panels = mod_panels
        (cond_in, wide_clear, cond_silu, panel_full, row_sb, cols_full, gates_turned, gates_sb, gates_out) = (
            signal(x) for x in ("cond_in", "wide_clear", "cond_silu", "panel_full", "row_sb", "cols_full",
                                "gates_turned", "gates_sb", "gates_out"))
        cols_taken = signal("cols_taken")
        with nc.Block() as block:
            @block.sync
            def _(sp):
                for m in range(3, n_panels):
                    sp.wait_ge(panel_full.sem, panel_full.upto(m - 3))
                    sp.dma_start(panel[m % 3], wm[:, :, m * 1024:(m + 1) * 1024]).then_inc(panel_in[m % 3].sem, 16)
                sp.wait_ge(gates_sb.sem, gates_sb.upto(0))
                for s in range(2):
                    for g in range(2):
                        sp.dma_start(mod_rows[s, g].rearrange("(k d) -> k d", d=P),
                                     gate_rows_sb[:, (2 * s + g) * P:(2 * s + g + 1) * P]).then_inc(gates_out.sem, 16)
                sp.wait_ge(gates_out.sem, gates_out.upto(3, 16))

            @block.scalar
            def _(act):
                act.wait_ge(cond_in.sem, cond_in.upto(1, 16))
                act.wait_ge(wide_clear.sem, wide_clear.upto(0))
                nc.scalar.activation(wide[:, :, 0:2], cond, ACT.Silu).then_inc(cond_silu.sem, 1)
                beside[1](act)
                for m in range(n_panels):
                    act.wait_ge(panel_full.sem, panel_full.upto(m))
                    if m >= 2:
                        act.wait_ge(cols_full.sem, cols_full.upto(m - 2))
                    nc.scalar.activation(row[:, m % 2, :], pair[m % 2], ACT.Copy).then_inc(row_sb.sem, 1)

            @block.tensor
            def _(pe):
                pe.wait_ge(cond_silu.sem, cond_silu.upto(0))
                if tables:
                    tables.wait(pe)
                for m in range(n_panels):
                    pe.wait_ge(panel_in[m % 3].sem, panel_in[m % 3].upto(m // 3, 16))
                    if m >= 2:
                        pe.wait_ge(row_sb.sem, row_sb.upto(m - 2))
                    for half in range(2):
                        for k in range(KD):
                            p0 = 32 * (k % 4)
                            ins = nc.tensor.matmul(pair[m % 2][p0:p0 + 32, half * 512:(half + 1) * 512], lhsT=wide[:, k, :],
                                                   rhs=panel[m % 3][:, k, half * 512:(half + 1) * 512], start=k < 4, stop=k >= 4)
                    ins.then_inc(panel_full.sem, 1)
                    pe.wait_ge(row_sb.sem, row_sb.upto(m))
                    if m >= 2:
                        pe.wait_ge(cols_taken.sem, cols_taken.upto(m - 2))
                    for j in range(8):
                        ins = nc.tensor.matmul(bank[4 + m % 2][:, 2 * j:2 * j + 2], lhsT=row[:, m % 2, j * P:(j + 1) * P],
                                               rhs=cst(at1, "pick2"), start=True, stop=True)
                    ins.then_inc(cols_full.sem, 1)
                pe.wait_ge(cols_taken.sem, cols_taken.upto(n_panels - 1))
                for s in range(2):
                    for g in range(2):
                        a = 16 + 24 * g
                        ins = nc.tensor.transpose(bank[6][0:8, (2 * s + g) * P:(2 * s + g + 1) * P],
                                                  m3[:, a:a + 8, s], cst(at1, "ident"))
                ins.then_inc(gates_turned.sem, 1)

            @block.vector
            def _(dve):
                nc.vector.memset(wide, 0.0).then_inc(wide_clear.sem, 1)
                beside[0](dve)
                dve.wait_ge(cond_in.sem, cond_in.upto(1, 16))
                for m in range(n_panels):
                    dve.wait_ge(cols_full.sem, cols_full.upto(m))
                    b = bm[:, 8 * m:8 * m + 8].unsqueeze(2).to_broadcast([P, 8, 2])
                    v = bank[4 + m % 2][:, 0:16].rearrange("p (a b) -> p a b", b=2)
                    one = 1.0 if m in (1, 4) else 0.0
                    nc.vector.scalar_tensor_tensor(m3[:, 8 * m:8 * m + 8, :], v, one, b, ALU.add, ALU.add).then_inc(cols_taken.sem, 1)
                dve.wait_ge(gates_turned.sem, gates_turned.upto(0))
                dve.wait_ge(cond_silu.sem, cond_silu.upto(0))
                nc.vector.tensor_copy(gate_rows_sb, bank[6][0:8, :]).then_inc(gates_sb.sem, 1)
        cond_in.advance(32)
        beside[3]()
        if tables:
            tables.done()
        for s in (wide_clear, cond_silu, gates_turned, gates_sb):
            s.advance(1)
        for s in panel_in:
            s.advance(32)
        for s in (panel_full, row_sb, cols_full, cols_taken):
            s.advance(n_panels)
        gates_out.advance(64)

    def glu_pad(glu, padded, chunks):
        width = 2 * HALF + SEQ + (2 * HALF + CTX if chunks > TX else 0)
        cleared, sig, ready = signal("pads_cleared"), signal("gate_sigmoid"), signal("glu_ready")
        with nc.Block() as block:
            @block.gpsimd
            def _(pool):
                nc.gpsimd.memset(padded[:, :, 0:width], 0.0).then_inc(cleared.sem, 1)

            @block.scalar
            def _(act):
                nc.scalar.activation(glu[:, 2:4, 0:chunks * P], glu[:, 2:4, 0:chunks * P], ACT.Sigmoid).then_inc(sig.sem, 1)

            @block.vector
            def _(dve):
                dve.wait_ge(cleared.sem, cleared.upto(0))
                dve.wait_ge(sig.sem, sig.upto(0))
                ins = nc.vector.tensor_tensor(padded[:, :, HALF:HALF + SEQ], glu[:, 0:2, 0:SEQ], glu[:, 2:4, 0:SEQ], ALU.mult)
                if chunks > TX:
                    a = 3 * HALF + SEQ
                    ins = nc.vector.tensor_tensor(padded[:, :, a:a + CTX], glu[:, 0:2, SEQ:], glu[:, 2:4, SEQ:], ALU.mult)
                ins.then_inc(ready.sem, 1)
        cleared.advance(1)
        sig.advance(1)
        ready.advance(1)
        return width - 2 * HALF

    def clear(views):
        s = signal("cleared")
        with nc.Block() as block:
            @block.gpsimd
            def _(pool):
                for v in views[1:]:
                    nc.gpsimd.memset(v, 0.0).then_inc(s.sem, 1)

            @block.vector
            def _(dve):
                nc.vector.memset(views[0], 0.0).then_inc(s.sem, 1)
        s.advance(len(views))

    def silu_rows(rows):
        s = signal("row_silu")
        with nc.Block() as block:
            @block.scalar
            def _(act):
                for dst, src in rows:
                    nc.scalar.activation(dst, src, ACT.Silu).then_inc(s.sem, 1)
        s.advance(len(rows))

    def project_out(chunks, mixt, wo, wo_ahead, gtile=None, gates_ahead=None, tmp=None):
        n = 2 * chunks
        full, taken = signal("bank_full"), signal("gated_taken")
        stats = row_stats(chunks, 2)
        with nc.Block() as block:
            @block.tensor
            def _(pe):
                wo_ahead.wait(pe)
                for g in range(n):
                    t, h = g // 2, g % 2
                    if g >= 8:
                        pe.wait_ge(taken.sem, taken.upto(g - 8))
                    for k in range(KD):
                        ins = nc.tensor.matmul(bank[g % 8], lhsT=mixt[:, k, t * P:(t + 1) * P],
                                               rhs=wo(k, slice(h * 512, (h + 1) * 512)), start=k == 0, stop=k == KD - 1)
                    ins.then_inc(full.sem, 1)

            @block.vector
            def _(dve):
                chain = Chain(dve, "dve_chain")
                if gtile:
                    gates_ahead.wait(dve)
                for g in range(n):
                    t, h = g // 2, g % 2
                    r = res[:, t, h * 512:(h + 1) * 512]
                    dve.wait_ge(full.sem, full.upto(g))
                    if gtile:
                        chain.link(nc.vector.tensor_tensor(tmp[:, g % 2, :], bank[g % 8],
                                                           gtile[0 if t < TX else 1][:, h * 512:(h + 1) * 512], ALU.mult))
                        ins = nc.vector.scalar_tensor_tensor(r, r, ALPHA, tmp[:, g % 2, :], ALU.mult, ALU.add)
                    else:
                        ins = nc.vector.tensor_tensor(r, r, bank[g % 8], ALU.add)
                    ins.then_inc(taken.sem, 1)
                    dve.wait_ge(taken.sem, taken.upto(g))
                    ins = nc.vector.bn_stats(stats[:, t, 6 * h:6 * h + 6], r)
                chain.link(ins)
        full.advance(n)
        taken.advance(n)
        wo_ahead.done()
        if gtile:
            gates_ahead.done()

    def route(l, chunks, wr, logit, aff, pos, msk, af, at_, work, best):
        ntok = chunks * P
        products([dict(mm=[(0, ht[:, k, t * P:(t + 1) * P], wr[:, k, :]) for k in range(KD)],
                       out=out("copy", (0, P, 0, E, logit[:, t, :]))) for t in range(chunks)])
        lg = logit[:, 0:chunks, :]
        a3 = aff[:, 0:chunks, :]
        m1 = af[:, 0:chunks]
        shifted, powered, soft = signal("logits_shifted"), signal("logits_exp"), signal("affinity")
        with nc.Block() as block:
            @block.vector
            def _(dve):
                chain = Chain(dve, "dve_chain")
                chain.link(nc.vector.tensor_reduce(m1, lg, AX.X, ALU.max))
                nc.vector.tensor_tensor(lg, lg, m1.unsqueeze(2).to_broadcast([P, chunks, E]), ALU.subtract).then_inc(shifted.sem, 1)
                dve.wait_ge(powered.sem, powered.upto(0))
                chain.link(nc.vector.tensor_reduce(m1, lg, AX.X, ALU.add))
                chain.link(nc.vector.reciprocal(m1, m1))
                nc.vector.tensor_tensor(a3, lg, m1.unsqueeze(2).to_broadcast([P, chunks, E]), ALU.mult).then_inc(soft.sem, 1)

            @block.scalar
            def _(act):
                act.wait_ge(shifted.sem, shifted.upto(0))
                nc.scalar.activation(lg, lg, ACT.Exp).then_inc(powered.sem, 1)
        shifted.advance(1)
        powered.advance(1)
        soft.advance(1)
        groups = []
        for t0, t1 in ((0, TX), (TX, T))[:1 if chunks == TX else 2]:
            groups.append(dict(mm=[((t - t0) * P, aff[:, t, :], None) for t in range(t0, t1)],
                               out=out("copy", (0, E, 0, (t1 - t0) * P, at_[:, t0 * P:t1 * P]))))
        products(groups)
        picked = signal("picked")
        streams = [(0, SEQ, CAP_X), (SEQ, SEQ + CTX, CAP_C)][:1 if chunks == TX else 2]
        with nc.Block() as block:
            @block.vector
            def _(dve):
                chain = Chain(dve, "dve_chain")
                for a, b, cap in streams:
                    for _ in range(cap // 8):
                        chain.link(nc.vector.max(best, at_[:, a:b]))
                        chain.link(nc.vector.match_replace(at_[:, a:b], best, at_[:, a:b], -1.0))
                nc.vector.tensor_scalar(work, at_[:, 0:ntok], 0.0, None, ALU.is_lt).then_inc(picked.sem, 1)
        picked.advance(1)
        products([dict(mm=[(t * E, work[:, t * P:(t + 1) * P], None) for t in range(chunks)],
                       out=out("copy", (0, P, 0, chunks * E, msk[:, 0:chunks, :])))])
        groups = []
        mm = []
        for t in range(chunks):
            t0 = 0 if t < TX else TX
            for s in range(t0, t + 1):
                mm.append((t * E, cst(at1, "tri" if s == t else "ones"), msk[:, s, :]))
        groups.append(dict(mm=mm, out=out("copy", (0, P, 0, chunks * E, pos[:, 0:chunks, :]))))
        products(groups)
        slot = signal("slots_ready")
        with nc.Block() as block:
            @block.vector
            def _(dve):
                chain = Chain(dve, "dve_chain")
                p3, k3 = pos[:, 0:chunks, :], msk[:, 0:chunks, :]
                chain.link(nc.vector.tensor_tensor(p3, p3, k3, ALU.mult))
                nc.vector.tensor_scalar(p3, p3, -1.0, None, ALU.add).then_inc(slot.sem, 1)
        slot.advance(1)

    def expert_pieces(l):
        piece = [mem(RING0 + 4 * K1 * i, 4, D) for i in range(6)]
        src = [t_in[("w_gate", "w_up", "w_down")[j // 2]][l].rearrange("e (k p) n -> p e k n", p=P)
               [:, :, 4 * (j % 2):4 * (j % 2) + 4, :] for j in range(6)]
        return piece, src, [signal(f"piece_in{j}") for j in range(6)]

    def start_experts(l):
        piece, src, landed = expert_pieces(l)
        with nc.Block() as block:
            @block.sync
            def _(sp):
                for j in range(6):
                    sp.dma_start(piece[j], src[j][:, 0, :, :]).then_inc(landed[j].sem, 16)

    def experts(l, chunks, aff, pos, acc, base, gtile, gates_ahead):
        ctx_too = chunks > TX
        a = base

        def take(*dims):
            nonlocal a
            v = mem(a, *dims)
            a += int(np.prod(dims))
            return v

        raw_x, raw_c = take(512), take(256)
        tok_x, tok_c = take(4, 2, CAP_X), take(2, 4, CAP_C)
        hid_x, hid_c = take(512), take(256)
        turn_x, turn_c = take(4, 2, CAP_X), take(2, 4, CAP_C)
        y_x, y_c = take(D), take(D)
        sel_x, sel_c = take(TX, CAP_X), take(TC, CAP_C)
        gat_x, gat_c = take(TX, P), take(TC, P)
        gt_x, gt_c = take(TX * P), take(TC * P)
        slot_col, aff_col = take(T), take(T)
        assert a <= EXTRA0 + 7 * K1 + 512, a - EXTRA0
        piece, src, landed = expert_pieces(l)
        (used, cols_copied, picks, raw_full, raw_sb, tok_turned, tok_scaled, tok_ready, silu_ready, hid_ready, hid_turned,
         hid_sb, y_sb, gates_ready, gates_turned, gates_sb, spread, added, cleared) = (signal(x) for x in (
             "piece_used", "cols_copied", "picks_ready", "raw_full", "raw_sb", "tok_turned", "tok_scaled", "tok_ready",
             "silu_ready", "hid_ready", "hid_turned", "hid_sb", "y_sb", "gates_ready", "pair_gates_turned",
             "pair_gates_sb", "spread", "added", "sums_cleared"))
        scaled = signal("sums_scaled")
        n_out = 2 * chunks
        m3 = mod[:, :].rearrange("p (m s) -> p m s", s=2)

        def per_feature(m0, s):
            if s == 0:
                v = m3[:, m0:m0 + 8, 0].rearrange("p (h b) -> p b h", b=4)
                return v.unsqueeze(3).to_broadcast([P, 4, 2, CAP_X])
            v = m3[:, m0:m0 + 8, 1].rearrange("p (q b) -> p b q", b=2)
            return v.unsqueeze(3).to_broadcast([P, 2, 4, CAP_C])

        def count(s, turn, each, j):
            i, par = turn
            return i * (2 * each) + (s.base + par * each + j)

        def pair(s, turn, each, j):
            return turn[0] * each + (s.base + j)

        def pairs(eng, prologue, step):
            prologue()
            step((0, 0), True, False)
            step((0, 1), True, False)
            with eng.Fori(1, E // 2 - 1) as i:
                step((i, 0), False, False)
                step((i, 1), False, False)
            step((E // 2 - 1, 0), False, False)
            step((E // 2 - 1, 1), False, True)

        with nc.Block() as block:
            @block.gpsimd
            def _(pool):
                nc.gpsimd.memset(gat_c, 0.0).then_inc(cleared.sem, 1)
                nc.gpsimd.memset(y_c, 0.0).then_inc(cleared.sem, 1)
                for t in range(chunks):
                    nc.gpsimd.tensor_scalar(acc[:, t, :], acc[:, t, :], ALPHA, None, ALU.mult).then_inc(scaled.sem, 1)

            @block.sync
            def _(sp):
                with sp.Fori(0, E - 1) as e:
                    for j in range(6):
                        sp.wait_ge(used.sem, e * 6 + (used.base + j + 1))
                        sp.dma_start(piece[j], src[j][:, bass.ds(e + 1, 1), :, :].rearrange("p o k n -> p (o k) n")).then_inc(landed[j].sem, 16)

            @block.vector
            def _(dve):
                def pick(turn, ahead):
                    i, par = turn
                    e = i * 2 + (par + ahead)
                    nc.vector.tensor_copy(slot_col[:, 0:chunks].unsqueeze(2), pos[:, 0:chunks, bass.ds(e, 1)])
                    nc.vector.tensor_copy(aff_col[:, 0:chunks].unsqueeze(2), aff[:, 0:chunks, bass.ds(e, 1)]).then_inc(cols_copied.sem, 1)
                    dve.wait_ge(cols_copied.sem, count(cols_copied, turn, 1, 1 + ahead))
                    for t in range(chunks):
                        cap, sel = (CAP_X, sel_x[:, t, :]) if t < TX else (CAP_C, sel_c[:, t - TX, :])
                        ins = nc.vector.tensor_scalar(sel, cst(at1, "slots")[:, 0:cap], slot_col[:, t:t + 1], None, ALU.is_equal)
                    ins.then_inc(picks.sem, 1)

                def modulate(turn, ahead):
                    dve.wait_ge(tok_turned.sem, count(tok_turned, turn, 1, 1 + ahead))
                    x4 = bank[4].rearrange("p (b h s) -> p b h s", b=4, h=2)
                    c4 = bank[5][:, 0:256].rearrange("p (b q s) -> p b q s", b=2, q=4)
                    ins = nc.vector.tensor_tensor(tok_x, x4, per_feature(32, 0), ALU.mult)
                    if ctx_too:
                        ins = nc.vector.tensor_tensor(tok_c, c4, per_feature(32, 1), ALU.mult)
                    ins.then_inc(tok_scaled.sem, 1)
                    dve.wait_ge(tok_scaled.sem, count(tok_scaled, turn, 1, 1 + ahead))
                    ins = nc.vector.tensor_tensor(tok_x, tok_x, per_feature(24, 0), ALU.add)
                    if ctx_too:
                        ins = nc.vector.tensor_tensor(tok_c, tok_c, per_feature(24, 1), ALU.add)
                    ins.then_inc(tok_ready.sem, 1)

                def gates(par):
                    for t in range(chunks):
                        cap, gat = (CAP_X, gat_x[:, t, :]) if t < TX else (CAP_C, gat_c[:, t - TX, :])
                        ins = nc.vector.tensor_scalar(gat[:, par * cap:(par + 1) * cap], cst(at1, "slots")[:, 0:cap],
                                                      slot_col[:, t:t + 1], aff_col[:, t:t + 1], ALU.is_equal, ALU.mult)
                    ins.then_inc(gates_ready.sem, 1)

                def prologue():
                    dve.wait_ge(cleared.sem, cleared.upto(1))
                    pick((0, 0), 0)
                    modulate((0, 0), 0)
                    gates(0)

                def step(turn, first, last):
                    i, par = turn
                    if not last:
                        dve.wait_ge(raw_full.sem, count(raw_full, turn, 1, 1))
                        dve.wait_ge(gates_ready.sem, count(gates_ready, turn, 1, 1))
                        pick(turn, 1)
                    dve.wait_ge(silu_ready.sem, count(silu_ready, turn, 1, 1))
                    dve.wait_ge(used.sem, count(used, turn, 6, 4))
                    ins = nc.vector.tensor_tensor(hid_x, hid_x, bank[2], ALU.mult)
                    if ctx_too:
                        ins = nc.vector.tensor_tensor(hid_c, hid_c, bank[3][:, 0:256], ALU.mult)
                    ins.then_inc(hid_ready.sem, 1)
                    if not last:
                        modulate(turn, 1)
                        if par == 1:
                            dve.wait_ge(gates_turned.sem, pair(gates_turned, turn, 1, 1))
                        gates(1 - par)
                    if par == 0 and not first:
                        add_pair(turn)
                    if first and par == 0:
                        gates_ahead.wait(dve)
                    dve.wait_ge(used.sem, count(used, turn, 6, 6))
                    for h in range(2):
                        ins = nc.vector.tensor_tensor(y_x[64 * par:64 * par + 64, h * 512:(h + 1) * 512], bank[6][64 * h:64 * h + 64, :],
                                                      gtile[0][64 * h:64 * h + 64, h * 512:(h + 1) * 512], ALU.mult)
                    if ctx_too:
                        for q in range(4):
                            ins = nc.vector.tensor_tensor(y_c[32 * par:32 * par + 32, q * 256:(q + 1) * 256],
                                                          bank[7][32 * q:32 * q + 32, 0:256],
                                                          gtile[1][32 * q:32 * q + 32, q * 256:(q + 1) * 256], ALU.mult)
                    ins.then_inc(y_sb.sem, 1)
                    if par == 1 and first:
                        dve.wait_ge(scaled.sem, scaled.upto(chunks - 1))

                def add_pair(turn):
                    for n in range(n_out):
                        dve.wait_ge(spread.sem, pair(spread, turn, n_out, n + 1 - n_out))
                        o = acc[:, n // 2, (n % 2) * 512:(n % 2) * 512 + 512]
                        nc.vector.tensor_tensor(o, o, bank[n % 4], ALU.add).then_inc(added.sem, 1)
                    dve.wait_ge(added.sem, pair(added, turn, n_out, 0))

                pairs(dve, prologue, step)
                add_pair((E // 2, 0))

            @block.scalar
            def _(act):
                def copy_raw(turn, ahead):
                    act.wait_ge(raw_full.sem, count(raw_full, turn, 1, 1 + ahead))
                    ins = nc.scalar.activation(raw_x, bank[4], ACT.Copy)
                    if ctx_too:
                        ins = nc.scalar.activation(raw_c, bank[5][:, 0:256], ACT.Copy)
                    ins.then_inc(raw_sb.sem, 1)

                def step(turn, first, last):
                    i, par = turn
                    act.wait_ge(used.sem, count(used, turn, 6, 2))
                    if par or not first:
                        act.wait_ge(hid_turned.sem, count(hid_turned, turn, 1, 0))
                    ins = nc.scalar.activation(hid_x, bank[0], ACT.Silu)
                    if ctx_too:
                        ins = nc.scalar.activation(hid_c, bank[1][:, 0:256], ACT.Silu)
                    ins.then_inc(silu_ready.sem, 1)
                    if not last:
                        act.wait_ge(tok_turned.sem, count(tok_turned, turn, 1, 1))
                        copy_raw(turn, 1)
                    act.wait_ge(hid_turned.sem, count(hid_turned, turn, 1, 1))
                    if par or not first:
                        act.wait_ge(used.sem, count(used, turn, 6, 0))
                    ins = nc.scalar.activation(turn_x.rearrange("p b h s -> p (b h s)"), bank[6], ACT.Copy)
                    if ctx_too:
                        ins = nc.scalar.activation(turn_c.rearrange("p b q s -> p (b q s)"), bank[7][:, 0:256], ACT.Copy)
                    ins.then_inc(hid_sb.sem, 1)
                    if par == 1:
                        act.wait_ge(gates_turned.sem, pair(gates_turned, turn, 1, 1))
                        if not first:
                            act.wait_ge(spread.sem, pair(spread, turn, n_out, 0))
                        ins = nc.scalar.activation(gt_x, bank[0], ACT.Copy)
                        if ctx_too:
                            ins = nc.scalar.activation(gt_c, bank[1][:, 0:256], ACT.Copy)
                        ins.then_inc(gates_sb.sem, 1)

                pairs(act, lambda: copy_raw((0, 0), 0), step)

            @block.tensor
            def _(pe):
                ident = cst(at1, "ident")

                def gather(turn, ahead):
                    pe.wait_ge(picks.sem, count(picks, turn, 1, 1 + ahead))
                    for t in range(TX):
                        for h in range(2):
                            ins = nc.tensor.matmul(bank[4][64 * h:64 * h + 64, :], lhsT=sel_x[:, t, :],
                                                   rhs=lnx[:, t, h * 512:(h + 1) * 512], start=t == 0, stop=t == TX - 1)
                    for t in range(TX, chunks):
                        for q in range(4):
                            ins = nc.tensor.matmul(bank[5][32 * q:32 * q + 32, 0:256], lhsT=sel_c[:, t - TX, :],
                                                   rhs=lnx[:, t, q * 256:(q + 1) * 256], start=t == TX, stop=t == T - 1)
                    ins.then_inc(raw_full.sem, 1)

                def turn_tokens():
                    for b in range(4):
                        ins = nc.tensor.transpose(bank[4][:, b * P:(b + 1) * P], raw_x[:, b * P:(b + 1) * P], ident)
                    if ctx_too:
                        for b in range(2):
                            ins = nc.tensor.transpose(bank[5][:, b * P:(b + 1) * P], raw_c[:, b * P:(b + 1) * P], ident)
                    ins.then_inc(tok_turned.sem, 1)

                def stream(turn, j0, lhs_x, lhs_c, out_x, out_c):
                    for k in range(KD):
                        w = piece[j0 + k // 4]
                        if k % 4 == 0:
                            pe.wait_ge(landed[j0 + k // 4].sem, count(landed[j0 + k // 4], turn, 16, 16))
                        for h in range(2):
                            ins = nc.tensor.matmul(out_x[64 * h:64 * h + 64, :], lhsT=lhs_x[:, k % 4, k // 4, :],
                                                   rhs=w[:, k % 4, h * 512:(h + 1) * 512], start=k == 0, stop=k == KD - 1)
                        if ctx_too:
                            for q in range(4):
                                ins = nc.tensor.matmul(out_c[32 * q:32 * q + 32, 0:256], lhsT=lhs_c[:, k % 2, k // 2, :],
                                                       rhs=w[:, k % 4, q * 256:(q + 1) * 256], start=k == 0, stop=k == KD - 1)
                        if k % 4 == 3:
                            ins.then_inc(used.sem, 1)

                def prologue():
                    gather((0, 0), 0)
                    pe.wait_ge(raw_sb.sem, count(raw_sb, (0, 0), 1, 1))
                    turn_tokens()

                def step(turn, first, last):
                    i, par = turn
                    pe.wait_ge(tok_ready.sem, count(tok_ready, turn, 1, 1))
                    if par or not first:
                        pe.wait_ge(hid_ready.sem, count(hid_ready, turn, 1, 0))
                    if par == 0 and not first:
                        pe.wait_ge(gates_sb.sem, pair(gates_sb, turn, 1, 0))
                    if par == 1 and not first:
                        pe.wait_ge(added.sem, pair(added, turn, n_out, 0))
                    stream(turn, 0, tok_x, tok_c, bank[0], bank[1])
                    stream(turn, 2, tok_x, tok_c, bank[2], bank[3])
                    if not last:
                        gather(turn, 1)
                        if not ctx_too:
                            pe.wait_ge(raw_sb.sem, count(raw_sb, turn, 1, 2))
                            turn_tokens()
                    pe.wait_ge(hid_ready.sem, count(hid_ready, turn, 1, 1))
                    if par or not first:
                        pe.wait_ge(y_sb.sem, count(y_sb, turn, 1, 0))
                    for b in range(4):
                        ins = nc.tensor.transpose(bank[6][:, b * P:(b + 1) * P], hid_x[:, b * P:(b + 1) * P], ident)
                    if ctx_too:
                        for b in range(2):
                            ins = nc.tensor.transpose(bank[7][:, b * P:(b + 1) * P], hid_c[:, b * P:(b + 1) * P], ident)
                    ins.then_inc(hid_turned.sem, 1)
                    if ctx_too and not last:
                        pe.wait_ge(raw_sb.sem, count(raw_sb, turn, 1, 2))
                        turn_tokens()
                    if par == 0 and not first:
                        spread_pair(turn)
                    if par == 1:
                        pe.wait_ge(gates_ready.sem, count(gates_ready, turn, 1, 1))
                        for t in range(chunks):
                            o = bank[0][:, t * P:(t + 1) * P] if t < TX else bank[1][:, (t - TX) * P:(t - TX + 1) * P]
                            ins = nc.tensor.transpose(o, gat_x[:, t, :] if t < TX else gat_c[:, t - TX, :], ident)
                        ins.then_inc(gates_turned.sem, 1)
                    pe.wait_ge(hid_sb.sem, count(hid_sb, turn, 1, 1))
                    stream(turn, 4, turn_x, turn_c, bank[6], bank[7])

                def spread_pair(turn):
                    for n in range(n_out):
                        t, h = n // 2, n % 2
                        if n >= 4:
                            pe.wait_ge(added.sem, pair(added, turn, n_out, n - 3 - n_out))
                        gt, y = (gt_x[:, t * P:(t + 1) * P], y_x) if t < TX else (gt_c[:, (t - TX) * P:(t - TX + 1) * P], y_c)
                        nc.tensor.matmul(bank[n % 4], lhsT=gt, rhs=y[:, h * 512:(h + 1) * 512],
                                         start=True, stop=True).then_inc(spread.sem, 1)

                pairs(pe, prologue, step)
                pe.wait_ge(y_sb.sem, y_sb.upto(E - 1))
                pe.wait_ge(gates_sb.sem, gates_sb.upto(E // 2 - 1))
                spread_pair((E // 2, 0))
        cleared.advance(2)
        scaled.advance(chunks)
        gates_ahead.done()
        for s in landed:
            s.advance(16 * E)
        used.advance(6 * E)
        for s in (cols_copied, picks, raw_full, raw_sb, tok_turned, tok_scaled, tok_ready, silu_ready, hid_ready,
                  hid_turned, hid_sb, y_sb, gates_ready):
            s.advance(E)
        gates_turned.advance(E // 2)
        gates_sb.advance(E // 2)
        spread.advance(n_out * E // 2)
        added.advance(n_out * E // 2)

    def finish_debug(name, v):
        if debug != name:
            return False
        s = signal("debug_out")
        with nc.Block() as block:
            @block.sync
            def _(sp):
                sp.dma_start(out_dbg(v), v).then_inc(s.sem, 16)
                sp.wait_ge(s.sem, s.upto(0, 16))
        s.advance(16)
        return True

    def out_dbg(v):
        return nc.dram_tensor("dbg", list(v.shape), F32, kind="ExternalOutput").ap()

    def head_norms(u2, hx, sq, wt, w_ahead):
        H = A_HEADS + 6
        squared, v_ready, v_root, normed, weighted = (signal(x) for x in (
            "squared", "var_ready", "root_ready", "heads_normed", "heads_weighted"))
        ss, ve, rs = (small[:, 64 * i:64 * i + TX * H].rearrange("p (t h) -> p t h", h=H) for i in range(3))

        def spans(t):
            yield u2[:, t, 0:512], lambda b: b[:, t, 0:8, :].rearrange("p h d -> p (h d)"), (0, 8)
            ks = u2[:, t, 512:1280].rearrange("p (i n) -> p i n", n=256)[:, :, 0:128]
            yield ks, lambda b: b[:, t, 8:14, :].rearrange("p (i g) d -> p i (g d)", g=2), (8, 14)

        with nc.Block() as block:
            @block.scalar
            def _(act):
                for t in range(TX):
                    for x, at_buf, _ in spans(t):
                        nc.scalar.activation(at_buf(sq), x, ACT.Square).then_inc(squared.sem, 1)
                act.wait_ge(v_ready.sem, v_ready.upto(0))
                nc.scalar.activation(ve, ve, ACT.Sqrt).then_inc(v_root.sem, 1)

            @block.vector
            def _(dve):
                chain = Chain(dve, "dve_chain")
                for t in range(TX):
                    dve.wait_ge(squared.sem, squared.upto(2 * t + 1))
                    ins = nc.vector.tensor_reduce(ss[:, t, :], sq[:, t, :, :], AX.X, ALU.add)
                chain.link(ins)
                nc.vector.tensor_scalar(ve, ss, 1.0 / HD, LN_EPS, ALU.mult, ALU.add).then_inc(v_ready.sem, 1)
                dve.wait_ge(v_root.sem, v_root.upto(0))
                chain.link(nc.vector.reciprocal(rs, ve))
                for t in range(TX):
                    for x, at_buf, (h0, h1) in spans(t):
                        x3 = x.rearrange("p (h d) -> p h d", d=HD) if h0 == 0 else x.rearrange("p i (g d) -> p i g d", d=HD)
                        o3 = hx[:, t, h0:h1, :]
                        r3 = rs[:, t, h0:h1].unsqueeze(2).to_broadcast([P, h1 - h0, HD])
                        if h0 == 0:
                            nc.vector.tensor_tensor(o3, x3, r3, ALU.mult).then_inc(normed.sem, 1)
                        else:
                            for i in range(3):
                                ins = nc.vector.tensor_tensor(o3[:, 2 * i:2 * i + 2, :], x3[:, i], r3[:, 2 * i:2 * i + 2, :], ALU.mult)
                            ins.then_inc(normed.sem, 1)

            @block.gpsimd
            def _(pool):
                w_ahead.wait(pool)
                for t in range(TX):
                    pool.wait_ge(normed.sem, normed.upto(2 * t + 1))
                    nc.gpsimd.tensor_tensor(hx[:, t, :, :], hx[:, t, :, :], wt, ALU.mult).then_inc(weighted.sem, 1)
        w_ahead.done()
        squared.advance(2 * TX)
        v_ready.advance(1)
        v_root.advance(1)
        normed.advance(2 * TX)
        weighted.advance(TX)

    def retain(u2, rr, kz, rqt, rkt, it, state, mixb):
        units = [(t, h) for t in range(TX) for h in range(4)]
        n = len(units)
        zetad, inner_full, inner_sb, full, taken = (signal(x) for x in (
            "keys_decayed", "inner_full", "inner_decayed", "unit_full", "unit_taken"))

        def place(h):
            return slice(64 * (h % 2), 64 * (h % 2) + 64), h // 2

        with nc.Block() as block:
            @block.gpsimd
            def _(pool):
                for t, h in units:
                    nc.gpsimd.tensor_scalar(kz[:, t, h, :], rr[:, t, 4 + h, :], cst(at2, "zeta")[:, h:h + 1], None,
                                            ALU.mult).then_inc(zetad.sem, 1)

            @block.tensor
            def _(pe):
                for i in range(n + 1):
                    if i < n:
                        t, h = units[i]
                        rows, j = place(h)
                        if i >= 2:
                            pe.wait_ge(inner_sb.sem, inner_sb.upto(i - 2))
                        cols = slice(t * P, (t + 1) * P)
                        nc.tensor.matmul(bank[i % 2][:, 0:P], lhsT=rkt[rows, j, cols], rhs=rqt[rows, j, cols],
                                         start=True, stop=True).then_inc(inner_full.sem, 1)
                    u = i - 1
                    if u >= 0:
                        t, h = units[u]
                        rows, j = place(h)
                        v = u2[:, t, 1816 + h * P:1816 + (h + 1) * P]
                        pe.wait_ge(inner_sb.sem, inner_sb.upto(u))
                        if u >= 2:
                            pe.wait_ge(taken.sem, taken.upto(u - 2))
                        ins = nc.tensor.matmul(bank[2 + u % 2][:, 0:P], lhsT=it[:, u % 2, :], rhs=v, start=True, stop=True)
                        if t > 0:
                            ins = nc.tensor.matmul(bank[4 + u % 2][:, 0:P], lhsT=rqt[rows, j, t * P:(t + 1) * P],
                                                   rhs=state[rows, j, :], start=True, stop=True)
                        if t < TX - 1:
                            pe.wait_ge(zetad.sem, zetad.upto(u))
                            ins = nc.tensor.matmul(bank[6 + u % 2][rows, 0:P], lhsT=kz[:, t, h, :], rhs=v, start=True, stop=True)
                        ins.then_inc(full.sem, 1)

            @block.vector
            def _(dve):
                chain = Chain(dve, "dve_chain")
                for i in range(n + 1):
                    if i < n:
                        t, h = units[i]
                        dve.wait_ge(inner_full.sem, inner_full.upto(i))
                        if i >= 2:
                            dve.wait_ge(full.sem, full.upto(i - 2))
                        nc.vector.tensor_tensor(it[:, i % 2, :], bank[i % 2][:, 0:P],
                                                cst(at2, "decay")[:, h * P:(h + 1) * P], ALU.mult).then_inc(inner_sb.sem, 1)
                    u = i - 1
                    if u >= 0:
                        t, h = units[u]
                        rows, j = place(h)
                        y = mixb[:, t, 512 + h * P:512 + (h + 1) * P]
                        dve.wait_ge(full.sem, full.upto(u))
                        ins = nc.vector.tensor_copy(y, bank[2 + u % 2][:, 0:P])
                        if t > 0:
                            chain.link(ins)
                            ins = nc.vector.scalar_tensor_tensor(y, bank[4 + u % 2][:, 0:P], cst(at2, "xi")[:, h:h + 1], y,
                                                                 ALU.mult, ALU.add)
                        if t == 0:
                            ins = nc.vector.tensor_copy(state[rows, j, :], bank[6 + u % 2][rows, 0:P])
                        elif t < TX - 1:
                            ins = nc.vector.scalar_tensor_tensor(state[rows, j, :], state[rows, j, :], cst(at2, "gc")[rows, h:h + 1],
                                                                 bank[6 + u % 2][rows, 0:P], ALU.mult, ALU.add)
                        ins.then_inc(taken.sem, 1)
        zetad.advance(n)
        for s in (inner_full, inner_sb, full, taken):
            s.advance(n)

    lncol = small[:, 688:704].rearrange("p (i k) -> p i k", k=KD)
    in2_cuts = [(a, min(a + 512, IN2_W)) for a in range(0, IN2_W, 512)]

    def start_second():
        tables = Ahead([(consts[:, 0:c2.shape[1]], t_in["consts2"]), (lncol[:, 0, :], t_in["ln1_w_cols"][0]),
                        (lncol[:, 1, :], t_in["ln2_w_cols"][0])], "second_in")
        w = mem(RING0, KD, IN2_W)
        w_src = t_in["w_in_2"][0].rearrange("(k p) n -> p k n", p=P)
        return tables, [Ahead([(w[:, :, a:b], w_src[:, :, a:b])], f"w_in{i}") for i, (a, b) in enumerate(in2_cuts)]

    def sparse_attention_block(tables_ahead, w_ahead):
        wt = mem(LNX0 + 12832, A_HEADS + 6, HD)
        qn, kn = t_in["q_norm_w_2"], t_in["k_norm_w_2"]
        head_w_ahead = Ahead([(wt[:, 0:8, :], bass.AP(qn.tensor, qn.offset, [[0, P], [0, 8], [1, HD]]))]
                             + [(wt[:, 8 + 2 * i:10 + 2 * i, :], bass.AP(kn.tensor, kn.offset + i * HD, [[0, P], [0, 2], [1, HD]]))
                                for i in range(3)], "head_w_in")
        normalise([(res[:, t, :], lnx[:, t, :]) for t in range(TX)], LN_EPS, mean=False)
        turn_rows(lnx, lambda s, k: lncol[:, 0, k:k + 1], None, TX, tables_ahead)
        u2 = mem(LNX0, TX, IN2_W)
        w = mem(RING0, KD, IN2_W)
        groups = []
        for i, (a, b) in enumerate(in2_cuts):
            for t in range(TX):
                groups.append(dict(need=i + 1,
                                   mm=[(0, ht[:, k, t * P:(t + 1) * P], w[:, k, a:b]) for k in range(KD)],
                                   out=out("copy", (0, P, 0, b - a, u2[:, t, a:b]))))
        products(groups, ahead=w_ahead)
        H = A_HEADS + 6
        hx = mem(RING0, TX * H, HD).rearrange("p (t h) d -> p t h d", h=H)
        sq = mem(RING0 + 3584, TX * H, HD).rearrange("p (t h) d -> p t h d", h=H)
        qr, kr = mem(RING0 + 7168, TX, 512), mem(RING0 + 9216, TX, 384)
        rr = mem(RING0 + 10752, TX, 512)
        dup = mem(RING0 + 13696, TX, 512)
        w1 = [mem(RES0 + 4 * K1 + 4096 * i, 16, CMP_HID) for i in range(2)]
        w2 = [mem(LNX0 + 11776 + 128 * i, 2, HD) for i in range(2)]
        pe_ = [mem(LNX0 + 12800 + 16 * i, 16) for i in range(2)]
        compress_ahead = Ahead([(pe_[i], t_in[f"cmp_pe_{kind}_cols"][0]) for i, kind in enumerate("kv")]
                               + [(w1[i], t_in[f"cmp_w{kind}1_2"][0].rearrange("(j p) n -> p j n", p=P)) for i, kind in enumerate("kv")]
                               + [(w2[i], t_in[f"cmp_w{kind}2_2"][0].rearrange("(j p) n -> p j n", p=P)) for i, kind in enumerate("kv")],
                               "compress_in")
        head_norms(u2, hx, sq, wt, head_w_ahead)
        jobs = []
        for t in range(TX):
            for g in range(A_KV):
                jobs.append((hx[:, t, 4 * g:4 * g + 4, :], qr[:, t, :].rearrange("p (j g d) -> p g j d", g=A_KV, d=HD)[:, g], t, 4))
            jobs.append((hx[:, t, 8:14, :], kr[:, t, :].rearrange("p (h d) -> p h d", d=HD), t, 6))
            jobs.append((u2[:, t, 1304:1816].rearrange("p (h d) -> p h d", d=HD), rr[:, t, :].rearrange("p (h d) -> p h d", d=HD), t, 8))
        rotate(jobs, at2, 32)
        gts = mem(LNX0 + TX * IN2_W, TX, 24)
        doubled, gated = signal("rows_doubled"), signal("branch_gates")
        with nc.Block() as block:
            @block.scalar
            def _(act):
                nc.scalar.activation(gts, u2[:, :, 1280:1304], ACT.Sigmoid).then_inc(gated.sem, 1)

            @block.vector
            def _(dve):
                for t in range(TX):
                    for i, src in enumerate((kr[:, t, 0:128], u2[:, t, 640:768])):
                        d = dup[:, t, 256 * i:256 * i + 256].rearrange("p (g c d) -> p g c d", g=2, c=2)
                        x = src.rearrange("p (g d) -> p g d", d=HD)
                        for c in range(2):
                            nc.vector.tensor_copy(d[:, :, c, :], x).then_inc(doubled.sem, 1)
                dve.wait_ge(gated.sem, gated.upto(0))
                some = cst(at2, "some").unsqueeze(2).to_broadcast([P, TX, 8])
                nc.vector.tensor_tensor(gts[:, :, 0:8], gts[:, :, 0:8], some, ALU.mult).then_inc(doubled.sem, 1)
        doubled.advance(4 * TX + 1)
        gated.advance(1)
        qt, kst, kwt = mem(RING0 + 15744, 4, SEQ), mem(RING0 + 17792, 2, SEQ), mem(RING0 + 18816, 2, SEQ)
        rqt, rkt = mem(RING0 + 19840, 2, SEQ), mem(RING0 + 20864, 2, SEQ)
        kc2 = mem(RING0 + 21888, 4, SEQ)
        clear([kst, kwt])
        groups = []

        def turn(src, dst, scale=None):
            mm = [(t * P, src(t), None) for t in range(TX)]
            o = out("copy", (0, P, 0, SEQ, dst)) if scale is None else out("scale", (0, P, 0, SEQ, dst, scale))
            groups.append(dict(mm=mm, out=o))

        for j in range(4):
            turn(lambda t: qr[:, t, j * P:(j + 1) * P], qt[:, j, :], SCALE)
        for i, dst in ((1, kst), (2, kwt)):
            groups.append(dict(mm=[(t * P, kr[:, t, i * P:(i + 1) * P], None) for t in range(TX)],
                               out=out("copy", (0, 64, 0, SEQ, dst[0:64, 0, :]), (64, P, 0, SEQ, dst[64:P, 1, :]))))
        for j in range(2):
            turn(lambda t: rr[:, t, j * P:(j + 1) * P], rqt[:, j, :])
            turn(lambda t: rr[:, t, 256 + j * P:256 + (j + 1) * P], rkt[:, j, :], SCALE)
        for i in range(4):
            groups.append(dict(mm=[(t * P, dup[:, t, i * P:(i + 1) * P], None) for t in range(TX)],
                               out=out("copy", (0, 64, 0, SEQ, kc2[0:64, i, :]), (64, P, 1, SEQ, kc2[64:P, i, 0:SEQ - 1]))))
        products(groups)
        win = mem(RING0 + 13696, 32, 64)
        hraw = mem(RING0 + 8480, CMP_HID)
        hc = mem(RING0 + 8740, 2, P)
        kcmp, vcmp = mem(RING0 + 9000, 2, 32), mem(RING0 + 9064, 2 * HD, parts=N_CMP)
        windowed, first_full, hidden, hidden_turned, hidden_sb = (signal(x) for x in (
            "windowed", "first_layer", "hidden_silu", "hidden_turned", "hidden_sb"))
        NW = 2 * N_CMP
        with nc.Block() as block:
            @block.gpsimd
            def _(pool):
                nc.gpsimd.memset(kcmp, 0.0).then_inc(windowed.sem, 1)
                nc.gpsimd.memset(win[:, :, NW:64], 0.0).then_inc(windowed.sem, 1)

            @block.vector
            def _(dve):
                compress_ahead.wait(dve)
                for j in range(16):
                    for i in range(2):
                        x = kc2[:, 2 * i:2 * i + 2, 2 * j:2 * j + 16 * (N_CMP - 1) + 1:16]
                        o = win[:, 2 * j + i, 0:NW].rearrange("p (g n) -> p g n", g=2)
                        ins = nc.vector.tensor_scalar(o, x, pe_[i][:, j:j + 1], None, ALU.add)
                ins.then_inc(windowed.sem, 1)
                dve.wait_ge(hidden_turned.sem, hidden_turned.upto(0))
                nc.vector.tensor_copy(hc, bank[1][:, 0:2 * P].rearrange("p (a b) -> p a b", b=P)).then_inc(hidden_sb.sem, 1)

            @block.tensor
            def _(pe):
                pe.wait_ge(windowed.sem, windowed.upto(2))
                compress_ahead.wait(pe)
                for j in range(16):
                    for i in range(2):
                        ins = nc.tensor.matmul(bank[0][64 * i:64 * i + 64, 0:CMP_HID], lhsT=win[:, 2 * j + i, :],
                                               rhs=w1[i][:, j, :], start=j == 0, stop=j == 15)
                ins.then_inc(first_full.sem, 1)
                pe.wait_ge(hidden.sem, hidden.upto(0))
                for h in range(2):
                    ins = nc.tensor.transpose(bank[1][:, h * P:(h + 1) * P], hraw[:, h * P:(h + 1) * P], cst(at2, "ident"))
                ins.then_inc(hidden_turned.sem, 1)

            @block.scalar
            def _(act):
                act.wait_ge(first_full.sem, first_full.upto(0))
                nc.scalar.activation(hraw, bank[0][:, 0:CMP_HID], ACT.Silu).then_inc(hidden.sem, 1)
        compress_ahead.done()
        windowed.advance(3)
        for s in (first_full, hidden, hidden_turned, hidden_sb):
            s.advance(1)
        groups = []
        for g in range(2):
            cols = slice(g * N_CMP, (g + 1) * N_CMP)
            groups.append(dict(p0=64 * g, mm=[(0, w2[0][:, h, :], hc[:, h, cols]) for h in range(2)],
                               out=out("copy", (64 * g, 64 * g + 64, 0, N_CMP, kcmp[64 * g:64 * g + 64, g, 0:N_CMP]))))
            groups.append(dict(mm=[(0, hc[:, h, 64 + g * N_CMP:64 + (g + 1) * N_CMP], w2[1][:, h, :]) for h in range(2)],
                               out=out("copy", (0, N_CMP, 0, HD, vcmp[:, g * HD:(g + 1) * HD]))))
        products(groups)
        mixb = mem(HT0, TX, D)
        units = []
        for branch in range(3):
            for h in range(A_HEADS):
                g, j = h // 4, h % 4
                for t in range(TX):
                    u = dict(v0=g * HD, q=qt[:, j, t * P:(t + 1) * P], out=mixb[:, t, h * HD:(h + 1) * HD],
                             gate=gts[:, t, branch * 8 + h:branch * 8 + h + 1], add=branch > 0)
                    if branch == 0:
                        seen = cst(at2, "seen")[:, t * 32:t * 32 + N_CMP]
                        u.update(keys=[(0, kcmp[:, g, 0:N_CMP])], evac=[(0, 0, N_CMP, seen)], n=N_CMP, v=[vcmp])
                    else:
                        s0 = 0 if branch == 1 else max(0, t - 2)
                        kT = kst if branch == 1 else kwt
                        m = t - s0
                        vcol = slice(896, 1024) if branch == 1 else slice(1152, 1280)
                        evac = []
                        for s in range(s0, t + 1):
                            bias = cst(at2, "lower") if s == t else cst(at2, "above") if branch == 2 and s == t - 2 else None
                            if bias is None and evac and evac[-1][3] is None:
                                evac[-1] = (evac[-1][0], evac[-1][1], evac[-1][2] + P, None)
                            else:
                                evac.append(((s - s0) * P, (s - s0) * P, P, bias))
                        u.update(keys=[(0, kT[:, g, s0 * P:(t + 1) * P])], evac=evac, n=(t + 1 - s0) * P,
                                 v=[u2[:, s, vcol] for s in range(s0, t + 1)])
                    units.append(u)
        attend(units, RING0, at2)
        rw = mem(LNX0 + 12 * K1, 512)
        wo = [mem(RING0 + 5120, 4, D), mem(RING0 + 12800, 4, D)]
        wo_src = t_in["w_out_2"][0].rearrange("(k p) n -> p k n", p=P)
        ret_w_ahead = Ahead([(rw, t_in["ret_norm_w_2"][0].rearrange("h d -> (h d)").partition_broadcast(P))], "ret_norm_in")
        wo_ahead = Ahead([(wo[i], wo_src[:, 4 * i:4 * i + 4, :]) for i in range(2)], "w_out_in")
        kz = mem(RING0, TX * 4, HD).rearrange("p (t h) d -> p t h d", h=4)
        it, state = mem(RING0 + 1024, 2, P), mem(RING0 + 1280, 2, P)
        retain(u2, rr.rearrange("p t (h d) -> p t h d", d=HD), kz, rqt, rkt, it, state, mixb)
        normalise([(mixb[:, t, 512 + h * P:512 + (h + 1) * P],) * 2 for t in range(TX) for h in range(4)], LN_EPS, width=P)
        weighted, gate_silu, gated = signal("rows_weighted"), signal("ret_gate_silu"), signal("rows_gated")
        with nc.Block() as block:
            @block.gpsimd
            def _(pool):
                ret_w_ahead.wait(pool)
                for t in range(TX):
                    nc.gpsimd.tensor_tensor(mixb[:, t, 512:D], mixb[:, t, 512:D], rw, ALU.mult).then_inc(weighted.sem, 1)

            @block.scalar
            def _(act):
                for t in range(TX):
                    nc.scalar.activation(u2[:, t, 2328:2840], u2[:, t, 2328:2840], ACT.Silu).then_inc(gate_silu.sem, 1)

            @block.vector
            def _(dve):
                for t in range(TX):
                    dve.wait_ge(weighted.sem, weighted.upto(t))
                    dve.wait_ge(gate_silu.sem, gate_silu.upto(t))
                    nc.vector.tensor_tensor(mixb[:, t, 512:D], mixb[:, t, 512:D], u2[:, t, 2328:2840], ALU.mult).then_inc(gated.sem, 1)
        for s in (weighted, gate_silu, gated):
            s.advance(TX)
        ret_w_ahead.done()
        if finish_debug("mix2", mixb):
            return
        mixt = mem(RING0 + 16896, KD, SEQ)
        slot = [mem(RING0 + 4 * K1 * i, KD, 512) for i in range(4)]
        wu = t_in["w_up_2"][0].rearrange("(k p) n -> p k n", p=P)
        up_ahead = Ahead([(slot[0], wu[:, :, 0:512])], "w_up_in")
        products([dict(mm=[(t * P, mixb[:, t, k * P:(k + 1) * P], None) for t in range(TX)],
                       out=out("copy", (0, P, 0, SEQ, mixt[:, k, :]))) for k in range(KD)])
        project_out(TX, mixt, lambda k, cols: wo[k // 4][:, k % 4, cols], wo_ahead)
        normalise([(res[:, t, :], lnx[:, t, :]) for t in range(TX)], LN_EPS, mean=False, counted=True)
        turn_rows(lnx, lambda s, k: lncol[:, 1, k:k + 1], None, TX)
        wd = t_in["w_down_2"][0].rearrange("(c p) n -> p c n", p=P)
        down_slot = [mem(RING0 + 4 * K1 * ((i + 4) % 5), 4, D) for i in range(5)]
        down_in = [signal(f"down_in{i}") for i in range(5)]
        with nc.Block() as block:
            @block.sync
            def _(sp):
                sp.dma_start(down_slot[0], wd[:, 0:4, :]).then_inc(down_in[0].sem, 16)
        NF = FF2 // P
        hid = [mem(LNX0 + 512 * c, 512) if c < 27 else mem(RING0 + 20 * K1 + 512 * (c - 27), 512) for c in range(NF)]
        products([dict(need=c // 4 + 1, mm=[(0, slot[c // 4 % 4][:, k, (c % 4) * P:(c % 4 + 1) * P], ht[:, k, 0:SEQ]) for k in range(KD)],
                       out=out("relu2", (0, P, 0, SEQ, hid[c]))) for c in range(NF)],
                 [(slot[n % 4], wu[:, :, n * 512:(n + 1) * 512], 4 * (n - 3) if n >= 4 else 0) for n in range(1, 8)], ahead=[up_ahead])
        used, complete, finished, stored = signal("down_used"), signal("down_complete"), signal("out_ready"), signal("stored")
        with nc.Block() as block:
            @block.sync
            def _(sp):
                for n in range(1, 8):
                    if n >= 5:
                        sp.wait_ge(used.sem, used.upto(n - 5))
                    sp.dma_start(down_slot[n % 5], wd[:, 4 * n:4 * n + 4, :]).then_inc(down_in[n % 5].sem, 16)
                for t in range(TX):
                    sp.wait_ge(finished.sem, finished.upto(2 * t + 1))
                    sp.dma_start(final.rearrange("o (t p) d -> p (o t) d", p=P)[:, t, :], res[:, t, :]).then_inc(stored.sem, 16)
                sp.wait_ge(stored.sem, stored.upto(TX - 1, 16))

            @block.tensor
            def _(pe):
                def product(n, c, t, m):
                    return nc.tensor.matmul(bank[2 * t + m], lhsT=hid[c][:, t * P:(t + 1) * P],
                                            rhs=down_slot[n % 5][:, c % 4, m * 512:(m + 1) * 512],
                                            start=c == 0, stop=c == NF - 1)

                for n in range(8):
                    pe.wait_ge(down_in[n % 5].sem, down_in[n % 5].upto(n // 5, 16))
                    if n < 7:
                        for c in range(4 * n, 4 * n + 4):
                            for t in range(TX):
                                for m in range(2):
                                    ins = product(n, c, t, m)
                        ins.then_inc(used.sem, 1)
                    else:
                        for t in range(TX):
                            for m in range(2):
                                for c in range(4 * n, 4 * n + 4):
                                    ins = product(n, c, t, m)
                                ins.then_inc(complete.sem, 1)

            @block.vector
            def _(dve):
                for i in range(8):
                    dve.wait_ge(complete.sem, complete.upto(i))
                    o = res[:, i // 2, (i % 2) * 512:(i % 2 + 1) * 512]
                    nc.vector.tensor_tensor(o, o, bank[i], ALU.add).then_inc(finished.sem, 1)

    final = out_ap
    with ctx:
        tables_ahead = Ahead([(consts[:, 0:c1.shape[1]], t_in["consts1"])], "tables_in")
        rows_ahead = Ahead([(res[:, 0:TX, :], t_in["x"][0].rearrange("(t p) d -> p t d", p=P)),
                            (res[:, TX:T, :], t_in["ctx"][0].rearrange("(t p) d -> p t d", p=P))], "rows_in")
        m3 = mod[:, :].rearrange("p (m s) -> p m s", s=2)
        start_adaln(0)
        bias_ahead = Ahead([(bias_rows[l].rearrange("(c n) -> c n", c=64),
                             t_in["nat_bias"][l].rearrange("h r c -> (h r c)").partition_broadcast(64)) for l in range(LAYERS)],
                           "bias_rows_in")
        for l in range(LAYERS):
            last = l == LAYERS - 1
            nt = TX if last else T
            parts = normalise_parts([(res[:, t, :], lnx[:, t, :]) for t in range(T)], LN_EPS, beside=True,
                                    loaded=rows_ahead if l == 0 else None)
            adaln(l, parts, tables_ahead if l == 0 else None)
            if l == 0:
                rows_ahead.done()
                bias_ahead.wait_now()
            if finish_debug(f"mod{l}", mod[:, :]):
                return
            w = mem(RING0, KD, IN_W)
            w_src = t_in["w_in"][l].rearrange("(k p) n -> p k n", p=P)
            w_ahead = [Ahead([(w[:, :, n * 512:(n + 1) * 512], w_src[:, :, n * 512:(n + 1) * 512])], f"w_in{n}") for n in range(4)]
            turn_rows(lnx, lambda s, k: m3[:, 8 + k, s:s + 1], lambda s, k: m3[:, k, s:s + 1], T)
            if finish_debug(f"ht{l}", ht[:, :, :]):
                return
            qkv = mem(LNX0, T, QKV_W)
            glu = mem(LNX0 + T * QKV_W, 4, SEQ + CTX)
            wo = mem(RING0 + 16 * K1, KD, D)
            groups = []
            for n in range(3):
                for t in range(T):
                    groups.append(dict(need=n + 1,
                                       mm=[(0, ht[:, k, t * P:(t + 1) * P], w[:, k, n * 512:(n + 1) * 512]) for k in range(KD)],
                                       out=out("copy", (0, P, 0, 512, qkv[:, t, n * 512:(n + 1) * 512]))))
            for c in range(4):
                for c0, c1_ in ((0, SEQ), (SEQ, SEQ + CTX))[:1 if last else 2]:
                    groups.append(dict(need=4,
                                       mm=[(0, w[:, k, 3 * 512 + c * P:3 * 512 + (c + 1) * P], ht[:, k, c0:c1_]) for k in range(KD)],
                                       out=out("copy", (0, P, 0, c1_ - c0, glu[:, c, c0:c1_]))))
            products(groups, ahead=w_ahead)
            qr = mem(HT0, T, 512)
            kr = mem(HT0 + T * 512, T, P)
            jobs = []
            for t in range(TX):
                for g in range(A_KV):
                    srcq = qkv[:, t, g * 256:(g + 1) * 256].rearrange("p (j d) -> p j d", d=HD)
                    dstq = qr[:, t, :].rearrange("p (j g d) -> p g j d", g=A_KV, d=HD)[:, g]
                    jobs.append((srcq, dstq, t, A_GROUP))
                jobs.append((qkv[:, t, 512:640].rearrange("p (j d) -> p j d", d=HD),
                             kr[:, t, :].rearrange("p (j d) -> p j d", d=HD), t, A_KV))
            rotate(jobs, at1, 16)
            if not last:
                moved = signal("queries_moved")
                with nc.Block() as block:
                    @block.vector
                    def _(dve):
                        for t in range(TX, T):
                            for g in range(A_KV):
                                nc.vector.tensor_copy(
                                    qr[:, t, :].rearrange("p (j g d) -> p g j d", g=A_KV, d=HD)[:, g],
                                    qkv[:, t, g * 256:(g + 1) * 256].rearrange("p (j d) -> p j d", d=HD)).then_inc(moved.sem, 1)
                moved.advance(2 * TC)
            QT0 = RING0
            qta, kta = mem(QT0, A_GROUP, 768), mem(QT0 + 4 * 768, 2, 768)
            qtb, ktb = mem(QT0 + 6 * 768, 2, 768), mem(QT0 + 8 * 768, 4, 768)
            wcol, bcol = small[:, 512:512 + 2 * TAPS].rearrange("p (c t) -> p c t", t=TAPS), small[:, 480:482]
            sink, nsink = small[:, 32:40], small[:, 40:48]
            columns_ahead = Ahead([(sink, t_in["a_sink"][l].partition_broadcast(P)), (wcol, t_in["conv_w_cols"][l]),
                                   (bcol, t_in["conv_b_cols"][l])], "columns_in")
            wo_ahead = Ahead([(wo, t_in["w_out"][l].rearrange("(k p) n -> p k n", p=P))], "w_out_in")
            clear([kta, ktb])
            groups = []
            for c0, c1_ in ((0, TX), (TX, T)):
                n = (c1_ - c0) * P
                cols = slice(c0 * P, c1_ * P)
                latent = c0 == 0
                if latent or not last:
                    for j in range(A_GROUP):
                        mm = [((t - c0) * P, qr[:, t, j * P:(j + 1) * P], None) for t in range(c0, c1_)]
                        groups.append(dict(mm=mm, out=out("scale", (0, P, 0, n, qta[:, j, cols], SCALE))))
                    for j in range(2):
                        groups.append(dict(mm=[((t - c0) * P, qkv[:, t, 768 + j * P:768 + (j + 1) * P], None) for t in range(c0, c1_)],
                                           out=out("scale", (0, P, 0, n, qtb[:, j, cols], SCALE))))
                groups.append(dict(mm=[((t - c0) * P, kr[:, t, :] if latent else qkv[:, t, 512:640], None) for t in range(c0, c1_)],
                                   out=out("copy", (0, 64, 0, n, kta[0:64, 0, cols]), (64, P, 0, n, kta[64:P, 1, cols]))))
                for j in range(2):
                    groups.append(dict(mm=[((t - c0) * P, qkv[:, t, 1024 + j * P:1024 + (j + 1) * P], None) for t in range(c0, c1_)],
                                       out=out("copy", (0, 64, 0, n, ktb[0:64, 2 * j, cols]), (64, P, 0, n, ktb[64:P, 2 * j + 1, cols]))))
            products(groups)
            padded = mem(RING0 + 12 * 768 + 4864, 2, 4 * HALF + SEQ + CTX)
            span = glu_pad(glu, padded, nt)
            negated = signal("sinks_negated")
            with nc.Block() as block:
                @block.vector
                def _(dve):
                    columns_ahead.wait(dve)
                    nc.vector.tensor_scalar(nsink, sink, -1.0, None, ALU.mult).then_inc(negated.sem, 1)
            negated.advance(1)
            columns_ahead.done()
            mix = mem(HT0, T, D)
            units = []
            for h in range(A_HEADS):
                g, j = h // A_GROUP, h % A_GROUP
                sk = dict(sink=sink[:, h:h + 1], nsink=nsink[:, h:h + 1])
                for t in range(nt):
                    u = dict(q=qta[:, j, t * P:(t + 1) * P], out=mix[:, t, h * HD:(h + 1) * HD], v0=g * HD, **sk)
                    vcol = slice(640, 768)
                    u["keys"] = [(0, kta[:, g, SEQ:SEQ + CTX])]
                    u["evac"] = [(0, 0, CTX, None)]
                    u["v"] = [qkv[:, s, vcol] for s in range(TX, T)]
                    u["n"] = CTX
                    if t < TX:
                        s0, s1 = max(0, t - 1), min(TX - 1, t + 1)
                        u["keys"].append((512, kta[:, g, s0 * P:(s1 + 1) * P]))
                        for s in range(s0, s1 + 1):
                            bias = cst(at1, "upper") if s < t else cst(at1, "lower") if s > t else None
                            u["evac"].append((512 + (s - s0) * P, u["n"], P, bias))
                            u["v"].append(qkv[:, s, vcol])
                            u["n"] += P
                    units.append(u)
            biases = {}
            for h in range(B_HEADS):
                j = h // 2
                for t in range(nt):
                    vcol = slice(1280 + j * P, 1280 + (j + 1) * P)
                    u = dict(v0=(h % 2) * HD, q=qtb[:, j, t * P:(t + 1) * P], out=mix[:, t, 512 + h * HD:512 + (h + 1) * HD])
                    if t < TX:
                        u["keys"] = [(0, ktb[:, h, 0:SEQ]), (512, ktb[:, h, SEQ:SEQ + CTX])]
                        u["evac"] = [(0, 0, SEQ, True), (512, SEQ, CTX, None)]
                        u["v"] = [qkv[:, s, vcol] for s in range(T)]
                        u["n"] = SEQ + CTX
                        biases[len(units)] = [
                            bass.AP(bias_rows.tensor, bias_rows[l].offset + h * RB_R * RB_C + (7 - r) * RB_C + RB_C // 2,
                                    [[B_HEADS * RB_R * RB_C - 1, 64], [RB_C, ROWS], [1, GRID]])
                            for r in (2 * t, 2 * t + 1)]
                    else:
                        u["keys"] = [(0, ktb[:, h, SEQ:SEQ + CTX])]
                        u["evac"] = [(0, 0, CTX, None)]
                        u["v"] = [qkv[:, s, vcol] for s in range(TX, T)]
                        u["n"] = CTX
                    units.append(u)
            PAD = 4 * HALF + SEQ + CTX
            y = mem(LNX0 + T * QKV_W, 2, PAD)
            buf = [mem(LNX0 + T * QKV_W + 2 * PAD, 800), mem(LNX0 + T * QKV_W + 3072, 800)]
            attend(units, RING0 + 12 * 768, at1, biases, (padded, y, wcol, bcol, span, buf))
            cg, cb = mem(RING0, C_CH), mem(RING0 + C_CH, C_CH)
            conv_ln = Ahead([(cg, t_in["conv_ln_g"][l].partition_broadcast(P)), (cb, t_in["conv_ln_b"][l].partition_broadcast(P))], "conv_ln_in")
            gtile = [mem(RING0 + 7 * K1 + K1 * i, D) for i in range(2)]
            gain, shift_ = mem(RING0 + 9 * K1, D), mem(RING0 + 10 * K1, D)
            wr = small[:, 576:704].rearrange("p (k e) -> p k e", e=E)
            gates_ahead = Ahead([(gtile[s], mod_rows[s, 0].partition_broadcast(P)) for s in range(2)], "gates_in")
            ln1_ahead = Ahead([(gain, t_in["ln1_g"][l].partition_broadcast(P)), (shift_, t_in["ln1_b"][l].partition_broadcast(P)),
                               (wr, t_in["w_router"][l].rearrange("(k p) e -> p k e", p=P))], "ln_in")
            groups = []
            for t in range(nt):
                a = t * P if t < TX else SEQ + 2 * HALF + (t - TX) * P
                groups.append(dict(mm=[(c * P, y[:, c, a:a + P], None) for c in range(2)],
                                   out=out("copy", (0, P, 0, C_CH, mix[:, t, 768:1024]))))
            products(groups)
            rows = [(mix[:, t, 768:1024], mix[:, t, 768:1024]) for t in range(nt)]
            normalise(rows, LN_EPS, post=[(cg, cb)] * nt, width=C_CH, ahead=conv_ln)
            silu_rows(rows)
            if finish_debug(f"mix{l}", mix[:, 0:nt, :]):
                return
            mixt = mem(RING0, KD, 768)
            groups = []
            for k in range(KD):
                for c0, c1_ in ((0, TX), (TX, T))[:1 if last else 2]:
                    groups.append(dict(mm=[((t - c0) * P, mix[:, t, k * P:(k + 1) * P], None) for t in range(c0, c1_)],
                                       out=out("copy", (0, P, 0, (c1_ - c0) * P, mixt[:, k, c0 * P:c1_ * P]))))
            products(groups)
            project_out(nt, mixt, lambda k, cols: wo[:, k, cols], wo_ahead, gtile, gates_ahead, mem(RING0 + 11 * K1, 2, 512))
            normalise([(res[:, t, :], res[:, t, :]) for t in range(nt)], LN_EPS, post=[(gain, shift_)] * nt, ahead=ln1_ahead,
                      counted=True)
            if finish_debug(f"res1_{l}", res[:, 0:nt, :]):
                return
            start_experts(l)
            normalise([(res[:, t, :], lnx[:, t, :]) for t in range(nt)], LN_EPS)
            turn_rows(lnx, lambda s, k: m3[:, 32 + k, s:s + 1], lambda s, k: m3[:, 24 + k, s:s + 1], nt)
            X0 = EXTRA0
            aff, pos = mem(X0, T, E), mem(X0 + T * E, T, E)
            msk, logit = mem(X0 + 2 * T * E, T, E), mem(X0 + 3 * T * E, T, E)
            af = small[:, 16:24]
            at_ = mem(X0 + 4 * T * E, 768, parts=E)
            work = mem(X0 + 4 * T * E + 768, nt * P, parts=E)
            best = small[0:E, 0:8]
            route(l, nt, wr, logit, aff, pos, msk, af, at_, work, best)
            if finish_debug(f"pos{l}", pos[:, 0:nt, :]):
                return
            gtile = [mem(HT0 + K1 * i, D) for i in range(2)]
            gain, shift_ = mem(HT0 + 2 * K1, D), mem(HT0 + 3 * K1, D)
            gates_ahead = Ahead([(gtile[s], mod_rows[s, 1].partition_broadcast(P)) for s in range(2)], "gates_in")
            ln2_ahead = Ahead([(gain, t_in["ln2_g"][l].partition_broadcast(P)), (shift_, t_in["ln2_b"][l].partition_broadcast(P))], "ln_in")
            experts(l, nt, aff, pos, res, X0 + 2 * T * E, gtile, gates_ahead)
            if finish_debug(f"moe{l}", res[:, 0:nt, :]):
                return
            if last:
                second_ahead = start_second()
            else:
                start_adaln(l + 1)
            normalise([(res[:, t, :], res[:, t, :]) for t in range(nt)], LN_EPS, post=[(gain, shift_)] * nt, ahead=ln2_ahead)
            if finish_debug(f"res2_{l}", res[:, 0:nt, :]):
                return
        sparse_attention_block(*second_ahead)


_INPUTS = ["x", "c", "ctx", "c_ctx", "w_mod", "b_mod", "w_in", "a_sink", "nat_bias", "conv_w", "conv_b", "conv_ln_g",
           "conv_ln_b", "w_out", "ln1_g", "ln1_b", "w_router", "w_gate", "w_up", "w_down", "ln2_g", "ln2_b", "ln1_w_2",
           "w_in_2", "q_norm_w_2", "k_norm_w_2", "cmp_pe_k_2", "cmp_pe_v_2", "cmp_wk1_2", "cmp_wk2_2", "cmp_wv1_2",
           "cmp_wv2_2", "ret_norm_w_2", "w_out_2", "ln2_w_2", "w_up_2", "w_down_2"]


def extra_layout(inputs):
    def cols(a):
        a = np.asarray(a)
        a = a.reshape(a.shape[:-1] + (a.shape[-1] // P, P))
        return np.ascontiguousarray(np.swapaxes(a, -1, -2))

    cond = np.stack([cols(inputs["c"][0]), cols(inputs["c_ctx"])], -1).reshape(P, 2 * KD)
    taps = np.asarray(inputs["conv_w"]).transpose(0, 2, 1).reshape(LAYERS, 2, P, TAPS).transpose(0, 2, 1, 3)
    return {"cond_cols": cond, "b_mod_cols": cols(inputs["b_mod"]),
            "ln1_w_cols": cols(inputs["ln1_w_2"]), "ln2_w_cols": cols(inputs["ln2_w_2"]),
            "cmp_pe_k_cols": cols(np.asarray(inputs["cmp_pe_k_2"]).reshape(1, -1)),
            "cmp_pe_v_cols": cols(np.asarray(inputs["cmp_pe_v_2"]).reshape(1, -1)),
            "conv_w_cols": np.ascontiguousarray(taps), "conv_b_cols": cols(inputs["conv_b"])}


def kernel(**inputs):
    import concourse.bacc as bacc
    from concourse.bass_utils import run_bass_kernel_spmd

    nc = bacc.Bacc("TRN2", target_bir_lowering=False, num_devices=1)
    (c1, _), (c2, _) = shape_constants()
    arrays = {name: np.ascontiguousarray(inputs[name]) for name in _INPUTS}
    arrays |= {"consts1": c1, "consts2": c2} | extra_layout(inputs)
    t_in = {name: nc.dram_tensor(f"in_{name}", a.shape, mybir.dt.from_np(a.dtype), kind="ExternalInput").ap()
            for name, a in arrays.items()}
    out = nc.dram_tensor("out", [1, SEQ, D], F32, kind="ExternalOutput").ap()
    build(nc, t_in, out)
    r = run_bass_kernel_spmd(nc, [{f"in_{name}": a for name, a in arrays.items()}], core_ids=[0])
    return r.results[0]["out"]
```
